# Optimizing a Trainium2 kernel written in Bass

```python
import jax, jax.numpy as jnp
from jax import lax
import numpy as np
import math
import jax
import jax.numpy as jnp

D_MODEL = 1024
BATCH = 1
SEQ = 2048
DEPTH = 1

D_MIX = D_MODEL
NORM_EPS = 1e-6

GLA_HEADS = 4
GLA_DK = 64
GLA_DV = 128
GLA_KW = GLA_HEADS * GLA_DK
GLA_VW = GLA_HEADS * GLA_DV
GLA_GATE_RANK = 16
GLA_TAU = 16.0
GLA_CHUNK = 64

RWKV_HEAD = 64
RWKV_W = D_MIX - GLA_VW
RWKV_HEADS = RWKV_W // RWKV_HEAD
RWKV_DECAY_RANK = 64
RWKV_A_RANK = 64
RWKV_GN_EPS = 64e-5

GLA_SPLITS = (GLA_KW, GLA_KW, GLA_VW, GLA_GATE_RANK, GLA_VW)
RWKV_SHIFT_SPLITS = (RWKV_W, RWKV_W, RWKV_W, RWKV_DECAY_RANK, RWKV_A_RANK)
GLA_IN = sum(GLA_SPLITS)
RWKV_SHIFT_W = sum(RWKV_SHIFT_SPLITS)
RWKV_IN = RWKV_SHIFT_W + RWKV_W
IN_WIDTH = GLA_IN + RWKV_IN


def _split(t, sizes):
    idx = np.cumsum(np.array(sizes))[:-1].tolist()
    return jnp.split(t, idx, axis=-1)

def _rmsnorm(x, w):
    xf = x.astype(jnp.float32)
    y = xf * lax.rsqrt(jnp.mean(xf * xf, axis=-1, keepdims=True) + NORM_EPS)
    return (y * w.astype(jnp.float32)).astype(x.dtype)

def _gla_chunked(q, k, v, log_a):
    B, T, H, DK = q.shape
    DV = v.shape[-1]
    C = GLA_CHUNK
    N = T // C

    def to_chunks(t):
        return t.reshape(B, N, C, H, t.shape[-1]).transpose(1, 0, 3, 2, 4)

    qc, kc, vc, gc = to_chunks(q), to_chunks(k), to_chunks(v), to_chunks(log_a)
    b = jnp.cumsum(gc, axis=3)
    b_last = b[:, :, :, -1:, :]
    q_in = qc * jnp.exp(b)
    k_in = kc * jnp.exp(-b)
    k_st = kc * jnp.exp(b_last - b)
    causal = jnp.tril(jnp.ones((C, C), dtype=bool))
    scores = jnp.einsum('nbhid,nbhjd->nbhij', q_in, k_in)
    scores = jnp.where(causal, scores, 0.0)
    o_intra = jnp.einsum('nbhij,nbhjv->nbhiv', scores, vc)
    d_state = jnp.einsum('nbhjd,nbhjv->nbhdv', k_st, vc)
    chunk_decay = jnp.exp(b_last[:, :, :, 0, :])

    def step(S, inp):
        dS, dec = inp
        return S * dec[..., None] + dS, S

    S0 = jnp.zeros((B, H, DK, DV), jnp.float32)
    _, S_prev = lax.scan(step, S0, (d_state, chunk_decay))
    o_inter = jnp.einsum('nbhid,nbhdv->nbhiv', q_in, S_prev)
    o = o_intra + o_inter
    return o.transpose(1, 0, 3, 2, 4).reshape(B, T, H, DV)

def _rwkv7_scan(r, decay, k, v, kk, a):
    B, T, H, N = r.shape

    def step(S, inp):
        r_t, w_t, k_t, v_t, kk_t, a_t = inp
        sa = jnp.einsum('bhvk,bhk->bhv', S, -kk_t)
        S = (S * w_t[:, :, None, :]
             + sa[..., None] * (kk_t * a_t)[:, :, None, :]
             + v_t[..., None] * k_t[:, :, None, :])
        y = jnp.einsum('bhvk,bhk->bhv', S, r_t)
        return S, y

    xs = tuple(t.transpose(1, 0, 2, 3) for t in (r, decay, k, v, kk, a))
    S0 = jnp.zeros((B, H, N, N), jnp.float32)
    _, y = lax.scan(step, S0, xs)
    return y.transpose(1, 0, 2, 3)

def _hybrid_layer(x, norm_w, w_in, gla_gate_up, gla_gate_bias, gla_norm_w,
                  rwkv_mu, rwkv_w0, rwkv_w_up, rwkv_a0, rwkv_a_up, rwkv_k_k,
                  rwkv_k_a, rwkv_r_k, rwkv_ln_w, rwkv_ln_b, w_out):
    B, T, _ = x.shape
    f32 = jnp.float32
    h = _rmsnorm(x, norm_w)
    u = (h @ w_in).astype(f32)
    gla_u, rwkv_u = u[..., :GLA_IN], u[..., GLA_IN:]

    gq, gk, gv, glr, gg = _split(gla_u, GLA_SPLITS)
    log_a = jax.nn.log_sigmoid(glr @ gla_gate_up.astype(f32) + gla_gate_bias.astype(f32)) / GLA_TAU
    q = gq.reshape(B, T, GLA_HEADS, GLA_DK) * (GLA_DK ** -0.5)
    k = gk.reshape(B, T, GLA_HEADS, GLA_DK)
    v = gv.reshape(B, T, GLA_HEADS, GLA_DV)
    o = _gla_chunked(q, k, v, log_a.reshape(B, T, GLA_HEADS, GLA_DK))
    o = o * lax.rsqrt(jnp.mean(o * o, axis=-1, keepdims=True) + NORM_EPS) * gla_norm_w.astype(f32)
    gla_out = o.reshape(B, T, GLA_VW) * jax.nn.silu(gg)

    shifted_cols = rwkv_u[..., :RWKV_SHIFT_W]
    rg = rwkv_u[..., RWKV_SHIFT_W:]
    prev = jnp.pad(shifted_cols, ((0, 0), (1, 0), (0, 0)))[:, :-1]
    mixed = shifted_cols + (prev - shifted_cols) * rwkv_mu.astype(f32)
    r, rk, rv, wl, al = _split(mixed, RWKV_SHIFT_SPLITS)
    w = -jax.nn.softplus(-(rwkv_w0.astype(f32) + jnp.tanh(wl) @ rwkv_w_up.astype(f32))) - 0.5
    decay = jnp.exp(-jnp.exp(w))
    a = jax.nn.sigmoid(rwkv_a0.astype(f32) + al @ rwkv_a_up.astype(f32))
    kk = (rk * rwkv_k_k.astype(f32)).reshape(B, T, RWKV_HEADS, RWKV_HEAD)
    kk = kk / jnp.maximum(jnp.linalg.norm(kk, axis=-1, keepdims=True), 1e-12)
    rk = rk * (1.0 + (a - 1.0) * rwkv_k_a.astype(f32))
    hs = (B, T, RWKV_HEADS, RWKV_HEAD)
    r_h, k_h, v_h = r.reshape(hs), rk.reshape(hs), rv.reshape(hs)
    y = _rwkv7_scan(r_h, decay.reshape(hs), k_h, v_h, kk, a.reshape(hs))
    mu = jnp.mean(y, axis=-1, keepdims=True)
    var = jnp.mean(jnp.square(y - mu), axis=-1, keepdims=True)
    y = ((y - mu) * lax.rsqrt(var + RWKV_GN_EPS)).reshape(B, T, RWKV_W)
    y = y * rwkv_ln_w.astype(f32) + rwkv_ln_b.astype(f32)
    bonus = jnp.sum(r_h * k_h * rwkv_r_k.astype(f32), axis=-1, keepdims=True) * v_h
    rwkv_out = (y + bonus.reshape(B, T, RWKV_W)) * jax.nn.silu(rg)

    merged = jnp.concatenate([gla_out, rwkv_out], axis=-1).astype(x.dtype)
    return x + merged @ w_out

def first_inputs(seed: int = 0) -> dict:
    key = jax.random.key(seed)
    ks = jax.random.split(key, 20)
    n = jax.random.normal
    L = DEPTH
    return {
        "x": n(ks[0], (BATCH, SEQ, D_MODEL), jnp.float32),
        "norm_w": 1.0 + 0.05 * n(ks[1], (L, D_MODEL), jnp.float32),
        "w_in": n(ks[2], (L, D_MODEL, IN_WIDTH), jnp.float32) * D_MODEL ** -0.5,
        "gla_gate_up": n(ks[3], (L, GLA_GATE_RANK, GLA_KW), jnp.float32) * GLA_GATE_RANK ** -0.5,
        "gla_gate_bias": 0.1 * n(ks[4], (L, GLA_KW), jnp.float32),
        "gla_norm_w": 1.0 + 0.05 * n(ks[5], (L, GLA_DV), jnp.float32),
        "rwkv_mu": jax.random.uniform(ks[6], (L, RWKV_SHIFT_W), jnp.float32),
        "rwkv_w0": jax.random.uniform(ks[7], (L, RWKV_W), jnp.float32, -6.0, -1.0),
        "rwkv_w_up": 0.1 * n(ks[8], (L, RWKV_DECAY_RANK, RWKV_W), jnp.float32),
        "rwkv_a0": 0.1 * n(ks[9], (L, RWKV_W), jnp.float32),
        "rwkv_a_up": 0.1 * n(ks[10], (L, RWKV_A_RANK, RWKV_W), jnp.float32),
        "rwkv_k_k": 0.85 + 0.05 * n(ks[11], (L, RWKV_W), jnp.float32),
        "rwkv_k_a": 1.0 + 0.05 * n(ks[12], (L, RWKV_W), jnp.float32),
        "rwkv_r_k": 0.1 * n(ks[13], (L, RWKV_HEADS, RWKV_HEAD), jnp.float32),
        "rwkv_ln_w": 1.0 + 0.05 * n(ks[14], (L, RWKV_W), jnp.float32),
        "rwkv_ln_b": 0.02 * n(ks[15], (L, RWKV_W), jnp.float32),
        "w_out": n(ks[16], (L, D_MIX, D_MODEL), jnp.float32) * D_MIX ** -0.5,
        "final_norm_w": 1.0 + 0.05 * n(ks[17], (D_MODEL,), jnp.float32),
    }

def first_block(x, norm_w, w_in, gla_gate_up, gla_gate_bias, gla_norm_w, rwkv_mu,
              rwkv_w0, rwkv_w_up, rwkv_a0, rwkv_a_up, rwkv_k_k, rwkv_k_a,
              rwkv_r_k, rwkv_ln_w, rwkv_ln_b, w_out, final_norm_w):
    for l in range(DEPTH):
        x = _hybrid_layer(x, norm_w[l], w_in[l], gla_gate_up[l], gla_gate_bias[l],
                          gla_norm_w[l], rwkv_mu[l], rwkv_w0[l], rwkv_w_up[l],
                          rwkv_a0[l], rwkv_a_up[l], rwkv_k_k[l], rwkv_k_a[l],
                          rwkv_r_k[l], rwkv_ln_w[l], rwkv_ln_b[l], w_out[l])
    return _rmsnorm(x, final_norm_w)


GRID_W = 64
CTX_LEN = 256
N_MIXERS = 3
MIX_SHORTCONV = 0
MIX_HYENA = 1
MIX_ATTN = 2
CONV_W = 3
EPS = 1e-6
HY_ORDER = 2
HY_EMB = 33
HY_BANDS = (HY_EMB - 1) // 2
HY_FILTER_HIDDEN = 64
HY_FAST_DECAY = 0.3
HY_SLOW_DECAY = 1.5
HY_TARGET = 1e-2
HEAD_DIM = 128
N_Q_HEADS = D_MODEL // HEAD_DIM
N_KV_HEADS = 2
Q_PER_KV = N_Q_HEADS // N_KV_HEADS
AXIS_DIM = HEAD_DIM // 2
ROPE_THETA = 10000.0
Q_BLOCK = 128
N_EXPERTS = 16
EC_CAPACITY_FACTOR = 2
D_EXPERT = D_MODEL


def _layers_of(kind):
    return list(range(kind, DEPTH, N_MIXERS))

def rms_norm(x, g):
    xf = x.astype(jnp.float32)
    y = xf * lax.rsqrt(jnp.mean(xf * xf, axis=-1, keepdims=True) + EPS)
    return (y * g.astype(jnp.float32)).astype(x.dtype)

def modulate(x, shift, scale):
    return x * (1.0 + scale) + shift

def dwconv_centred(x, w):
    L = x.shape[1]
    p = CONV_W // 2
    xp = jnp.pad(x, ((0, 0), (p, p), (0, 0)))
    y = xp[:, 0:L] * w[0]
    for k in range(1, CONV_W):
        y = y + xp[:, k:k + L] * w[k]
    return y

def short_conv_mixer(h, w_in, conv_w, w_out):
    gate_b, gate_c, v = jnp.split(h @ w_in, 3, axis=-1)
    return (gate_b * dwconv_centred(gate_c * v, conv_w)) @ w_out

def hyena_filter_spectrum(L, w1, b1, w2, b2, w3, sin_freq):
    f32 = jnp.float32
    t = jnp.linspace(0.0, 1.0, L, dtype=f32)[:, None]
    bands = jnp.linspace(1e-4, HY_BANDS - 1, HY_BANDS, dtype=f32)[None, :]
    ang = (2.0 * math.pi / L) * jnp.arange(L, dtype=f32)[:, None] * bands
    z = jnp.concatenate([t, jnp.cos(ang), -jnp.sin(ang)], axis=-1)
    freq = sin_freq.astype(f32)
    a = jnp.sin(freq * (z @ w1.astype(f32) + b1.astype(f32)))
    a = jnp.sin(freq * (a @ w2.astype(f32) + b2.astype(f32)))
    h = (a @ w3.astype(f32)).reshape(L, 2, HY_ORDER, D_MODEL)
    deltas = jnp.abs(jnp.linspace(math.log(HY_TARGET) / HY_SLOW_DECAY,
                                  math.log(HY_TARGET) / HY_FAST_DECAY, D_MODEL, dtype=f32))
    h = h * jnp.exp(-t * deltas[None, :])[:, None, None, :]
    fwd = h[:, 0]
    bwd = h[1:, 1][::-1]
    full = jnp.concatenate([fwd, jnp.zeros((1, HY_ORDER, D_MODEL), f32), bwd], axis=0)
    full = full / jnp.sum(jnp.abs(full), axis=0, keepdims=True)
    return jnp.fft.rfft(full, axis=0)

def long_conv(u, filt_f, skip):
    L = u.shape[1]
    uf = u.astype(jnp.float32)
    y = jnp.fft.irfft(jnp.fft.rfft(uf, n=2 * L, axis=1) * filt_f[None], n=2 * L, axis=1)[:, :L]
    return (y + uf * skip.astype(jnp.float32)).astype(u.dtype)

def hyena_mixer(h, w_in, conv_w, f_w1, f_b1, f_w2, f_b2, f_w3, sin_freq, skip, w_out):
    L = h.shape[1]
    parts = jnp.split(dwconv_centred(h @ w_in, conv_w), HY_ORDER + 1, axis=-1)
    z, gates = parts[0], parts[1:]
    filt = hyena_filter_spectrum(L, f_w1, f_b1, f_w2, f_b2, f_w3, sin_freq)
    for o in range(HY_ORDER):
        z = gates[o] * long_conv(z, filt[:, o], skip[o])
    return z @ w_out

def axial_rope_tables(n_tokens, dtype):
    f32 = jnp.float32
    rows = n_tokens // GRID_W
    row = jnp.repeat(jnp.arange(rows, dtype=f32), GRID_W)
    col = jnp.tile(jnp.arange(GRID_W, dtype=f32), rows)
    inv = ROPE_THETA ** (-jnp.arange(0, AXIS_DIM, 2, dtype=f32) / AXIS_DIM)

    def axis_angles(pos):
        a = pos[:, None] * inv[None, :]
        return jnp.concatenate([a, a], axis=-1)

    ang = jnp.concatenate([axis_angles(row), axis_angles(col)], axis=-1)
    return jnp.cos(ang).astype(dtype), jnp.sin(ang).astype(dtype)

def _rotate_axial(x):
    q = AXIS_DIM // 2
    xr, xc = x[..., :AXIS_DIM], x[..., AXIS_DIM:]
    return jnp.concatenate([-xr[..., q:], xr[..., :q], -xc[..., q:], xc[..., :q]], axis=-1)

def apply_rope(x, cos, sin):
    return x * cos + _rotate_axial(x) * sin

def _attend(q, k, v):
    s = jnp.einsum('bqkgd,bskd->bkgqs', q, k, preferred_element_type=jnp.float32) * (HEAD_DIM ** -0.5)
    p = jax.nn.softmax(s, axis=-1)
    return jnp.einsum('bkgqs,bskd->bqkgd', p.astype(v.dtype), v)

def gqa_mixer(h_lat, h_ctx, w_qkv, q_g, k_g, w_o, ctx_out):
    B, L, _ = h_lat.shape
    Lc = h_ctx.shape[1]
    QD = N_Q_HEADS * HEAD_DIM
    KVD = N_KV_HEADS * HEAD_DIM

    def heads_q(t, n):
        return rms_norm(t.reshape(B, n, N_KV_HEADS, Q_PER_KV, HEAD_DIM), q_g)

    def heads_kv(t, n):
        k = rms_norm(t[..., :KVD].reshape(B, n, N_KV_HEADS, HEAD_DIM), k_g)
        v = t[..., KVD:].reshape(B, n, N_KV_HEADS, HEAD_DIM)
        return k, v

    qkv_l = h_lat @ w_qkv
    q_l = heads_q(qkv_l[..., :QD], L)
    k_l, v_l = heads_kv(qkv_l[..., QD:], L)
    cos, sin = axial_rope_tables(L, q_l.dtype)
    q_l = apply_rope(q_l, cos[None, :, None, None], sin[None, :, None, None])
    k_l = apply_rope(k_l, cos[None, :, None], sin[None, :, None])
    if ctx_out:
        qkv_c = h_ctx @ w_qkv
        q_c = heads_q(qkv_c[..., :QD], Lc)
        kv_c = qkv_c[..., QD:]
    else:
        kv_c = h_ctx @ w_qkv[:, QD:]
    k_c, v_c = heads_kv(kv_c, Lc)

    k_all = jnp.concatenate([k_c, k_l], axis=1)
    v_all = jnp.concatenate([v_c, v_l], axis=1)
    n_blk = L // Q_BLOCK
    qb = jnp.moveaxis(q_l.reshape(B, n_blk, Q_BLOCK, N_KV_HEADS, Q_PER_KV, HEAD_DIM), 1, 0)
    o_l = lax.map(lambda qblk: _attend(qblk, k_all, v_all), qb)
    y_l = jnp.moveaxis(o_l, 0, 1).reshape(B, L, QD) @ w_o
    y_c = _attend(q_c, k_c, v_c).reshape(B, Lc, QD) @ w_o if ctx_out else None
    return y_l, y_c

def expert_choice_ffn(h, w_router, w_gate, w_up, w_down):
    B, N, D = h.shape
    cap = EC_CAPACITY_FACTOR * N // N_EXPERTS
    aff = jax.nn.softmax((h @ w_router).astype(jnp.float32), axis=-1)
    g, idx = lax.top_k(jnp.swapaxes(aff, 1, 2), cap)
    xs = jax.vmap(lambda hb, ib: hb[ib])(h, idx)
    hid = jax.nn.silu(jnp.einsum('becd,edf->becf', xs, w_gate)) * jnp.einsum('becd,edf->becf', xs, w_up)
    ys = jnp.einsum('becf,efd->becd', hid, w_down) * g[..., None].astype(h.dtype)
    return jax.vmap(lambda yb, ib: jnp.zeros((N, D), yb.dtype).at[ib.reshape(-1)].add(yb.reshape(-1, D)))(ys, idx)

def second_inputs(seed: int = 0) -> dict:
    key = jax.random.key(seed)
    ks = iter(jax.random.split(key, 40))
    D, F = D_MODEL, D_EXPERT
    nA, nB, nC = (len(_layers_of(k)) for k in range(N_MIXERS))
    QKV = (N_Q_HEADS + 2 * N_KV_HEADS) * HEAD_DIM

    def nrm(shape, s):
        return jax.random.normal(next(ks), shape, jnp.float32) * s

    return {
        "x": nrm((BATCH, SEQ, D), 1.0),
        "c": nrm((BATCH, D), 1.0),
        "ctx": nrm((BATCH, CTX_LEN, D), 1.0),
        "c_ctx": nrm((D,), 1.0),
        "ada_w": nrm((DEPTH, D, 6 * D), 0.5 * D ** -0.5),
        "ada_b": nrm((DEPTH, 6 * D), 0.01),
        "norm_g": 1.0 + nrm((DEPTH, 2, D), 0.02),
        "sc_w_in": nrm((nA, D, 3 * D), D ** -0.5),
        "sc_conv": nrm((nA, CONV_W, D), CONV_W ** -0.5),
        "sc_w_out": nrm((nA, D, D), D ** -0.5),
        "hy_w_in": nrm((nB, D, (HY_ORDER + 1) * D), D ** -0.5),
        "hy_conv": nrm((nB, CONV_W, (HY_ORDER + 1) * D), CONV_W ** -0.5),
        "hy_f_w1": nrm((nB, HY_EMB, HY_FILTER_HIDDEN), HY_EMB ** -0.5),
        "hy_f_b1": nrm((nB, HY_FILTER_HIDDEN), 0.02),
        "hy_f_w2": nrm((nB, HY_FILTER_HIDDEN, HY_FILTER_HIDDEN), HY_FILTER_HIDDEN ** -0.5),
        "hy_f_b2": nrm((nB, HY_FILTER_HIDDEN), 0.02),
        "hy_f_w3": nrm((nB, HY_FILTER_HIDDEN, 2 * HY_ORDER * D), HY_FILTER_HIDDEN ** -0.5),
        "hy_sin_freq": 1.0 + nrm((nB, HY_FILTER_HIDDEN), 0.02),
        "hy_skip": nrm((nB, HY_ORDER, D), 1.0),
        "hy_w_out": nrm((nB, D, D), D ** -0.5),
        "at_w_qkv": nrm((nC, D, QKV), D ** -0.5),
        "at_q_g": 1.0 + nrm((nC, HEAD_DIM), 0.02),
        "at_k_g": 1.0 + nrm((nC, HEAD_DIM), 0.02),
        "at_w_o": nrm((nC, N_Q_HEADS * HEAD_DIM, D), (N_Q_HEADS * HEAD_DIM) ** -0.5),
        "moe_router": nrm((DEPTH, D, N_EXPERTS), D ** -0.5),
        "moe_w_gate": nrm((DEPTH, N_EXPERTS, D, F), D ** -0.5),
        "moe_w_up": nrm((DEPTH, N_EXPERTS, D, F), D ** -0.5),
        "moe_w_down": nrm((DEPTH, N_EXPERTS, F, D), F ** -0.5),
    }

def second_block(x, c, ctx, c_ctx, ada_w, ada_b, norm_g, sc_w_in, sc_conv, sc_w_out,
              hy_w_in, hy_conv, hy_f_w1, hy_f_b1, hy_f_w2, hy_f_b2, hy_f_w3, hy_sin_freq, hy_skip, hy_w_out,
              at_w_qkv, at_q_g, at_k_g, at_w_o, moe_router, moe_w_gate, moe_w_up, moe_w_down):
    last_attn = max(_layers_of(MIX_ATTN), default=-1)
    lat, cx = x, ctx
    silu_c = jax.nn.silu(c)
    silu_cc = jax.nn.silu(c_ctx)
    for i in range(DEPTH):
        kind = i % N_MIXERS
        j = i // N_MIXERS
        need_ctx = i <= last_attn
        upd_ctx = i < last_attn

        m_l = (silu_c @ ada_w[i] + ada_b[i])[:, None, :]
        sh1, sc1, g1, sh2, sc2, g2 = jnp.split(m_l, 6, axis=-1)
        hl = modulate(rms_norm(lat, norm_g[i, 0]), sh1, sc1)
        if need_ctx:
            m_c = silu_cc @ ada_w[i] + ada_b[i]
            csh1, csc1, cg1, csh2, csc2, cg2 = jnp.split(m_c, 6, axis=-1)
            hc = modulate(rms_norm(cx, norm_g[i, 0]), csh1, csc1)

        yc = None
        if kind == MIX_SHORTCONV:
            yl = short_conv_mixer(hl, sc_w_in[j], sc_conv[j], sc_w_out[j])
            if upd_ctx:
                yc = short_conv_mixer(hc, sc_w_in[j], sc_conv[j], sc_w_out[j])
        elif kind == MIX_HYENA:
            hy_args = (hy_w_in[j], hy_conv[j], hy_f_w1[j], hy_f_b1[j], hy_f_w2[j], hy_f_b2[j],
                       hy_f_w3[j], hy_sin_freq[j], hy_skip[j], hy_w_out[j])
            yl = hyena_mixer(hl, *hy_args)
            if upd_ctx:
                yc = hyena_mixer(hc, *hy_args)
        else:
            yl, yc = gqa_mixer(hl, hc, at_w_qkv[j], at_q_g[j], at_k_g[j], at_w_o[j], upd_ctx)

        lat = lat + g1 * yl
        hl2 = modulate(rms_norm(lat, norm_g[i, 1]), sh2, sc2)
        lat = lat + g2 * expert_choice_ffn(hl2, moe_router[i], moe_w_gate[i], moe_w_up[i], moe_w_down[i])
        if upd_ctx:
            cx = cx + cg1 * yc
            hc2 = modulate(rms_norm(cx, norm_g[i, 1]), csh2, csc2)
            cx = cx + cg2 * expert_choice_ffn(hc2, moe_router[i], moe_w_gate[i], moe_w_up[i], moe_w_down[i])
    return lat


def setup_inputs(seed=0):
    out = dict(first_inputs(seed))
    for name, value in second_inputs(seed + 1).items():
        if name != "x":
            out[name + "_2"] = value
    return out


def reference(
    x, norm_w, w_in, gla_gate_up, gla_gate_bias, gla_norm_w, rwkv_mu, rwkv_w0, rwkv_w_up,
    rwkv_a0, rwkv_a_up, rwkv_k_k, rwkv_k_a, rwkv_r_k, rwkv_ln_w, rwkv_ln_b, w_out, final_norm_w,
    c_2, ctx_2, c_ctx_2, ada_w_2, ada_b_2, norm_g_2, sc_w_in_2, sc_conv_2, sc_w_out_2,
    hy_w_in_2, hy_conv_2, hy_f_w1_2, hy_f_b1_2, hy_f_w2_2, hy_f_b2_2, hy_f_w3_2, hy_sin_freq_2,
    hy_skip_2, hy_w_out_2, at_w_qkv_2, at_q_g_2, at_k_g_2, at_w_o_2, moe_router_2, moe_w_gate_2,
    moe_w_up_2, moe_w_down_2,
):
    x = first_block(
        x, norm_w, w_in, gla_gate_up, gla_gate_bias, gla_norm_w, rwkv_mu, rwkv_w0, rwkv_w_up,
        rwkv_a0, rwkv_a_up, rwkv_k_k, rwkv_k_a, rwkv_r_k, rwkv_ln_w, rwkv_ln_b, w_out,
        final_norm_w,
    )
    return second_block(
        x, c_2, ctx_2, c_ctx_2, ada_w_2, ada_b_2, norm_g_2, sc_w_in_2, sc_conv_2, sc_w_out_2,
        hy_w_in_2, hy_conv_2, hy_f_w1_2, hy_f_b1_2, hy_f_w2_2, hy_f_b2_2, hy_f_w3_2,
        hy_sin_freq_2, hy_skip_2, hy_w_out_2, at_w_qkv_2, at_q_g_2, at_k_g_2, at_w_o_2,
        moe_router_2, moe_w_gate_2, moe_w_up_2, moe_w_down_2,
    )


_drawn_inputs = setup_inputs


def setup_inputs(seed=0):
    import zlib

    import numpy as np

    out = dict(_drawn_inputs(seed))
    spreads = {}
    factors = {'gla_gate_bias': 3.004,
     'rwkv_w_up': 3.572,
     'rwkv_a0': 3.399,
     'rwkv_k_k': 2.676,
     'rwkv_ln_w': 2.889,
     'rwkv_ln_b': 6.505,
     'ada_b_2': 3.568,
     'norm_g_2': 4.091}
    for name, (base, spread) in spreads.items():
        noise = np.random.default_rng([zlib.crc32(name.encode()), seed]).standard_normal(out[name].shape)
        drawn = base * np.exp(spread * noise) if base else spread * noise
        out[name] = jnp.asarray(drawn.astype(out[name].dtype))
    for name, factor in factors.items():
        out[name] = (out[name] * factor).astype(out[name].dtype)
    return out
```

```python
from contextlib import ExitStack

import numpy as np

import concourse.bass as bass
from concourse import mybir

F32 = mybir.dt.float32
U32 = mybir.dt.uint32
ALU = mybir.AluOpType
ACT = mybir.ActivationFunctionType
AX = mybir.AxisListType

P = 128
T = 2048
D = 1024
KD = D // P
TT = T // P
Q = 4
QT = T // Q
EPS = 1e-6
C = 64
NCH = T // C
GLA_Q, GLA_K, GLA_V, GLA_LR, GLA_G = 0, 256, 512, 1024, 1040
RWKV0 = 1552
RW_R, RW_K, RW_V, RW_L, RW_G = RWKV0, RWKV0 + 512, RWKV0 + 1024, RWKV0 + 1536, RWKV0 + 1664
RANK = 16
DECAY = float(np.exp(-0.5))
NE, CAP = 16, 256
LEVELS = 5


class Shared:
    pass


class Line:

    def __init__(self, engine, chain):
        self.engine, self.chain, self.n = engine, chain, {}

    def __call__(self, instruction, signal=None):
        s = signal if signal is not None else self.chain
        self.n[s.num] = self.n.get(s.num, 0) + 1
        instruction.then_inc(s, 1)
        self.engine.wait_ge(s, self.n[s.num])


def semaphores(nc, ctx, names):
    return {name: ctx.enter_context(nc.semaphore(f"{ctx.name}_{name}")) for name in names}


def meet(nc, s):
    numbers = [x.num for x in s.values()]
    nc.all_engine_barrier(sems_to_clear=range(min(numbers), max(numbers) + 1))


class Phase(ExitStack):

    def __init__(self, name):
        super().__init__()
        self.name = name


def sb(nc, ctx, name, shape, dt=F32):
    return ctx.enter_context(nc.sbuf_tensor(f"{ctx.name}_{name}", shape, dt))


def modulation(nc, k, c_col, ada_w, ada_b, ada_b_col, norm_g, norm_g_col):
    with Phase("mod") as ctx:
        s = semaphores(nc, ctx, ["small", "w0", "w1", "chain_v", "chain_a", "silu", "used", "summed", "psum", "rows", "stored"])
        w = sb(nc, ctx, "ada_tile", [P, 2, 6 * D])
        acc = sb(nc, ctx, "ada_acc", [P, 6 * D])
        cc = sb(nc, ctx, "c_cols", [P, KD])
        b_col = sb(nc, ctx, "ada_b_cols", [P, 2 * KD])
        g_col = sb(nc, ctx, "norm_g_cols", [P, KD])
        rows = sb(nc, ctx, "mod_rows", [1, 4 * D])
        b_row = sb(nc, ctx, "ada_b_row", [1, 4 * D])
        g_row = sb(nc, ctx, "norm_g_row", [1, D])
        bank = k.bank
        with nc.Block() as block:
            @block.sync
            def _(sp):
                sp.dma_start(cc[:], c_col).then_inc(s["small"], 16)
                sp.dma_start(b_col[:], ada_b_col).then_inc(s["small"], 16)
                sp.dma_start(g_col[:], norm_g_col).then_inc(s["small"], 16)
                sp.dma_start(b_row[:], ada_b[:, 2 * D:]).then_inc(s["small"], 16)
                sp.dma_start(g_row[:], norm_g[1:2, :]).then_inc(s["small"], 16)
                sp.dma_start(k.mask_sb[:], k.mask_in).then_inc(s["small"], 16)
                for kb in range(KD):
                    if kb >= 2:
                        sp.wait_ge(s["used"], kb - 1)
                    sp.dma_start(w[:, kb % 2, :], ada_w[kb * P:(kb + 1) * P, :]).then_inc((s["w0"], s["w1"])[kb % 2], 16)
                sp.wait_ge(s["rows"], 6)
                sp.dma_start(k.rows_dram.rearrange("(a r) d -> a (r d)", a=1), rows[:]).then_inc(s["stored"], 16)
                sp.wait_ge(s["stored"], 16)

            @block.scalar
            def _(act):
                act.wait_ge(s["small"], 96)
                nc.scalar.activation(cc[:], cc[:], ACT.Silu).then_inc(s["silu"], 1)

            @block.vector
            def _(dve):
                go = Line(dve, s["chain_v"])
                go(nc.vector.memset(k.ones[:], 1.0))
                dve.wait_ge(s["silu"], 1)
                for kb in range(KD):
                    dve.wait_ge((s["w0"], s["w1"])[kb % 2], 16 * (kb // 2 + 1))
                    if kb == 0:
                        go(nc.vector.tensor_scalar(acc[:], w[:, 0, :], cc[:, 0:1], None, ALU.mult), s["used"])
                    else:
                        go(nc.vector.scalar_tensor_tensor(acc[:], w[:, kb % 2, :], cc[:, kb:kb + 1], acc[:],
                                                          ALU.mult, ALU.add), s["used"])
                dve.wait_ge(s["psum"], 1)
                go(nc.vector.tensor_tensor(k.shift1[:], bank[7][:, 0:KD], b_col[:, 0:KD], ALU.add))
                go(nc.vector.tensor_tensor(k.gain1[:], bank[7][:, KD:2 * KD], b_col[:, KD:2 * KD], ALU.add))
                go(nc.vector.tensor_scalar_add(k.gain1[:], k.gain1[:], 1.0))
                go(nc.vector.tensor_tensor(k.gain1[:], k.gain1[:], g_col[:], ALU.mult))
                dve.wait_ge(s["psum"], 2)
                for n in range(4):
                    for h in range(2):
                        at = n * D + h * 512
                        b = bank[(2 * n + h) % 4]
                        if n >= 2:
                            dve.wait_ge(s["psum"], 3)
                        ins = nc.vector.tensor_tensor(rows[0:1, at:at + 512], b[0:1, :], b_row[0:1, at:at + 512], ALU.add)
                        if h:
                            go(ins, s["rows"])
                        else:
                            go(ins)
                go(nc.vector.tensor_scalar_add(rows[0:1, 2 * D:3 * D], rows[0:1, 2 * D:3 * D], 1.0), s["rows"])
                go(nc.vector.tensor_tensor(rows[0:1, 2 * D:3 * D], rows[0:1, 2 * D:3 * D], g_row[:], ALU.mult), s["rows"])

            @block.tensor
            def _(pe):
                pe.wait_ge(s["used"], KD)
                for j in range(2 * KD):
                    mm = nc.tensor.matmul(bank[7][:, j:j + 1], acc[:, j * P:(j + 1) * P], k.ones[:, 0:1],
                                          start=True, stop=True)
                mm.then_inc(s["psum"], 1)
                for n in range(8):
                    if n == 4:
                        pe.wait_ge(s["rows"], 2)
                    at = 2 * D + n * 512
                    mm = nc.tensor.matmul(bank[n % 4][0:1, :], k.ones[:, 0:1], acc[:, at:at + 512], start=True, stop=True)
                    if n % 4 == 3:
                        mm.then_inc(s["psum"], 1)
        meet(nc, s)


def norm_stats(nc, go_a, go_v, act, dve, s_sq, s_var, s_sd, n, x, junk, stat, role):
    if role == "act":
        go_a(nc.scalar.activation(junk, x, ACT.Square, accum_out=stat[:, 0:1]), s_sq)
        act.wait_ge(s_var, n + 1)
        go_a(nc.scalar.activation(stat[:, 2:3], stat[:, 1:2], ACT.Sqrt), s_sd)
    else:
        dve.wait_ge(s_sq, n + 1)
        go_v(nc.vector.tensor_scalar(stat[:, 1:2], stat[:, 0:1], 1.0 / D, EPS, ALU.mult, ALU.add), s_var)
        dve.wait_ge(s_sd, n + 1)
        go_v(nc.vector.reciprocal(stat[:, 3:4], stat[:, 2:3]))


def first_norm(nc, k, x, hT, norm_w_col):
    G = 4
    xv = x.rearrange("b (g n p) d -> (b g) p n d", n=G, p=P)
    with Phase("nrm") as ctx:
        s = semaphores(nc, ctx, ["x0", "x1", "x2", "x3", "w", "chain_v", "chain_a", "sq", "var", "sd", "scaled", "turned", "kept"])
        xt = sb(nc, ctx, "x_tile", [P, G, D])
        junk = sb(nc, ctx, "square", [P, D])
        stat = sb(nc, ctx, "stat", [P, G, 4])
        wc = sb(nc, ctx, "norm_cols", [P, KD])
        bank = k.bank
        with nc.Fori(0, TT // G) as g:
            with nc.Block() as block:
                @block.sync
                def _(sp):
                    sp.dma_start(wc[:], norm_w_col).then_inc(s["w"], 16)
                    for n in range(G):
                        sp.dma_start(xt[:, n, :], xv[g, :, n, :]).then_inc((s["x0"], s["x1"], s["x2"], s["x3"])[n], 16)

                @block.scalar
                def _(act):
                    go = Line(act, s["chain_a"])
                    for n in range(G):
                        act.wait_ge((s["x0"], s["x1"], s["x2"], s["x3"])[n], 16)
                        norm_stats(nc, go, None, act, None, s["sq"], s["var"], s["sd"], n, xt[:, n, :], junk[:], stat[:, n, :], "act")

                @block.vector
                def _(dve):
                    go = Line(dve, s["chain_v"])
                    dve.wait_ge(s["w"], 16)

                    def keep(n):
                        for b in range(2):
                            dve.wait_ge(s["turned"], 2 * n + b + 1)
                            go(nc.vector.tensor_tensor(
                                hT[:, 4 * b:4 * b + 4, bass.ds(g * (G * P) + n * P, P)],
                                bank[2 * (n % 2) + b][:].rearrange("p (k t) -> p k t", t=P),
                                wc[:, 4 * b:4 * b + 4].unsqueeze(2).to_broadcast([P, 4, P]), ALU.mult), s["kept"])
                    for n in range(G):
                        norm_stats(nc, None, go, None, dve, s["sq"], s["var"], s["sd"], n, None, None, stat[:, n, :], "dve")
                        go(nc.vector.tensor_scalar(xt[:, n, :], xt[:, n, :], stat[:, n, 3:4], None, ALU.mult), s["scaled"])
                        if n:
                            keep(n - 1)
                    keep(G - 1)

                @block.tensor
                def _(pe):
                    for n in range(G):
                        pe.wait_ge(s["scaled"], n + 1)
                        if n >= 2:
                            pe.wait_ge(s["kept"], 2 * (n - 1))
                        for b in range(2):
                            for j in range(4):
                                kb = 4 * b + j
                                mm = nc.tensor.transpose(bank[2 * (n % 2) + b][:, j * P:(j + 1) * P],
                                                         xt[:, n, kb * P:(kb + 1) * P], k.ident[:])
                            mm.then_inc(s["turned"], 1)
            meet(nc, s)


def rwkv(nc, k, hT, w_in, w_up, a_up, cols, mu_lora_col, mT):
    HP = 4
    wv = w_in.rearrange("(kb p) n -> p kb n", p=P)
    with Phase("heads") as outer:
        lora = sb(nc, outer, "lora", [P, T])
        with Phase("lr") as ctx:
            s = semaphores(nc, ctx, ["w", "mu", "u", "chain_v", "chain_a", "raw", "mixed"])
            w = sb(nc, ctx, "lora_w", [P, KD, P])
            raw = sb(nc, ctx, "lora_raw", [P, T + 1])
            mu = sb(nc, ctx, "lora_mu", [P, 1])
            diff = sb(nc, ctx, "lora_diff", [P, T])
            bank = k.bank
            with nc.Block() as block:
                @block.sync
                def _(sp):
                    sp.dma_start(w[:], wv[:, :, RW_L:RW_L + P]).then_inc(s["w"], 16)
                    sp.dma_start(mu[:], mu_lora_col).then_inc(s["mu"], 16)

                @block.tensor
                def _(pe):
                    pe.wait_ge(s["w"], 16)
                    for q in range(Q):
                        for kb in range(KD):
                            mm = nc.tensor.matmul(bank[q][:], w[:, kb, :], hT[:, kb, q * QT:(q + 1) * QT],
                                                  start=(kb == 0), stop=(kb == KD - 1))
                        mm.then_inc(s["u"], 1)

                @block.scalar
                def _(act):
                    go = Line(act, s["chain_a"])
                    for q in range(Q):
                        act.wait_ge(s["u"], q + 1)
                        go(nc.scalar.activation(raw[:, 1 + q * QT:1 + (q + 1) * QT], bank[q][:], ACT.Copy), s["raw"])
                    act.wait_ge(s["mixed"], 1)
                    go(nc.scalar.activation(lora[0:64, :], lora[0:64, :], ACT.Tanh))

                @block.vector
                def _(dve):
                    go = Line(dve, s["chain_v"])
                    go(nc.vector.memset(raw[:, 0:1], 0.0))
                    dve.wait_ge(s["raw"], Q)
                    dve.wait_ge(s["mu"], 16)
                    go(nc.vector.tensor_tensor(diff[:], raw[:, 0:T], raw[:, 1:T + 1], ALU.subtract))
                    go(nc.vector.scalar_tensor_tensor(lora[:], diff[:], mu[:, 0:1], raw[:, 1:T + 1], ALU.mult, ALU.add), s["mixed"])
            meet(nc, s)

        with Phase("rw") as ctx:
            s = semaphores(nc, ctx, [
                "w0", "w1", "w2", "w3", "par", "lup", "u", "wa", "ssq", "bon", "chain_v", "chain_a", "chain_g",
                "raw", "raw_read", "gate", "sig", "cum", "exps", "sq", "sqrt", "forms", "kk_sq", "rk", "bonus",
                "tr", "tr_kept", "sc", "sc_kept", "nt", "a", "t", "e", "e_kept", "dt", "x", "x_kept", "wu", "wu_kept",
                "q", "q_kept", "gh", "gh_kept", "state_mm", "state", "y", "y_kept", "ysq", "yvar", "ysd", "ynorm",
                "yt", "affine", "out", "stored"])
            wt = [sb(nc, ctx, f"w_block{i}", [P, KD, P]) for i in range(2)]
            lup = sb(nc, ctx, "lora_up", [P, P])
            par = sb(nc, ctx, "head_params", [P, 12])
            raws = [sb(nc, ctx, f"raw{i}", [P, T + 1]) for i in range(2)]
            KT, BB = raws[0][:, 0:T], raws[1][:, 0:T]
            r, kx, v, sg, sw, a, cs = [sb(nc, ctx, n, [P, T]) for n in ("r", "kx", "v", "sg", "sw", "a", "cs")]
            PR = sb(nc, ctx, "PR", [P, TT, 2, P])
            Pc, Rc = PR[:, :, 0, :], PR[:, :, 1, :]
            tmp = sb(nc, ctx, "tmp", [P, T])
            Y = tmp[:].rearrange("p (j n) -> p j n", n=P)
            lc = sb(nc, ctx, "chunk_decay", [P, NCH])
            scm = a[:].rearrange("p (q n t) -> p q n t", q=4, n=4)
            tt = cs[:, 0:1024].rearrange("p (q n t) -> p q n t", q=4, n=2)
            eb = cs[:, 1024:1536].rearrange("p (q t) -> p q t", q=4)
            wun = cs[:, 1536:2048].rearrange("p (j u t) -> p j u t", j=2, u=2)
            ptm = r[:, 0:768].rearrange("p (j n t) -> p j n t", j=2, n=3)
            px = r[:, 768:1280].rearrange("p (q t) -> p q t", q=4)
            qp = r[:, 1280:1536].rearrange("p (j t) -> p j t", j=2)
            gt = r[:, 1536:2048].rearrange("p (j c t) -> p j c t", j=2, c=2)
            nt = sb(nc, ctx, "levels", [P, 4, LEVELS, P])
            hh = sb(nc, ctx, "H", [P, 2, 2, P])
            M = sb(nc, ctx, "state", [P, P])
            gst = sb(nc, ctx, "group_stat", [P, 3, 2 * TT])
            bank = k.bank
            mk = k.mask
            c3 = lambda ap: ap.rearrange("p (n c) -> p n c", c=P)
            with nc.Fori(0, HP) as hp:
                with nc.Block() as block:
                    firsts = (RW_R, RW_K, RW_V, RW_G)

                    @block.sync
                    def _(sp):
                        sp.dma_start(par[:], cols[hp]).then_inc(s["par"], 16)
                        sp.dma_start(lup[0:64, :], w_up[:, bass.ds(hp * P, P)]).then_inc(s["lup"], 16)
                        sp.dma_start(lup[64:128, :], a_up[:, bass.ds(hp * P, P)]).then_inc(s["lup"], 16)
                        for i, at in enumerate(firsts):
                            if i >= 2:
                                sp.wait_ge(s["u"], Q * (i - 1))
                            sp.dma_start(wt[i % 2][:], wv[:, :, bass.ds(hp * P + at, P)]).then_inc((s["w0"], s["w1"], s["w2"], s["w3"])[i], 16)
                        sp.wait_ge(s["out"], 1)
                        sp.dma_start(mT[hp + 4], tmp[:]).then_inc(s["stored"], 16)
                        sp.wait_ge(s["stored"], 16)

                    @block.tensor
                    def _(pe):
                        for i in range(4):
                            pe.wait_ge((s["w0"], s["w1"], s["w2"], s["w3"])[i], 16)
                            for q in range(Q):
                                if i >= 2:
                                    if i == 2:
                                        pe.wait_ge(s["raw"], q + 1)
                                    else:
                                        pe.wait_ge(s["raw"], Q + q + 1)
                                for kb in range(KD):
                                    mm = nc.tensor.matmul(bank[4 * (i % 2) + q][:], wt[i % 2][:, kb, :],
                                                          hT[:, kb, q * QT:(q + 1) * QT], start=(kb == 0), stop=(kb == KD - 1))
                                mm.then_inc(s["u"], 1)
                        pe.wait_ge(s["lup"], 32)
                        for i in range(2):
                            if i == 0:
                                pe.wait_ge(s["raw"], 3 * Q)
                            else:
                                pe.wait_ge(s["gate"], Q)
                            for q in range(Q):
                                nc.tensor.matmul(bank[4 * i + q][:], lup[64 * i:64 * i + 64, :],
                                                 lora[64 * i:64 * i + 64, q * QT:(q + 1) * QT], start=True, stop=True).then_inc(s["wa"], 1)
                        pe.wait_ge(s["kk_sq"], 1)
                        for q in range(Q):
                            nc.tensor.matmul(bank[q][:], k.mask("head_ones"), BB[:, q * QT:(q + 1) * QT], start=True, stop=True).then_inc(s["ssq"], 1)
                        pe.wait_ge(s["rk"], 1)
                        for q in range(Q):
                            nc.tensor.matmul(bank[4 + q][:], k.mask("head_ones"), tmp[:, q * QT:(q + 1) * QT], start=True, stop=True).then_inc(s["bon"], 1)
                        pe.wait_ge(s["forms"], 1)
                        for g in range(TT // 2):
                            for jj in range(2):
                                j = 2 * g + jj
                                ts = slice(j * P, (j + 1) * P)
                                if jj:
                                    pe.wait_ge(s["tr_kept"], j)
                                elif g:
                                    pe.wait_ge(s["y_kept"], j)
                                for n, src in enumerate((Pc[:, j, :], BB[:, ts], KT[:, ts], v[:, ts])):
                                    mm = nc.tensor.transpose(bank[0][:, n * P:(n + 1) * P], src, k.ident[:])
                                mm.then_inc(s["tr"], 1)
                                for h in range(2):
                                    q = 2 * j + h
                                    hs = slice(64 * h, 64 * h + 64)
                                    if q >= 2:
                                        pe.wait_ge(s["sc_kept"], q - 1)
                                    b = bank[1 + q % 2]
                                    rhs = PR[hs, j, :, :].rearrange("p a t -> p (a t)")
                                    nc.tensor.matmul(b[:, 0:256], BB[hs, ts], rhs, start=True, stop=True)
                                    nc.tensor.matmul(b[:, 256:512], KT[hs, ts], rhs, start=True, stop=True).then_inc(s["sc"], 1)
                                if g and not jj:
                                    pe.wait_ge(s["t"], g * (LEVELS + 1))
                                for h in range(2):
                                    hs = slice(64 * h, 64 * h + 64)
                                    mm = nc.tensor.matmul(bank[4 + h][:, jj * P:(jj + 1) * P], Pc[hs, j, :], BB[hs, ts], start=True, stop=True)
                                if jj:
                                    mm.then_inc(s["a"], 1)
                            for l in range(LEVELS):
                                pe.wait_ge(s["t"], g * (LEVELS + 1) + l + 1)
                                if l == 0:
                                    pe.wait_ge(s["nt"], 4 * (g + 1))
                                for p in range(4):
                                    mm = nc.tensor.matmul(bank[3][:, p * P:(p + 1) * P], nt[:, p, l, :], tt[:, p, 0, :], start=True, stop=True)
                                mm.then_inc(s["e"], 1)
                                pe.wait_ge(s["e_kept"], g * LEVELS + l + 1)
                                for p in range(4):
                                    b, o = bank[4 + p // 2], 256 * (p % 2)
                                    nc.tensor.matmul(b[:, o:o + P], tt[:, p, 1, :], eb[:, p, :], start=True, stop=True)
                                    mm = nc.tensor.matmul(b[:, o + P:o + 2 * P], eb[:, p, :], tt[:, p, 1, :], start=True, stop=True)
                                mm.then_inc(s["dt"], 1)
                            pe.wait_ge(s["tr_kept"], 2 * g + 2)
                            for p in range(4):
                                mm = nc.tensor.matmul(bank[6][:, p * 64:(p + 1) * 64], scm[:, p, 2, :],
                                                      ptm[:, p // 2, 2, 64 * (p % 2):64 * (p % 2) + 64], start=True, stop=True)
                            mm.then_inc(s["x"], 1)
                            pe.wait_ge(s["x_kept"], g + 1)
                            pe.wait_ge(s["t"], (g + 1) * (LEVELS + 1))
                            for p in range(4):
                                mm = nc.tensor.matmul(bank[6][:, p * P:(p + 1) * P], tt[:, p, 1, :], px[:, p, :], start=True, stop=True)
                            mm.then_inc(s["wu"], 1)
                            pe.wait_ge(s["wu_kept"], 2 * (g + 1))
                            for p in range(4):
                                jj, h = p // 2, p % 2
                                mm = nc.tensor.matmul(bank[6][64 * h:64 * h + 64, jj * P:(jj + 1) * P],
                                                      wun[:, jj, 0, 64 * h:64 * h + 64], scm[:, p, 1, :], start=True, stop=True)
                            mm.then_inc(s["q"], 1)
                            pe.wait_ge(s["q_kept"], g + 1)
                            for jj in range(2):
                                j = 2 * g + jj
                                for c in range(2):
                                    cr = slice(64 * c, 64 * c + 64)
                                    nc.tensor.matmul(bank[1 + c][:, 0:P], wun[cr, jj, 0, :], ptm[cr, jj, 0, :], start=True, stop=True)
                                for c in range(2):
                                    cr = slice(64 * c, 64 * c + 64)
                                    nc.tensor.matmul(bank[1 + c][:, P:2 * P], ptm[cr, jj, 1, :], ptm[cr, jj, 2, :], start=True, stop=False)
                                    mm = nc.tensor.matmul(bank[1 + c][:, P:2 * P], ptm[cr, jj, 0, :], wun[cr, jj, 1, :], start=False, stop=True)
                                mm.then_inc(s["gh"], 1)
                                pe.wait_ge(s["gh_kept"], j + 1)
                                if jj == 1:
                                    pe.wait_ge(s["y_kept"], j)
                                for h in range(2):
                                    p = 2 * jj + h
                                    hs = slice(64 * h, 64 * h + 64)
                                    nc.tensor.matmul(bank[0][:, hs], scm[:, p, 3, :], ptm[:, jj, 2, hs], start=(h == 0), stop=False, skip_group_check=True)
                                    nc.tensor.matmul(bank[0][:, hs], scm[:, p, 1, :], wun[:, jj, 1, hs], start=False, stop=False, skip_group_check=True)
                                for c in range(2):
                                    n = 2 * j + c
                                    pe.wait_ge(s["state"], n + 1)
                                    cr = slice(64 * c, 64 * c + 64)
                                    mm = nc.tensor.matmul(bank[0][cr, 0:P], qp[:, jj, cr], M[:], start=False, stop=True, skip_group_check=True)
                                    if c:
                                        mm.then_inc(s["y"], 1)
                                    nc.tensor.matmul(bank[7][:, 0:P], gt[:, jj, c, :], M[:], start=True, stop=True).then_inc(s["state_mm"], 1)
                        pe.wait_ge(s["ynorm"], 1)
                        pe.wait_ge(s["state"], 2 * TT + 1)
                        for q in range(Q):
                            for j in range(4):
                                mm = nc.tensor.transpose(bank[q][:, j * P:(j + 1) * P], Y[:, 4 * q + j, :], k.ident[:])
                            mm.then_inc(s["yt"], 1)

                    @block.scalar
                    def _(act):
                        go = Line(act, s["chain_a"])
                        for i in range(3):
                            if i == 2:
                                act.wait_ge(s["raw_read"], 1)
                            for q in range(Q):
                                act.wait_ge(s["u"], Q * i + q + 1)
                                go(nc.scalar.activation(raws[i % 2][:, 1 + q * QT:1 + (q + 1) * QT], bank[4 * (i % 2) + q][:], ACT.Copy), s["raw"])
                        for q in range(Q):
                            act.wait_ge(s["u"], 3 * Q + q + 1)
                            go(nc.scalar.activation(sg[:, q * QT:(q + 1) * QT], bank[4 + q][:], ACT.Silu), s["gate"])
                        act.wait_ge(s["par"], 16)
                        for i, (dst, bias) in enumerate(((sw, 3), (a, 4))):
                            for q in range(Q):
                                act.wait_ge(s["wa"], Q * i + q + 1)
                                go(nc.scalar.activation(dst[:, q * QT:(q + 1) * QT], bank[4 * i + q][:], ACT.Sigmoid, bias=par[:, bias:bias + 1]), s["sig"])
                        act.wait_ge(s["cum"], 1)
                        go(nc.scalar.activation(Rc, cs[:].rearrange("p (j t) -> p j t", t=P), ACT.Exp, scale=-DECAY))
                        go(nc.scalar.activation(KT, cs[:], ACT.Exp, scale=DECAY))
                        act.wait_ge(s["cum"], 2)
                        go(nc.scalar.activation(Pc, tmp[:].rearrange("p (j t) -> p j t", t=P), ACT.Exp, scale=-DECAY), s["exps"])
                        act.wait_ge(s["sq"], 1)
                        go(nc.scalar.activation(BB, tmp[:], ACT.Square), s["kk_sq"])
                        for q in range(Q):
                            act.wait_ge(s["ssq"], q + 1)
                        for q in range(Q):
                            go(nc.scalar.activation(BB[:, q * QT:(q + 1) * QT], bank[q][:], ACT.Sqrt), s["sqrt"])
                        for g in range(TT // 2):
                            for l in range(LEVELS):
                                act.wait_ge(s["e"], g * LEVELS + l + 1)
                                go(nc.scalar.activation(eb, c3(bank[3][:]), ACT.Copy), s["e_kept"])
                            act.wait_ge(s["x"], g + 1)
                            go(nc.scalar.activation(px[:, :, 64:128], bank[6][:, 0:256].rearrange("p (n c) -> p n c", c=64), ACT.Copy), s["x_kept"])
                            act.wait_ge(s["wu"], g + 1)
                            for jj in range(2):
                                src = bank[6][:, jj * 256:(jj + 1) * 256].rearrange("p (h u c) -> p u h c", h=2, u=2)
                                go(nc.scalar.activation(wun[:, jj, :, :].rearrange("p u (h c) -> p u h c", h=2), src, ACT.Copy, scale=-1.0), s["wu_kept"])
                            for jj in range(2):
                                j = 2 * g + jj
                                act.wait_ge(s["y"], j + 1)
                                go(nc.scalar.activation(Y[:, j, :], bank[0][:, 0:P], ACT.Copy), s["y_kept"])
                        act.wait_ge(s["yvar"], 1)
                        go(nc.scalar.activation(gst[:, 2, :], gst[:, 1, :], ACT.Sqrt), s["ysd"])

                    @block.vector
                    def _(dve):
                        go = Line(dve, s["chain_v"])
                        dve.wait_ge(s["par"], 16)
                        for i in range(2):
                            go(nc.vector.memset(raws[i][:, 0:1], 0.0))
                        go(nc.vector.memset(M[:], 0.0), s["state"])
                        for i, dst in enumerate((r, kx, v)):
                            dve.wait_ge(s["raw"], Q * (i + 1))
                            raw = raws[i % 2]
                            go(nc.vector.tensor_tensor(tmp[:], raw[:, 0:T], raw[:, 1:T + 1], ALU.subtract))
                            go(nc.vector.scalar_tensor_tensor(dst[:], tmp[:], par[:, i:i + 1], raw[:, 1:T + 1], ALU.mult, ALU.add),
                               s["raw_read"])
                        dve.wait_ge(s["sig"], Q)
                        for n in range(NCH):
                            ins = nc.vector.tensor_tensor_scan(cs[:, n * C:(n + 1) * C], k.chunk_ones[:], sw[:, n * C:(n + 1) * C], 0.0, ALU.mult, ALU.add)
                        go(ins, s["cum"])
                        go(nc.vector.tensor_tensor(tmp[:], cs[:], sw[:], ALU.subtract), s["cum"])
                        dve.wait_ge(s["exps"], 1)
                        go(nc.vector.tensor_scalar(tmp[:], kx[:], par[:, 5:6], None, ALU.mult), s["sq"])
                        dve.wait_ge(s["sqrt"], Q)
                        go(nc.vector.tensor_scalar_max(BB, BB, 1e-12))
                        go(nc.vector.reciprocal(BB, BB))
                        go(nc.vector.tensor_tensor(tmp[:], tmp[:], BB, ALU.mult))
                        t3 = lambda ap: ap.rearrange("p (j t) -> p j t", t=P)
                        go(nc.vector.tensor_copy(lc[:], PR[:, :, 1, :].rearrange("p j (c t) -> p j c t", c=2)[:, :, :, C - 1]))
                        go(nc.vector.tensor_tensor(Pc, Pc, t3(tmp[:]), ALU.mult))
                        go(nc.vector.tensor_tensor(BB, tmp[:], a[:], ALU.mult))
                        go(nc.vector.tensor_tensor(BB, BB, KT, ALU.mult))
                        dve.wait_ge(s["sig"], 2 * Q)
                        go(nc.vector.tensor_scalar(a[:], a[:], -1.0, par[:, 6:7], ALU.add, ALU.mult))
                        go(nc.vector.scalar_tensor_tensor(kx[:], a[:], 1.0, kx[:], ALU.add, ALU.mult))
                        go(nc.vector.tensor_tensor(KT, KT, kx[:], ALU.mult))
                        go(nc.vector.tensor_tensor(Rc, Rc, t3(r[:]), ALU.mult))
                        go(nc.vector.scalar_tensor_tensor(tmp[:], r[:], par[:, 7:8], kx[:], ALU.mult, ALU.mult), s["rk"])
                        for q in range(Q):
                            dve.wait_ge(s["bon"], q + 1)
                            ins = nc.vector.tensor_tensor(sw[:, q * QT:(q + 1) * QT], bank[4 + q][:], v[:, q * QT:(q + 1) * QT], ALU.mult)
                            go(ins, s["forms"] if q == Q - 1 else None)
                        for g in range(TT // 2):
                            for jj in range(2):
                                j = 2 * g + jj
                                dve.wait_ge(s["tr"], j + 1)
                                go(nc.vector.tensor_copy(ptm[:, jj, :, :], c3(bank[0][:, P:512])))
                                go(nc.vector.tensor_copy(px[:, 2 * jj:2 * jj + 2, 0:64], bank[0][:, 0:P].rearrange("p (h c) -> p h c", h=2)), s["tr_kept"])
                                for h in range(2):
                                    p = 2 * jj + h
                                    q = 2 * j + h
                                    dve.wait_ge(s["sc"], q + 1)
                                    go(nc.vector.tensor_tensor(scm[:, p, :, :], c3(bank[1 + q % 2][:]), c3(mk("scores")), ALU.mult), s["sc_kept"])
                            dve.wait_ge(s["a"], g + 1)
                            n1t = mk("corner_t").unsqueeze(1).to_broadcast([P, 4, P])
                            one = k.ident[:].unsqueeze(1).to_broadcast([P, 4, P])
                            for h in range(2):
                                go(nc.vector.tensor_tensor(tt[:, h::2, 0, :], c3(bank[4 + h][:, 0:256]), mk("corner").unsqueeze(1).to_broadcast([P, 2, P]), ALU.mult))
                            go(nc.vector.tensor_tensor(tt[:, :, 0, :], tt[:, :, 0, :], one, ALU.add))
                            go(nc.vector.tensor_tensor(tt[:, :, 1, :], scm[:, :, 0, :], n1t, ALU.mult))
                            go(nc.vector.tensor_tensor(tt[:, :, 1, :], tt[:, :, 1, :], one, ALU.add), s["t"])
                            for l in range(LEVELS):
                                dve.wait_ge(s["dt"], g * LEVELS + l + 1)
                                for b in range(2):
                                    dst = tt[:, 2 * b:2 * b + 2, :, :].rearrange("p n a t -> p (n a t)")
                                    ins = nc.vector.tensor_tensor(dst, dst, bank[4 + b][:], ALU.add)
                                    if b:
                                        go(ins, s["t"])
                                    else:
                                        go(ins)
                            dve.wait_ge(s["q"], g + 1)
                            go(nc.vector.tensor_tensor(qp, c3(bank[6][:, 0:256]), PR[:, 2 * g:2 * g + 2, 1, :], ALU.add), s["q_kept"])
                            for jj in range(2):
                                j = 2 * g + jj
                                dve.wait_ge(s["gh"], j + 1)
                                hd = mk("heads").unsqueeze(1).to_broadcast([P, 2, P])
                                for c in range(2):
                                    go(nc.vector.tensor_tensor(gt[:, jj, c], bank[1 + c][:, 0:P], k.ident[:], ALU.add))
                                go(nc.vector.tensor_tensor(gt[:, jj], gt[:, jj], hd, ALU.mult))
                                for c in range(2):
                                    n = 2 * j + c
                                    ins = nc.vector.scalar_tensor_tensor(hh[:, jj, c, :], bank[1 + c][:, P:2 * P], lc[:, n:n + 1], mk("heads"), ALU.mult, ALU.mult)
                                    if c:
                                        go(ins, s["gh_kept"])
                                    else:
                                        go(ins)
                                for c in range(2):
                                    n = 2 * j + c
                                    dve.wait_ge(s["state_mm"], n + 1)
                                    go(nc.vector.scalar_tensor_tensor(M[:], bank[7][:, 0:P], lc[:, n:n + 1], hh[:, jj, c, :], ALU.mult, ALU.add), s["state"])
                        dve.wait_ge(s["y_kept"], TT)
                        Yg = tmp[:].rearrange("p (g n) -> p g n", n=64)
                        KTg = KT.rearrange("p (g n) -> p g n", n=64)
                        NG = 2 * TT
                        bc = lambda i: gst[:, i, :].unsqueeze(2).to_broadcast([P, NG, 64])
                        go(nc.vector.tensor_reduce(gst[:, 0, :], Yg, AX.X, ALU.add))
                        go(nc.vector.tensor_scalar(gst[:, 0, :], gst[:, 0, :], 1.0 / 64, None, ALU.mult))
                        go(nc.vector.tensor_tensor(Yg, Yg, bc(0), ALU.subtract))
                        go(nc.vector.tensor_tensor(KT, tmp[:], tmp[:], ALU.mult))
                        go(nc.vector.tensor_reduce(gst[:, 1, :], KTg, AX.X, ALU.add))
                        go(nc.vector.tensor_scalar(gst[:, 1, :], gst[:, 1, :], 1.0 / 64, 64e-5, ALU.mult, ALU.add), s["yvar"])
                        dve.wait_ge(s["ysd"], 1)
                        go(nc.vector.reciprocal(gst[:, 0, :], gst[:, 2, :]))
                        go(nc.vector.tensor_tensor(Yg, Yg, bc(0), ALU.mult), s["ynorm"])
                        dve.wait_ge(s["yt"], Q)
                        for q in range(Q):
                            qs = slice(q * QT, (q + 1) * QT)
                            go(nc.vector.tensor_scalar(tmp[:, qs], bank[q][:], par[:, 8:9], par[:, 9:10], ALU.mult, ALU.add))
                        go(nc.vector.tensor_tensor(tmp[:], tmp[:], sw[:], ALU.add))
                        go(nc.vector.tensor_tensor(tmp[:], tmp[:], sg[:], ALU.mult), s["out"])

                    @block.gpsimd
                    def _(pool):
                        go = Line(pool, s["chain_g"])
                        lm = mk("levels").rearrange("p (l t) -> p l t", t=P)
                        for g in range(TT // 2):
                            for p in range(4):
                                pool.wait_ge(s["sc_kept"], 4 * g + p + 1)
                                if g:
                                    pool.wait_ge(s["t"], g * (LEVELS + 1))
                                go(nc.gpsimd.tensor_tensor(nt[:, p, :, :], scm[:, p, 0, :].unsqueeze(1).to_broadcast([P, LEVELS, P]), lm, ALU.mult), s["nt"])
                meet(nc, s)


def gla(nc, k, hT, w_in, gate_up, gate_bias_col, norm_col, mT):
    wv = w_in.rearrange("(kb p) n -> p kb n", p=P)
    with Phase("gl") as ctx:
        s = semaphores(nc, ctx, [
            "w0", "w1", "w2", "w3", "w4", "w5", "wl", "par", "par2", "par3", "u", "lr", "lr_kept", "z", "kept", "zk", "chain_v", "chain_a",
            "ab", "ez", "ln", "cum", "exps", "forms", "tr", "tr_kept", "sc", "sc_kept", "ds", "state", "o", "o_kept",
            "osq", "ovar", "osd", "onorm", "ot", "out0", "out", "stored"])
        wt = [sb(nc, ctx, f"w_block{i}", [P, KD, P]) for i in range(2)]
        wl = sb(nc, ctx, "w_lr", [P, KD, RANK])
        gup = sb(nc, ctx, "gate_up", [RANK, P])
        gb = sb(nc, ctx, "gate_bias", [P, 1])
        nw = sb(nc, ctx, "norm_col", [P, 1])
        glr = sb(nc, ctx, "glr", [RANK, T])
        qx, kx, v0, v1, g0, g1, cs, z = [sb(nc, ctx, n, [P, T]) for n in ("qx", "kx", "v0", "v1", "g0", "g1", "cs", "z")]
        kst = sb(nc, ctx, "kst", [P, T])
        lc = sb(nc, ctx, "chunk_decay", [P, NCH])
        tm = sb(nc, ctx, "tm", [P, 2, 3, P])
        scm = sb(nc, ctx, "scores", [P, 2, 2, P])
        S = sb(nc, ctx, "state", [P, 2, P])
        O = [sb(nc, ctx, f"o{h}", [P, TT, P]) for h in range(2)]
        st = sb(nc, ctx, "o_stat", [P, 3, 2 * TT])
        bank = k.bank
        with nc.Fori(0, 2) as gp:
            with nc.Block() as block:
                @block.sync
                def _(sp):
                    sp.dma_start(wl[:], wv[:, :, GLA_LR:GLA_LR + RANK]).then_inc(s["wl"], 16)
                    sp.dma_start(gup[:], gate_up[:, bass.ds(gp * P, P)]).then_inc(s["par"], 16)
                    sp.dma_start(gb[:], gate_bias_col[gp]).then_inc(s["par2"], 16)
                    sp.dma_start(nw[:], norm_col).then_inc(s["par3"], 16)
                    ats = (gp * P + GLA_Q, gp * P + GLA_K, gp * 256 + GLA_V, gp * 256 + (GLA_V + P), gp * 256 + GLA_G, gp * 256 + (GLA_G + P))
                    for i, at in enumerate(ats):
                        if i >= 2:
                            sp.wait_ge(s["u"], Q * (i - 1))
                        sp.dma_start(wt[i % 2][:], wv[:, :, bass.ds(at, P)]).then_inc((s["w0"], s["w1"], s["w2"], s["w3"], s["w4"], s["w5"])[i], 16)
                    sp.wait_ge(s["out"], 1)
                    sp.dma_start(mT[gp * 2], g0[:]).then_inc(s["stored"], 16)
                    sp.dma_start(mT[gp * 2 + 1], g1[:]).then_inc(s["stored"], 16)
                    sp.wait_ge(s["stored"], 32)

                @block.tensor
                def _(pe):
                    for i in range(6):
                        pe.wait_ge((s["w0"], s["w1"], s["w2"], s["w3"], s["w4"], s["w5"])[i], 16)
                        for q in range(Q):
                            if i >= 2:
                                pe.wait_ge(s["kept"], Q * (i - 2) + q + 1)
                            for kb in range(KD):
                                mm = nc.tensor.matmul(bank[4 * (i % 2) + q][:], wt[i % 2][:, kb, :],
                                                      hT[:, kb, q * QT:(q + 1) * QT], start=(kb == 0), stop=(kb == KD - 1))
                            mm.then_inc(s["u"], 1)
                    pe.wait_ge(s["wl"], 16)
                    pe.wait_ge(s["kept"], 5 * Q)
                    for q in range(Q):
                        for kb in range(KD):
                            mm = nc.tensor.matmul(bank[q][0:RANK, :], wl[:, kb, :], hT[:, kb, q * QT:(q + 1) * QT],
                                                  start=(kb == 0), stop=(kb == KD - 1))
                        mm.then_inc(s["lr"], 1)
                    pe.wait_ge(s["par"], 16)
                    pe.wait_ge(s["kept"], 6 * Q)
                    for q in range(Q):
                        pe.wait_ge(s["lr_kept"], q + 1)
                        nc.tensor.matmul(bank[4 + q][:], gup[:], glr[:, q * QT:(q + 1) * QT], start=True, stop=True).then_inc(s["z"], 1)
                    pe.wait_ge(s["forms"], 1)
                    for j in range(TT):
                        ts = slice(j * P, (j + 1) * P)
                        jj = j % 2
                        if j >= 2:
                            pe.wait_ge(s["tr_kept"], j - 1)
                        for n, src in enumerate((kst[:, ts], v0[:, ts], v1[:, ts])):
                            mm = nc.tensor.transpose(bank[7 * jj][:, n * P:(n + 1) * P], src, k.ident[:])
                        mm.then_inc(s["tr"], 1)
                        if j:
                            pe.wait_ge(s["sc_kept"], j)
                        for h in range(2):
                            hs = slice(64 * h, 64 * h + 64)
                            mm = nc.tensor.matmul(bank[1 + h][:, 0:P], kx[hs, ts], qx[hs, ts], start=True, stop=True)
                        mm.then_inc(s["sc"], 1)
                        pe.wait_ge(s["sc_kept"], j + 1)
                        pe.wait_ge(s["tr_kept"], j + 1)
                        if j:
                            pe.wait_ge(s["o_kept"], j)
                        for h in range(2):
                            nc.tensor.matmul(bank[3 + h][:, 0:P], scm[:, jj, h, :], tm[:, jj, 1 + h, :],
                                             start=True, stop=False, skip_group_check=True)
                        for c in range(2):
                            n = 2 * j + c
                            cr = slice(64 * c, 64 * c + 64)
                            pe.wait_ge(s["state"], n + 1)
                            for h in range(2):
                                hs = slice(64 * h, 64 * h + 64)
                                nc.tensor.matmul(bank[5 + c][hs, 0:P], tm[cr, jj, 0, hs], tm[cr, jj, 1 + h, :], start=True, stop=True)
                            for h in range(2):
                                hs = slice(64 * h, 64 * h + 64)
                                mm = nc.tensor.matmul(bank[3 + h][cr, 0:P], qx[hs, j * P + 64 * c:j * P + 64 * c + 64],
                                                      S[hs, n % 2, :], start=False, stop=True, skip_group_check=True)
                            mm.then_inc(s["ds"], 1)
                    pe.wait_ge(s["onorm"], 1)
                    for h in range(2):
                        for q in range(Q):
                            for j in range(4):
                                mm = nc.tensor.transpose(bank[4 * h + q][:, j * P:(j + 1) * P], O[h][:, 4 * q + j, :], k.ident[:])
                            mm.then_inc(s["ot"], 1)

                @block.scalar
                def _(act):
                    go = Line(act, s["chain_a"])
                    for i, (dst, fn, sc) in enumerate(((qx, ACT.Copy, 0.125), (kx, ACT.Copy, 1.0), (v0, ACT.Copy, 1.0),
                                                       (v1, ACT.Copy, 1.0), (g0, ACT.Silu, 1.0), (g1, ACT.Silu, 1.0))):
                        for q in range(Q):
                            act.wait_ge(s["u"], Q * i + q + 1)
                            go(nc.scalar.activation(dst[:, q * QT:(q + 1) * QT], bank[4 * (i % 2) + q][:], fn, scale=sc), s["kept"])
                    for q in range(Q):
                        act.wait_ge(s["lr"], q + 1)
                        go(nc.scalar.activation(glr[:, q * QT:(q + 1) * QT], bank[q][0:RANK, :], ACT.Copy), s["lr_kept"])
                    act.wait_ge(s["par2"], 16)
                    for q in range(Q):
                        act.wait_ge(s["z"], q + 1)
                        go(nc.scalar.activation(z[:, q * QT:(q + 1) * QT], bank[4 + q][:], ACT.Identity, bias=gb[:, 0:1]), s["zk"])
                    go(nc.scalar.activation(cs[:], z[:], ACT.Abs))
                    go(nc.scalar.activation(cs[:], cs[:], ACT.Exp, scale=-1.0))
                    go(nc.scalar.activation(cs[:], cs[:], ACT.Ln, bias=1.0), s["ln"])
                    act.wait_ge(s["cum"], 2)
                    go(nc.scalar.activation(O[0][:].rearrange("p j t -> p (j t)"), cs[:], ACT.Exp))
                    go(nc.scalar.activation(O[1][:].rearrange("p j t -> p (j t)"), cs[:], ACT.Exp, scale=-1.0))
                    go(nc.scalar.activation(kst[:], z[:], ACT.Exp), s["exps"])
                    for j in range(TT):
                        jj = j % 2
                        act.wait_ge(s["tr"], j + 1)
                        if j >= 2:
                            act.wait_ge(s["ds"], 2 * (j - 1))
                        go(nc.scalar.activation(tm[:, jj, :, :], bank[7 * jj][:, 0:3 * P].rearrange("p (n c) -> p n c", c=P), ACT.Copy), s["tr_kept"])
                        act.wait_ge(s["ds"], 2 * (j + 1))
                        for h in range(2):
                            ins = nc.scalar.activation(O[h][:, j, :], bank[3 + h][:, 0:P], ACT.Copy)
                            if h:
                                go(ins, s["o_kept"])
                            else:
                                go(ins)
                    go(nc.scalar.activation(z[:], O[0][:].rearrange("p j t -> p (j t)"), ACT.Square))
                    go(nc.scalar.activation(cs[:], O[1][:].rearrange("p j t -> p (j t)"), ACT.Square), s["osq"])
                    act.wait_ge(s["ovar"], 1)
                    go(nc.scalar.activation(st[:, 1, :], st[:, 0, :], ACT.Sqrt), s["osd"])

                @block.vector
                def _(dve):
                    go = Line(dve, s["chain_v"])
                    go(nc.vector.memset(S[:, 0, :], 0.0), s["state"])
                    dve.wait_ge(s["ln"], 1)
                    go(nc.vector.tensor_scalar(z[:], z[:], 0.0, None, ALU.min))
                    go(nc.vector.tensor_tensor(z[:], z[:], cs[:], ALU.subtract))
                    go(nc.vector.tensor_scalar(z[:], z[:], 1.0 / 16, None, ALU.mult))
                    for n in range(NCH):
                        ins = nc.vector.tensor_tensor_scan(cs[:, n * C:(n + 1) * C], k.chunk_ones[:], z[:, n * C:(n + 1) * C], 0.0, ALU.mult, ALU.add)
                    go(ins, s["cum"])
                    csn = cs[:].rearrange("p (n t) -> p n t", t=C)
                    go(nc.vector.tensor_copy(lc[:], csn[:, :, C - 1]))
                    go(nc.vector.tensor_tensor(z[:].rearrange("p (n t) -> p n t", t=C), lc[:].unsqueeze(2).to_broadcast([P, NCH, C]), csn, ALU.subtract), s["cum"])
                    dve.wait_ge(s["exps"], 1)
                    e0, e1 = [O[h][:].rearrange("p j t -> p (j t)") for h in range(2)]
                    go(nc.vector.tensor_copy(lc[:], e0.rearrange("p (n t) -> p n t", t=C)[:, :, C - 1]))
                    go(nc.vector.tensor_tensor(kst[:], kst[:], kx[:], ALU.mult))
                    go(nc.vector.tensor_tensor(kx[:], kx[:], e1, ALU.mult))
                    go(nc.vector.tensor_tensor(qx[:], qx[:], e0, ALU.mult), s["forms"])
                    for j in range(TT):
                        jj = j % 2
                        dve.wait_ge(s["sc"], j + 1)
                        if j >= 2:
                            dve.wait_ge(s["ds"], 2 * (j - 1))
                        for h in range(2):
                            ins = nc.vector.tensor_tensor(scm[:, jj, h, :], bank[1 + h][:, 0:P], k.mask("inclusive"), ALU.mult)
                            go(ins, s["sc_kept"] if h else None)
                        for c in range(2):
                            n = 2 * j + c
                            dve.wait_ge(s["ds"], n + 1)
                            go(nc.vector.scalar_tensor_tensor(S[:, (n + 1) % 2, :], S[:, n % 2, :], lc[:, n:n + 1], bank[5 + c][:, 0:P], ALU.mult, ALU.add), s["state"])
                    dve.wait_ge(s["osq"], 1)
                    for h, sq in enumerate((z, cs)):
                        go(nc.vector.tensor_reduce(st[:, 0, h * TT:(h + 1) * TT], sq[:].rearrange("p (j t) -> p j t", t=P), AX.X, ALU.add))
                    go(nc.vector.tensor_scalar(st[:, 0, :], st[:, 0, :], 1.0 / P, EPS, ALU.mult, ALU.add), s["ovar"])
                    dve.wait_ge(s["osd"], 1)
                    go(nc.vector.reciprocal(st[:, 2, :], st[:, 1, :]))
                    for h in range(2):
                        ins = nc.vector.tensor_tensor(O[h][:], O[h][:], st[:, 2, h * TT:(h + 1) * TT].unsqueeze(2).to_broadcast([P, TT, P]), ALU.mult)
                        if h:
                            go(ins, s["onorm"])
                        else:
                            go(ins)
                    dve.wait_ge(s["par3"], 16)
                    for h, g in enumerate((g0, g1)):
                        for q in range(Q):
                            dve.wait_ge(s["ot"], 4 * h + q + 1)
                            qs = slice(q * QT, (q + 1) * QT)
                            ins = nc.vector.scalar_tensor_tensor(g[:, qs], bank[4 * h + q][:], nw[:, 0:1], g[:, qs], ALU.mult, ALU.mult)
                            if h and q == Q - 1:
                                go(ins, s["out"])
                            else:
                                go(ins)
            meet(nc, s)


def out_product(nc, k, mT, w, resid, gate_row, norm_row, shift_row, store, turn_dst, gain, shift, final):
    first = final is not None
    G = 4
    rv = resid.rearrange("(g n p) d -> g p n d", n=G, p=P)
    mv = mT.rearrange("kb p (g t) -> g p kb t", g=TT // G)
    with Phase("op" if first else "oq") as ctx:
        names = ["m", "w", "rows", "r0", "r1", "r2", "r3", "y", "y_read", "chain_v", "chain_a", "sq", "var", "sd", "sq2", "var2", "sd2",
                 "lat", "h", "turned", "kept", "logit", "exp", "row_stat", "aff", "aff_t", "aff_kept", "st_lat", "st_h0", "st_h1"]
        s = semaphores(nc, ctx, names)
        wt = sb(nc, ctx, "w_out", [P, KD, D])
        mt = sb(nc, ctx, "m_tile", [P, KD, G * P])
        x = sb(nc, ctx, "x_tile", [P, G, D])
        h = sb(nc, ctx, "h_tile", [P, 2, D])
        junk = sb(nc, ctx, "square", [P, D])
        stat = sb(nc, ctx, "stat", [P, G, 8])
        row_a = sb(nc, ctx, "row_a", [P, D])
        if not first:
            gated = sb(nc, ctx, "gated", [P, D])
            row_g = sb(nc, ctx, "row_gain", [P, D])
            row_s = sb(nc, ctx, "row_shift", [P, D])
            hT2 = sb(nc, ctx, "h2_turned", [P, KD, P])
            lg = sb(nc, ctx, "softmax", [P, 2, NE])
            ls = sb(nc, ctx, "softmax_stat", [P, 2, 4])
            router = sb(nc, ctx, "router", [P, KD, NE])
        bank = k.bank
        rs = (s["r0"], s["r1"], s["r2"], s["r3"])
        with nc.Block() as block:
            @block.sync
            def _(sp):
                sp.dma_start(wt[:], w.rearrange("(kb p) n -> p kb n", p=P)).then_inc(s["w"], 16)
                if first:
                    sp.dma_start(row_a[:], norm_row.to_broadcast([P, D])).then_inc(s["rows"], 16)
                else:
                    sp.dma_start(row_a[:], gate_row.to_broadcast([P, D])).then_inc(s["rows"], 16)
                    sp.dma_start(row_g[:], norm_row.to_broadcast([P, D])).then_inc(s["rows"], 16)
                    sp.dma_start(row_s[:], shift_row.to_broadcast([P, D])).then_inc(s["rows"], 16)
                    sp.dma_start(router[:], k.router.rearrange("(kb p) n -> p kb n", p=P)).then_inc(s["rows"], 16)
                sp.wait_ge(s["w"], 16)
                sp.wait_ge(s["rows"], 16 if first else 64)
        meet(nc, s)
        with nc.Fori(0, TT // G) as g:
            with nc.Block() as block:
                @block.sync
                def _(sp):
                    sp.dma_start(mt[:], mv[g]).then_inc(s["m"], 16)
                    for n in range(G):
                        sp.dma_start(x[:, n, :], rv[g, :, n, :]).then_inc(rs[n], 16)
                    sv = store.rearrange("(g n p) d -> g p n d", n=G, p=P)
                    hv = k.h2.rearrange("(g n p) d -> g p n d", n=G, p=P)
                    for n in range(G):
                        sp.wait_ge(s["lat"], n + 1)
                        sp.dma_start(sv[g, :, n, :], x[:, n, :]).then_inc(s["st_lat"], 16)
                        if not first:
                            sp.wait_ge(s["h"], n + 1)
                            sp.dma_start(hv[g, :, n, :], h[:, n % 2, :]).then_inc((s["st_h0"], s["st_h1"])[n % 2], 16)
                    sp.wait_ge(s["st_lat"], 16 * G)
                    if not first:
                        sp.wait_ge(s["st_h0"], 32)
                        sp.wait_ge(s["st_h1"], 32)

                @block.tensor
                def _(pe):
                    pe.wait_ge(s["m"], 16)

                    def product(n):
                        if n:
                            pe.wait_ge(s["y_read"], 2 * n)
                        for b in range(2):
                            for kb in range(KD):
                                mm = nc.tensor.matmul(bank[b][:], mt[:, kb, n * P:(n + 1) * P], wt[:, kb, b * 512:(b + 1) * 512],
                                                      start=(kb == 0), stop=(kb == KD - 1))
                            mm.then_inc(s["y"], 1)

                    def turn(n):
                        pe.wait_ge(s["h"], n + 1)
                        if n:
                            pe.wait_ge(s["kept"], 2 * n)
                        for b in range(2):
                            for j in range(4):
                                kb = 4 * b + j
                                mm = nc.tensor.transpose(bank[2 + b][:, j * P:(j + 1) * P], h[:, n % 2, kb * P:(kb + 1) * P], k.ident[:])
                            mm.then_inc(s["turned"], 1)
                        if not first:
                            pe.wait_ge(s["kept"], 2 * n + 2)
                            if n:
                                pe.wait_ge(s["exp"], n)
                            for kb in range(KD):
                                mm = nc.tensor.matmul(bank[4][:, 0:NE], hT2[:, kb, :], router[:, kb, :], start=(kb == 0), stop=(kb == KD - 1))
                            mm.then_inc(s["logit"], 1)
                            pe.wait_ge(s["aff"], n + 1)
                            if n:
                                pe.wait_ge(s["aff_kept"], n)
                            nc.tensor.transpose(bank[5][0:NE, 0:P], lg[:, n % 2, :], k.ident[:]).then_inc(s["aff_t"], 1)
                    for n in range(G):
                        product(n)
                        if n:
                            turn(n - 1)
                    turn(G - 1)

                @block.scalar
                def _(act):
                    go = Line(act, s["chain_a"])

                    def exponential(n):
                        act.wait_ge(s["row_stat"], 2 * n + 1)
                        go(nc.scalar.activation(lg[:, n % 2, :], bank[4][:, 0:NE], ACT.Exp, bias=ls[:, n % 2, 0:1], accum_out=ls[:, n % 2, 1:2]), s["exp"])
                    for n in range(G):
                        if first:
                            act.wait_ge(s["y_read"], 2 * (n + 1))
                        else:
                            act.wait_ge(s["lat"], n + 1)
                        norm_stats(nc, go, None, act, None, s["sq"], s["var"], s["sd"], n, x[:, n, :], junk[:], stat[:, n, 0:4], "act")
                        if first:
                            act.wait_ge(s["lat"], n + 1)
                            norm_stats(nc, go, None, act, None, s["sq2"], s["var2"], s["sd2"], n, x[:, n, :], junk[:], stat[:, n, 4:8], "act")
                        elif n:
                            exponential(n - 1)
                    if not first:
                        exponential(G - 1)

                @block.vector
                def _(dve):
                    go = Line(dve, s["chain_v"])

                    def keep(n):
                        for b in range(2):
                            dve.wait_ge(s["turned"], 2 * n + b + 1)
                            src = bank[2 + b][:].rearrange("p (k t) -> p k t", t=P)
                            if first:
                                dst = turn_dst[:, 4 * b:4 * b + 4, bass.ds(g * (G * P) + n * P, P)]
                                go(nc.vector.tensor_tensor(dst, src, gain[:, 4 * b:4 * b + 4].unsqueeze(2).to_broadcast([P, 4, P]), ALU.mult))
                                go(nc.vector.tensor_tensor(dst, dst, shift[:, 4 * b:4 * b + 4].unsqueeze(2).to_broadcast([P, 4, P]), ALU.add), s["kept"])
                            else:
                                go(nc.vector.tensor_copy(hT2[:, 4 * b:4 * b + 4, :], src), s["kept"])

                    def softmax(n):
                        dve.wait_ge(s["logit"], n + 1)
                        go(nc.vector.tensor_reduce(ls[:, n % 2, 2:3], bank[4][:, 0:NE], AX.X, ALU.max))
                        go(nc.vector.tensor_scalar(ls[:, n % 2, 0:1], ls[:, n % 2, 2:3], -1.0, None, ALU.mult), s["row_stat"])
                        dve.wait_ge(s["exp"], n + 1)
                        go(nc.vector.reciprocal(ls[:, n % 2, 3:4], ls[:, n % 2, 1:2]), s["row_stat"])
                        go(nc.vector.tensor_scalar(lg[:, n % 2, :], lg[:, n % 2, :], ls[:, n % 2, 3:4], None, ALU.mult), s["aff"])
                        dve.wait_ge(s["aff_t"], n + 1)
                        go(nc.vector.tensor_copy(turn_dst[:, bass.ds(g * (G * P) + n * P, P)], bank[5][0:NE, 0:P]), s["aff_kept"])
                    for n in range(G):
                        dve.wait_ge(rs[n], 16)
                        for b in range(2):
                            dve.wait_ge(s["y"], 2 * n + b + 1)
                            bs = slice(b * 512, (b + 1) * 512)
                            if first:
                                go(nc.vector.tensor_tensor(x[:, n, bs], x[:, n, bs], bank[b][:], ALU.add), s["y_read"])
                            else:
                                go(nc.vector.tensor_tensor(gated[:, bs], bank[b][:], row_a[:, bs], ALU.mult), s["y_read"])
                        if not first:
                            go(nc.vector.tensor_tensor(x[:, n, :], x[:, n, :], gated[:], ALU.add), s["lat"])
                        norm_stats(nc, None, go, None, dve, s["sq"], s["var"], s["sd"], n, None, None, stat[:, n, 0:4], "dve")
                        if first:
                            go(nc.vector.scalar_tensor_tensor(x[:, n, :], x[:, n, :], stat[:, n, 3:4], row_a[:], ALU.mult, ALU.mult), s["lat"])
                            norm_stats(nc, None, go, None, dve, s["sq2"], s["var2"], s["sd2"], n, None, None, stat[:, n, 4:8], "dve")
                            if n >= 2:
                                dve.wait_ge(s["turned"], 2 * (n - 1))
                            go(nc.vector.tensor_scalar(h[:, n % 2, :], x[:, n, :], stat[:, n, 7:8], None, ALU.mult), s["h"])
                            if n:
                                keep(n - 1)
                        else:
                            if n >= 2:
                                dve.wait_ge(s["turned"], 2 * (n - 1))
                                dve.wait_ge((s["st_h0"], s["st_h1"])[n % 2], 16)
                            go(nc.vector.scalar_tensor_tensor(h[:, n % 2, :], x[:, n, :], stat[:, n, 3:4], row_g[:], ALU.mult, ALU.mult))
                            go(nc.vector.tensor_tensor(h[:, n % 2, :], h[:, n % 2, :], row_s[:], ALU.add), s["h"])
                            if n:
                                keep(n - 1)
                                softmax(n - 1)
                    keep(G - 1)
                    if not first:
                        softmax(G - 1)

            meet(nc, s)


def short_conv(nc, k, hT, w_in, conv_col, zT):
    wv = w_in.rearrange("(kb p) n -> p kb n", p=P)
    with Phase("sc") as ctx:
        s = semaphores(nc, ctx, ["w0", "w1", "w2", "par", "u", "c_kept", "g_kept", "b_kept", "chain_v", "chain_a", "out", "stored"])
        wt = [sb(nc, ctx, f"w_block{i}", [P, KD, P]) for i in range(3)]
        cw = sb(nc, ctx, "conv_cols", [P, 3])
        gv = sb(nc, ctx, "gated", [P, T + 2])
        acc = sb(nc, ctx, "conv", [P, T])
        bank = k.bank
        with nc.Fori(0, KD) as cb:
            with nc.Block() as block:
                @block.sync
                def _(sp):
                    for i, at in enumerate((D, 2 * D, 0)):
                        sp.dma_start(wt[i][:], wv[:, :, bass.ds(cb * P + at, P)]).then_inc((s["w0"], s["w1"], s["w2"])[i], 16)
                    sp.dma_start(cw[:], conv_col[cb]).then_inc(s["par"], 16)
                    sp.wait_ge(s["out"], Q)
                    sp.dma_start(zT[cb], acc[:]).then_inc(s["stored"], 16)
                    sp.wait_ge(s["stored"], 16)

                @block.tensor
                def _(pe):
                    for i in range(3):
                        pe.wait_ge((s["w0"], s["w1"], s["w2"])[i], 16)
                        for q in range(Q):
                            if i == 2:
                                pe.wait_ge(s["c_kept"], q + 1)
                            for kb in range(KD):
                                mm = nc.tensor.matmul(bank[4 * (i % 2) + q][:], wt[i][:, kb, :], hT[:, kb, q * QT:(q + 1) * QT],
                                                      start=(kb == 0), stop=(kb == KD - 1))
                            mm.then_inc(s["u"], 1)

                @block.scalar
                def _(act):
                    go = Line(act, s["chain_a"])
                    for q in range(Q):
                        act.wait_ge(s["u"], q + 1)
                        go(nc.scalar.activation(gv[:, 1 + q * QT:1 + (q + 1) * QT], bank[q][:], ACT.Copy), s["c_kept"])

                @block.vector
                def _(dve):
                    go = Line(dve, s["chain_v"])
                    go(nc.vector.memset(gv[:, 0:1], 0.0))
                    go(nc.vector.memset(gv[:, T + 1:T + 2], 0.0))
                    for q in range(Q):
                        dve.wait_ge(s["c_kept"], q + 1)
                        dve.wait_ge(s["u"], Q + q + 1)
                        qs = slice(1 + q * QT, 1 + (q + 1) * QT)
                        go(nc.vector.tensor_tensor(gv[:, qs], gv[:, qs], bank[4 + q][:], ALU.mult))
                    dve.wait_ge(s["par"], 16)
                    go(nc.vector.tensor_scalar(acc[:], gv[:, 0:T], cw[:, 0:1], None, ALU.mult))
                    go(nc.vector.scalar_tensor_tensor(acc[:], gv[:, 1:T + 1], cw[:, 1:2], acc[:], ALU.mult, ALU.add))
                    go(nc.vector.scalar_tensor_tensor(acc[:], gv[:, 2:T + 2], cw[:, 2:3], acc[:], ALU.mult, ALU.add))
                    for q in range(Q):
                        dve.wait_ge(s["u"], 2 * Q + q + 1)
                        qs = slice(q * QT, (q + 1) * QT)
                        go(nc.vector.tensor_tensor(acc[:, qs], acc[:, qs], bank[q][:], ALU.mult), s["out"])
            meet(nc, s)


def choose(nc, k, aff, idx_all, gate_all):
    with Phase("ch") as ctx:
        s = semaphores(nc, ctx, ["chain_v", "picked", "turned"])
        vals = sb(nc, ctx, "top", [NE, CAP])
        idx = sb(nc, ctx, "top_idx", [NE, CAP], U32)
        idf = sb(nc, ctx, "top_idx_f", [NE, CAP])
        bank = k.bank
        with nc.Block() as block:
            @block.vector
            def _(dve):
                go = Line(dve, s["chain_v"])
                for i in range(CAP // 8):
                    e = slice(8 * i, 8 * i + 8)
                    go(nc.vector.max(vals[:, e], aff[:]))
                    go(nc.vector.max_index(idx[:, e], vals[:, e], aff[:]))
                    if i < CAP // 8 - 1:
                        go(nc.vector.match_replace(aff[:], vals[:, e], aff[:], -1.0))
                go(nc.vector.tensor_copy(idf[:], idx[:]), s["picked"])
                dve.wait_ge(s["turned"], 1)
                go(nc.vector.tensor_copy(idx_all[:], bank[0][:, 0:2 * NE]))
                go(nc.vector.tensor_copy(gate_all[:], bank[0][:, 2 * NE:4 * NE]))

            @block.tensor
            def _(pe):
                pe.wait_ge(s["picked"], 1)
                for n, src in enumerate((idf, vals)):
                    for h in range(2):
                        o = (2 * n + h) * NE
                        mm = nc.tensor.transpose(bank[0][:, o:o + NE], src[:, h * P:(h + 1) * P], k.ident[0:NE, 0:NE])
                mm.then_inc(s["turned"], 1)
        meet(nc, s)


def experts(nc, k, wg, wu, wd, idx_all, gate_all, out):
    gv = wg.rearrange("o e (kb p) f -> (o e) p kb f", p=P)
    uv = wu.rearrange("o e (kb p) f -> (o e) p kb f", p=P)
    dv = wd.rearrange("o e (kb p) d -> (o e) p kb d", p=P)
    with Phase("ex") as ctx:
        s = semaphores(nc, ctx, ["row", "gu0", "gu1", "gu2", "gu3", "gu4", "gu5", "gu6", "gu7", "d0", "d1", "d2", "d3",
                                 "turned", "x_kept", "gu", "silu", "hid", "y", "ys", "idx", "chain_v", "chain_a"])
        gathered = [ctx.enter_context(nc.semaphore(f"gathered{h}")) for h in range(2)]
        sent = [ctx.enter_context(nc.semaphore(f"sent{h}")) for h in range(2)]
        wgu = sb(nc, ctx, "w_gate_up", [P, 2, 4, KD, 256])
        wdn = sb(nc, ctx, "w_down", [P, 4, 2, D])
        xg = sb(nc, ctx, "x_gathered", [P, 2, D])
        xT = sb(nc, ctx, "x_turned", [P, KD, CAP])
        sl = sb(nc, ctx, "silu", [P, 2, CAP])
        hid = sb(nc, ctx, "hidden", [P, KD, CAP])
        ys = sb(nc, ctx, "y", [P, 2, D])
        g2 = sb(nc, ctx, "g2_row", [P, D])
        idx = sb(nc, ctx, "idx", [P, 2, 2], U32)
        gates = sb(nc, ctx, "gates", [P, 2])
        bank = k.bank
        gu = (s["gu0"], s["gu1"], s["gu2"], s["gu3"], s["gu4"], s["gu5"], s["gu6"], s["gu7"])
        ds = (s["d0"], s["d1"], s["d2"], s["d3"])
        idv = idx_all[:].rearrange("p (h e) -> p h e", h=2)
        gav = gate_all[:].rearrange("p (h e) -> p h e", h=2)

        def load_gate_up(sp, e, quarter, half):
            src = (gv, uv)[half]
            sp.dma_start(wgu[:, half, quarter, :, :], src[e, :, :, quarter * 256:(quarter + 1) * 256]).then_inc(gu[2 * quarter + half], 16)

        with nc.Block() as block:
            @block.sync
            def _(sp):
                for quarter in range(4):
                    for half in range(2):
                        load_gate_up(sp, 0, quarter, half)
                sp.dma_start(g2[:], k.rows_dram[3:4, :].to_broadcast([P, D])).then_inc(s["row"], 16)
                for n in gu:
                    sp.wait_ge(n, 16)
                sp.wait_ge(s["row"], 16)

            @block.vector
            def _(dve):
                nc.vector.tensor_copy(idx[:, :, 0], idv[:, :, 0]).then_inc(s["idx"], 1)

            @block.gpsimd
            def _(pool):
                pool.wait_ge(s["idx"], 1)
                for h in range(2):
                    pool.indirect_dma_start(out=xg[:, h, :], out_offset=None, in_=k.h2,
                                            in_offset=bass.IndirectOffsetOnAxis(ap=idx[:, h, 0:1], axis=0)).then_inc(gathered[h], 16)
                for h in range(2):
                    pool.wait_ge(gathered[h], 16)
        meet(nc, s)

        def turn(e, last):
            with nc.Block() as block:
                @block.sync
                def _(sp):
                    for n in range(4):
                        sp.dma_start(wdn[:, n, :, :], dv[e, :, 2 * n:2 * n + 2, :]).then_inc(ds[n], 16)
                    if not last:
                        for quarter in range(4):
                            sp.wait_ge(s["gu"], 4 * (quarter + 1))
                            for half in range(2):
                                load_gate_up(sp, e + 1, quarter, half)
                        for n in gu:
                            sp.wait_ge(n, 16)

                @block.gpsimd
                def _(pool):
                    pool.wait_ge(s["idx"], 1)
                    if not last:
                        pool.wait_ge(s["turned"], 4)
                        for h in range(2):
                            pool.indirect_dma_start(out=xg[:, h, :], out_offset=None, in_=k.h2,
                                                    in_offset=bass.IndirectOffsetOnAxis(ap=idx[:, h, 1:2], axis=0)).then_inc(gathered[h], 16)
                    for h in range(2):
                        pool.wait_ge(s["ys"], 2 * (h + 1))
                        pool.indirect_dma_start(out=out, out_offset=bass.IndirectOffsetOnAxis(ap=idx[:, h, 0:1], axis=0),
                                                in_=ys[:, h, :], in_offset=None, compute_op=ALU.add).then_inc(sent[h], 16)
                    for h in range(2):
                        pool.wait_ge(sent[h], e * 16 + 16)
                    if not last:
                        for h in range(2):
                            pool.wait_ge(gathered[h], e * 16 + 32)

                @block.tensor
                def _(pe):
                    for h in range(2):
                        for b in range(2):
                            for j in range(4):
                                kb = 4 * b + j
                                mm = nc.tensor.transpose(bank[4 + 2 * h + b][:, j * P:(j + 1) * P], xg[:, h, kb * P:(kb + 1) * P], k.ident[:])
                            mm.then_inc(s["turned"], 1)
                    pe.wait_ge(s["x_kept"], 4)
                    for f in range(KD):
                        if f >= 2:
                            pe.wait_ge(s["hid"], f - 1)
                        for half in range(2):
                            b = bank[2 * (f % 2) + half]
                            for kb in range(KD):
                                mm = nc.tensor.matmul(b[:, 0:CAP], wgu[:, half, f // 2, kb, (f % 2) * P:(f % 2 + 1) * P], xT[:, kb, :],
                                                      start=(kb == 0), stop=(kb == KD - 1))
                            mm.then_inc(s["gu"], 1)
                    for n in range(4):
                        pe.wait_ge(ds[n], 16)
                    pe.wait_ge(s["hid"], KD)
                    for h in range(2):
                        for b in range(2):
                            for f in range(KD):
                                mm = nc.tensor.matmul(bank[4 + 2 * h + b][:], hid[:, f, h * P:(h + 1) * P],
                                                      wdn[:, f // 2, f % 2, b * 512:(b + 1) * 512], start=(f == 0), stop=(f == KD - 1))
                            mm.then_inc(s["y"], 1)

                @block.scalar
                def _(act):
                    go = Line(act, s["chain_a"])
                    for f in range(KD):
                        act.wait_ge(s["gu"], 2 * f + 1)
                        if f >= 2:
                            act.wait_ge(s["hid"], f - 1)
                        go(nc.scalar.activation(sl[:, f % 2, :], bank[2 * (f % 2)][:, 0:CAP], ACT.Silu), s["silu"])

                @block.vector
                def _(dve):
                    go = Line(dve, s["chain_v"])
                    go(nc.vector.tensor_copy(gates[:], gav[:, :, bass.ds(e, 1)].rearrange("p h e -> p (h e)")))
                    if last:
                        go(nc.vector.tensor_copy(idx[:, :, 0:1], idv[:, :, bass.ds(e, 1)]), s["idx"])
                    else:
                        go(nc.vector.tensor_copy(idx[:], idv[:, :, bass.ds(e, 2)]), s["idx"])
                    for h in range(2):
                        for b in range(2):
                            dve.wait_ge(s["turned"], 2 * h + b + 1)
                            go(nc.vector.tensor_copy(xT[:, 4 * b:4 * b + 4, h * P:(h + 1) * P],
                                                     bank[4 + 2 * h + b][:].rearrange("p (k t) -> p k t", t=P)), s["x_kept"])
                    for f in range(KD):
                        dve.wait_ge(s["gu"], 2 * f + 2)
                        dve.wait_ge(s["silu"], f + 1)
                        go(nc.vector.tensor_tensor(hid[:, f, :], sl[:, f % 2, :], bank[2 * (f % 2) + 1][:, 0:CAP], ALU.mult), s["hid"])
                    for h in range(2):
                        for b in range(2):
                            dve.wait_ge(s["y"], 2 * h + b + 1)
                            bs = slice(b * 512, (b + 1) * 512)
                            go(nc.vector.scalar_tensor_tensor(ys[:, h, bs], bank[4 + 2 * h + b][:], gates[:, h:h + 1], g2[:, bs], ALU.mult, ALU.mult), s["ys"])
            meet(nc, s)

        with nc.Fori(0, NE - 1) as e:
            turn(e, False)
        turn(NE - 1, True)


MASKS = ("ident", "head_ones", "heads", "scores", "corner", "corner_t", "levels", "inclusive")


def mask_constants():
    i = np.arange(P)
    s, t = i[:, None], i[None, :]
    same = (s // C) == (t // C)
    strict, incl = (s < t) & same, (s <= t) & same
    heads = (s // 64) == (t // 64)

    def merge(b):
        return (s // (2 * b) == t // (2 * b)) & (s // b % 2 == 0) & (t // b % 2 == 1)

    parts = {
        "ident": s == t, "head_ones": heads, "heads": heads,
        "scores": np.concatenate([strict, incl, strict, incl], 1),
        "corner": -(merge(1).T.astype(np.float32)), "corner_t": -(merge(1).astype(np.float32)),
        "levels": np.concatenate([-(merge(2 << l).astype(np.float32)) for l in range(LEVELS)], 1),
        "inclusive": incl,
    }
    place, at, cols = {}, 0, []
    for name in MASKS:
        a = parts[name].astype(np.float32)
        place[name] = (at, a.shape[1])
        at += a.shape[1]
        cols.append(a)
    return np.ascontiguousarray(np.concatenate(cols, 1)), place, at


def hybrid_conv_moe(nc, x, norm_w_col, w_in, gate_up, gate_bias_col, gla_norm_col, mu_lora_col, w_up, a_up,
                    rwkv_cols, w_out, final_norm, c_col, ada_w, ada_b, ada_b_col, norm_g, norm_g_col,
                    sc_w_in, sc_conv_col, sc_w_out, router, wg, wu, wd, masks, out):
    _, place, width = mask_constants()
    k = Shared()
    k.router = router
    k.rows_dram = nc.dram_tensor("mod_rows_dram", [4, D], F32).ap()
    k.h2 = nc.dram_tensor("h2_dram", [T, D], F32).ap()
    lat = nc.dram_tensor("lat_dram", [T, D], F32).ap()
    mT = nc.dram_tensor("merged_dram", [KD, P, T], F32).ap()
    zT = nc.dram_tensor("z_dram", [KD, P, T], F32).ap()
    k.mask_in = masks
    k.bank = [nc.alloc_psum_tensor(f"bank{i}", [P, 512], F32) for i in range(8)]
    with Phase("mixers") as top:
        k.mask_sb = sb(nc, top, "masks", [P, width])
        k.mask = lambda name: k.mask_sb[:, place[name][0]:place[name][0] + place[name][1]]
        k.ident = k.mask_sb[:, 0:P]
        k.ones = sb(nc, top, "ones", [P, C])
        k.chunk_ones = k.ones
        k.shift1 = sb(nc, top, "shift1", [P, KD])
        k.gain1 = sb(nc, top, "gain1", [P, KD])
        modulation(nc, k, c_col, ada_w[0], ada_b, ada_b_col, norm_g[0], norm_g_col)
        hT = sb(nc, top, "hT", [P, KD, T])
        first_norm(nc, k, x, hT, norm_w_col)
        rwkv(nc, k, hT, w_in[0], w_up[0], a_up[0], rwkv_cols, mu_lora_col, mT)
        gla(nc, k, hT, w_in[0], gate_up[0], gate_bias_col, gla_norm_col, mT)
        out_product(nc, k, mT, w_out[0], x[0], None, final_norm, None, lat, hT, k.gain1, k.shift1, True)
        short_conv(nc, k, hT, sc_w_in[0], sc_conv_col, zT)
    with Phase("moe") as top:
        mask2 = sb(nc, top, "ident2", [P, P])
        aff = sb(nc, top, "affinity", [NE, T])
        idx_all = sb(nc, top, "idx_all", [P, 2 * NE], U32)
        gate_all = sb(nc, top, "gate_all", [P, 2 * NE])
        k.ident = mask2
        s = semaphores(nc, top, ["load"])
        with nc.Block() as block:
            @block.sync
            def _(sp):
                sp.dma_start(mask2[:], masks[:, 0:P]).then_inc(s["load"], 16)
                sp.wait_ge(s["load"], 16)
        meet(nc, s)
        rows = k.rows_dram
        out_product(nc, k, zT, sc_w_out[0], lat, rows[0:1, :], rows[2:3, :], rows[1:2, :], out[0], aff, None, None, None)
        choose(nc, k, aff, idx_all, gate_all)
        experts(nc, k, wg, wu, wd, idx_all, gate_all, out[0])


def lay_out(inputs):
    f = lambda name: np.ascontiguousarray(inputs[name])
    col = lambda v, n: np.ascontiguousarray(v.reshape(n, P).T)
    mu = f("rwkv_mu")[0]
    hp = lambda v: v.reshape(4, P)
    zero = np.zeros((4, P), np.float32)
    params = [hp(mu[0:512]), hp(mu[512:1024]), hp(mu[1024:1536]), hp(f("rwkv_w0")[0]), hp(f("rwkv_a0")[0]),
              hp(f("rwkv_k_k")[0]), hp(f("rwkv_k_a")[0]), hp(f("rwkv_r_k")[0].reshape(-1)),
              hp(f("rwkv_ln_w")[0]), hp(f("rwkv_ln_b")[0]), zero, zero]
    ada_b = f("ada_b_2")
    return {
        "x": f("x"), "norm_w_col": col(f("norm_w")[0], KD), "w_in": f("w_in"), "gate_up": f("gla_gate_up"),
        "gate_bias_col": np.ascontiguousarray(f("gla_gate_bias")[0].reshape(2, P, 1)),
        "gla_norm_col": np.ascontiguousarray(f("gla_norm_w")[0].reshape(P, 1)),
        "mu_lora_col": np.ascontiguousarray(mu[1536:1664].reshape(P, 1)), "w_up": f("rwkv_w_up"), "a_up": f("rwkv_a_up"),
        "rwkv_cols": np.ascontiguousarray(np.stack(params, -1)), "w_out": f("w_out"),
        "final_norm": np.ascontiguousarray(f("final_norm_w").reshape(1, D)), "c_col": col(f("c_2")[0], KD),
        "ada_w": f("ada_w_2"), "ada_b": ada_b, "ada_b_col": col(ada_b[0, 0:2 * D], 2 * KD), "norm_g": f("norm_g_2"),
        "norm_g_col": col(f("norm_g_2")[0, 0], KD), "sc_w_in": f("sc_w_in_2"),
        "sc_conv_col": np.ascontiguousarray(f("sc_conv_2")[0].reshape(3, KD, P).transpose(1, 2, 0)),
        "sc_w_out": f("sc_w_out_2"), "router": np.ascontiguousarray(f("moe_router_2")[0]),
        "wg": f("moe_w_gate_2"), "wu": f("moe_w_up_2"), "wd": f("moe_w_down_2"), "masks": mask_constants()[0],
    }


def kernel(**inputs):
    import concourse.bacc as bacc
    from concourse.bass_utils import run_bass_kernel_spmd

    nc = bacc.Bacc("TRN2", target_bir_lowering=False, num_devices=1)
    arrays, args = {}, []
    for name, a in lay_out(inputs).items():
        arrays[f"in_{name}"] = a
        args.append(nc.dram_tensor(f"in_{name}", a.shape, mybir.dt.from_np(a.dtype), kind="ExternalInput").ap())
    args.append(nc.dram_tensor("out_0", (1, T, D), F32, kind="ExternalOutput").ap())
    hybrid_conv_moe(nc, *args)
    r = run_bass_kernel_spmd(nc, [arrays], core_ids=[0])
    return r.results[0]["out_0"]
```

```python
from contextlib import ExitStack

import numpy as np

import concourse.bass as bass
from concourse import mybir

F32 = mybir.dt.float32
U32 = mybir.dt.uint32
ALU = mybir.AluOpType
ACT = mybir.ActivationFunctionType
AX = mybir.AxisListType

P = 128
T = 2048
D = 1024
KD = D // P
TT = T // P
Q = 4
QT = T // Q
EPS = 1e-6
C = 64
NCH = T // C
GLA_Q, GLA_K, GLA_V, GLA_LR, GLA_G = 0, 256, 512, 1024, 1040
RWKV0 = 1552
RW_R, RW_K, RW_V, RW_L, RW_G = RWKV0, RWKV0 + 512, RWKV0 + 1024, RWKV0 + 1536, RWKV0 + 1664
RANK = 16
DECAY = float(np.exp(-0.5))
NE, CAP = 16, 256
LEVELS = 5


class Shared:
    pass


class Line:

    def __init__(self, engine, chain):
        self.engine, self.chain, self.n = engine, chain, {}

    def __call__(self, instruction, signal=None):
        s = signal if signal is not None else self.chain
        self.n[s.num] = self.n.get(s.num, 0) + 1
        instruction.then_inc(s, 1)
        self.engine.wait_ge(s, self.n[s.num])


def semaphores(nc, ctx, names):
    return {name: ctx.enter_context(nc.semaphore(f"{ctx.name}_{name}")) for name in names}


def meet(nc, s):
    numbers = [x.num for x in s.values()]
    nc.all_engine_barrier(sems_to_clear=range(min(numbers), max(numbers) + 1))


class Phase(ExitStack):

    def __init__(self, name):
        super().__init__()
        self.name = name


def sb(nc, ctx, name, shape, dt=F32):
    return ctx.enter_context(nc.sbuf_tensor(f"{ctx.name}_{name}", shape, dt))


def modulation(nc, k, c_col, ada_w, ada_b, ada_b_col, norm_g, norm_g_col):
    with Phase("mod") as ctx:
        s = semaphores(nc, ctx, ["small", "w0", "w1", "chain_v", "chain_a", "silu", "used", "summed", "psum", "rows", "stored"])
        w = sb(nc, ctx, "ada_tile", [P, 2, 6 * D])
        acc = sb(nc, ctx, "ada_acc", [P, 6 * D])
        cc = sb(nc, ctx, "c_cols", [P, KD])
        b_col = sb(nc, ctx, "ada_b_cols", [P, 2 * KD])
        g_col = sb(nc, ctx, "norm_g_cols", [P, KD])
        rows = sb(nc, ctx, "mod_rows", [1, 4 * D])
        b_row = sb(nc, ctx, "ada_b_row", [1, 4 * D])
        g_row = sb(nc, ctx, "norm_g_row", [1, D])
        bank = k.bank
        with nc.Block() as block:
            @block.sync
            def _(sp):
                sp.dma_start(cc[:], c_col).then_inc(s["small"], 16)
                sp.dma_start(b_col[:], ada_b_col).then_inc(s["small"], 16)
                sp.dma_start(g_col[:], norm_g_col).then_inc(s["small"], 16)
                sp.dma_start(b_row[:], ada_b[:, 2 * D:]).then_inc(s["small"], 16)
                sp.dma_start(g_row[:], norm_g[1:2, :]).then_inc(s["small"], 16)
                sp.dma_start(k.mask_sb[:], k.mask_in).then_inc(s["small"], 16)
                for kb in range(KD):
                    if kb >= 2:
                        sp.wait_ge(s["used"], kb - 1)
                    sp.dma_start(w[:, kb % 2, :], ada_w[kb * P:(kb + 1) * P, :]).then_inc((s["w0"], s["w1"])[kb % 2], 16)
                sp.wait_ge(s["rows"], 6)
                sp.dma_start(k.rows_dram.rearrange("(a r) d -> a (r d)", a=1), rows[:]).then_inc(s["stored"], 16)
                sp.wait_ge(s["stored"], 16)

            @block.scalar
            def _(act):
                act.wait_ge(s["small"], 96)
                nc.scalar.activation(cc[:], cc[:], ACT.Silu).then_inc(s["silu"], 1)

            @block.vector
            def _(dve):
                go = Line(dve, s["chain_v"])
                go(nc.vector.memset(k.ones[:], 1.0))
                dve.wait_ge(s["silu"], 1)
                for kb in range(KD):
                    dve.wait_ge((s["w0"], s["w1"])[kb % 2], 16 * (kb // 2 + 1))
                    if kb == 0:
                        go(nc.vector.tensor_scalar(acc[:], w[:, 0, :], cc[:, 0:1], None, ALU.mult), s["used"])
                    else:
                        go(nc.vector.scalar_tensor_tensor(acc[:], w[:, kb % 2, :], cc[:, kb:kb + 1], acc[:],
                                                          ALU.mult, ALU.add), s["used"])
                dve.wait_ge(s["psum"], 1)
                go(nc.vector.tensor_tensor(k.shift1[:], bank[7][:, 0:KD], b_col[:, 0:KD], ALU.add))
                go(nc.vector.tensor_tensor(k.gain1[:], bank[7][:, KD:2 * KD], b_col[:, KD:2 * KD], ALU.add))
                go(nc.vector.tensor_scalar_add(k.gain1[:], k.gain1[:], 1.0))
                go(nc.vector.tensor_tensor(k.gain1[:], k.gain1[:], g_col[:], ALU.mult))
                dve.wait_ge(s["psum"], 2)
                for n in range(4):
                    for h in range(2):
                        at = n * D + h * 512
                        b = bank[(2 * n + h) % 4]
                        if n >= 2:
                            dve.wait_ge(s["psum"], 3)
                        ins = nc.vector.tensor_tensor(rows[0:1, at:at + 512], b[0:1, :], b_row[0:1, at:at + 512], ALU.add)
                        if h:
                            go(ins, s["rows"])
                        else:
                            go(ins)
                go(nc.vector.tensor_scalar_add(rows[0:1, 2 * D:3 * D], rows[0:1, 2 * D:3 * D], 1.0), s["rows"])
                go(nc.vector.tensor_tensor(rows[0:1, 2 * D:3 * D], rows[0:1, 2 * D:3 * D], g_row[:], ALU.mult), s["rows"])

            @block.tensor
            def _(pe):
                pe.wait_ge(s["used"], KD)
                for j in range(2 * KD):
                    mm = nc.tensor.matmul(bank[7][:, j:j + 1], acc[:, j * P:(j + 1) * P], k.ones[:, 0:1],
                                          start=True, stop=True)
                mm.then_inc(s["psum"], 1)
                for n in range(8):
                    if n == 4:
                        pe.wait_ge(s["rows"], 2)
                    at = 2 * D + n * 512
                    mm = nc.tensor.matmul(bank[n % 4][0:1, :], k.ones[:, 0:1], acc[:, at:at + 512], start=True, stop=True)
                    if n % 4 == 3:
                        mm.then_inc(s["psum"], 1)
        meet(nc, s)


def norm_stats(nc, go_a, go_v, act, dve, s_sq, s_var, s_sd, n, x, junk, stat, role):
    if role == "act":
        go_a(nc.scalar.activation(junk, x, ACT.Square, accum_out=stat[:, 0:1]), s_sq)
        act.wait_ge(s_var, n + 1)
        go_a(nc.scalar.activation(stat[:, 2:3], stat[:, 1:2], ACT.Sqrt), s_sd)
    else:
        dve.wait_ge(s_sq, n + 1)
        go_v(nc.vector.tensor_scalar(stat[:, 1:2], stat[:, 0:1], 1.0 / D, EPS, ALU.mult, ALU.add), s_var)
        dve.wait_ge(s_sd, n + 1)
        go_v(nc.vector.reciprocal(stat[:, 3:4], stat[:, 2:3]))


def first_norm(nc, k, x, hT, norm_w_col):
    G = 4
    xv = x.rearrange("b (g n p) d -> (b g) p n d", n=G, p=P)
    with Phase("nrm") as ctx:
        s = semaphores(nc, ctx, ["x0", "x1", "x2", "x3", "w", "chain_v", "chain_a", "sq", "var", "sd", "scaled", "turned", "kept"])
        xt = sb(nc, ctx, "x_tile", [P, G, D])
        junk = sb(nc, ctx, "square", [P, D])
        stat = sb(nc, ctx, "stat", [P, G, 4])
        wc = sb(nc, ctx, "norm_cols", [P, KD])
        bank = k.bank
        with nc.Fori(0, TT // G) as g:
            with nc.Block() as block:
                @block.sync
                def _(sp):
                    sp.dma_start(wc[:], norm_w_col).then_inc(s["w"], 16)
                    for n in range(G):
                        sp.dma_start(xt[:, n, :], xv[g, :, n, :]).then_inc((s["x0"], s["x1"], s["x2"], s["x3"])[n], 16)

                @block.scalar
                def _(act):
                    go = Line(act, s["chain_a"])
                    for n in range(G):
                        act.wait_ge((s["x0"], s["x1"], s["x2"], s["x3"])[n], 16)
                        norm_stats(nc, go, None, act, None, s["sq"], s["var"], s["sd"], n, xt[:, n, :], junk[:], stat[:, n, :], "act")

                @block.vector
                def _(dve):
                    go = Line(dve, s["chain_v"])
                    dve.wait_ge(s["w"], 16)

                    def keep(n):
                        for b in range(2):
                            dve.wait_ge(s["turned"], 2 * n + b + 1)
                            go(nc.vector.tensor_tensor(
                                hT[:, 4 * b:4 * b + 4, bass.ds(g * (G * P) + n * P, P)],
                                bank[2 * (n % 2) + b][:].rearrange("p (k t) -> p k t", t=P),
                                wc[:, 4 * b:4 * b + 4].unsqueeze(2).to_broadcast([P, 4, P]), ALU.mult), s["kept"])
                    for n in range(G):
                        norm_stats(nc, None, go, None, dve, s["sq"], s["var"], s["sd"], n, None, None, stat[:, n, :], "dve")
                        go(nc.vector.tensor_scalar(xt[:, n, :], xt[:, n, :], stat[:, n, 3:4], None, ALU.mult), s["scaled"])
                        if n:
                            keep(n - 1)
                    keep(G - 1)

                @block.tensor
                def _(pe):
                    for n in range(G):
                        pe.wait_ge(s["scaled"], n + 1)
                        if n >= 2:
                            pe.wait_ge(s["kept"], 2 * (n - 1))
                        for b in range(2):
                            for j in range(4):
                                kb = 4 * b + j
                                mm = nc.tensor.transpose(bank[2 * (n % 2) + b][:, j * P:(j + 1) * P],
                                                         xt[:, n, kb * P:(kb + 1) * P], k.ident[:])
                            mm.then_inc(s["turned"], 1)
            meet(nc, s)


def rwkv(nc, k, hT, w_in, w_up, a_up, cols, mu_lora_col, mT):
    HP = 4
    wv = w_in.rearrange("(kb p) n -> p kb n", p=P)
    with Phase("heads") as outer:
        lora = sb(nc, outer, "lora", [P, T])
        with Phase("lr") as ctx:
            s = semaphores(nc, ctx, ["w", "mu", "u", "chain_v", "chain_a", "raw", "mixed"])
            w = sb(nc, ctx, "lora_w", [P, KD, P])
            raw = sb(nc, ctx, "lora_raw", [P, T + 1])
            mu = sb(nc, ctx, "lora_mu", [P, 1])
            diff = sb(nc, ctx, "lora_diff", [P, T])
            bank = k.bank
            with nc.Block() as block:
                @block.sync
                def _(sp):
                    sp.dma_start(w[:], wv[:, :, RW_L:RW_L + P]).then_inc(s["w"], 16)
                    sp.dma_start(mu[:], mu_lora_col).then_inc(s["mu"], 16)

                @block.tensor
                def _(pe):
                    pe.wait_ge(s["w"], 16)
                    for q in range(Q):
                        for kb in range(KD):
                            mm = nc.tensor.matmul(bank[q][:], w[:, kb, :], hT[:, kb, q * QT:(q + 1) * QT],
                                                  start=(kb == 0), stop=(kb == KD - 1))
                        mm.then_inc(s["u"], 1)

                @block.scalar
                def _(act):
                    go = Line(act, s["chain_a"])
                    for q in range(Q):
                        act.wait_ge(s["u"], q + 1)
                        go(nc.scalar.activation(raw[:, 1 + q * QT:1 + (q + 1) * QT], bank[q][:], ACT.Copy), s["raw"])
                    act.wait_ge(s["mixed"], 1)
                    go(nc.scalar.activation(lora[0:64, :], lora[0:64, :], ACT.Tanh))

                @block.vector
                def _(dve):
                    go = Line(dve, s["chain_v"])
                    go(nc.vector.memset(raw[:, 0:1], 0.0))
                    dve.wait_ge(s["raw"], Q)
                    dve.wait_ge(s["mu"], 16)
                    go(nc.vector.tensor_tensor(diff[:], raw[:, 0:T], raw[:, 1:T + 1], ALU.subtract))
                    go(nc.vector.scalar_tensor_tensor(lora[:], diff[:], mu[:, 0:1], raw[:, 1:T + 1], ALU.mult, ALU.add), s["mixed"])
            meet(nc, s)

        with Phase("rw") as ctx:
            s = semaphores(nc, ctx, [
                "w0", "w1", "w2", "w3", "par", "lup", "u", "wa", "ssq", "bon", "chain_v", "chain_a", "chain_g",
                "raw", "raw_read", "gate", "sig", "cum", "exps", "inv", "kk", "kk_sq", "sqrt", "forms", "rk",
                "tr", "tr_kept", "sc", "sc_kept", "nt", "a", "t", "e", "e_kept", "dt", "x", "x_kept", "wu", "wu_kept",
                "q", "q_kept", "gh", "gh_kept", "state_mm", "state", "y", "y_kept", "yvar", "ysd", "ynorm",
                "yt", "out", "stored"])
            wt = [sb(nc, ctx, f"w_block{i}", [P, KD, P]) for i in range(2)]
            lup = sb(nc, ctx, "lora_up", [P, P])
            par = sb(nc, ctx, "head_params", [P, 12])
            raws = [sb(nc, ctx, f"raw{i}", [P, T + 1]) for i in range(2)]
            KT, BB = raws[0][:, 0:T], raws[1][:, 0:T]
            r, kx, v, sg, sw, a, cs = [sb(nc, ctx, n, [P, T]) for n in ("r", "kx", "v", "sg", "sw", "a", "cs")]
            PR = sb(nc, ctx, "PR", [P, TT, 2, P])
            Pc, Rc = PR[:, :, 0, :], PR[:, :, 1, :]
            tmp = sb(nc, ctx, "tmp", [P, T])
            Y = tmp[:].rearrange("p (j n) -> p j n", n=P)
            lc = sb(nc, ctx, "chunk_decay", [P, NCH])
            scm = [x[:].rearrange("p (q n t) -> p q n t", q=4, n=4) for x in (a, cs)]
            tt = [kx[:, i * 1024:(i + 1) * 1024].rearrange("p (q n t) -> p q n t", q=4, n=2) for i in range(2)]
            ptm = [r[:, i * 768:(i + 1) * 768].rearrange("p (j n t) -> p j n t", j=2, n=3) for i in range(2)]
            eb = r[:, 1536:2048].rearrange("p (q t) -> p q t", q=4)
            px = sb(nc, ctx, "PX", [P, 2, 4, P])
            wun = sb(nc, ctx, "WU", [P, 2, 2, P])
            qp = sb(nc, ctx, "Qp", [P, 2, P])
            gt = sb(nc, ctx, "GT", [P, 2, 2, P])
            hh = sb(nc, ctx, "H", [P, 2, 2, P])
            nt = sb(nc, ctx, "levels", [P, 2, 4, P])
            M = sb(nc, ctx, "state", [P, P])
            gst = sb(nc, ctx, "group_stat", [P, 3, 2 * TT])
            bank = k.bank
            mk = k.mask
            NB = TT // 2
            c3 = lambda ap: ap.rearrange("p (n c) -> p n c", c=P)
            heads2 = [slice(0, 64), slice(64, 128)]
            with nc.Fori(0, HP) as hp:
                with nc.Block() as block:
                    firsts = (RW_K, RW_R, RW_V, RW_G)

                    @block.sync
                    def _(sp):
                        sp.dma_start(lup[0:64, :], w_up[:, bass.ds(hp * P, P)]).then_inc(s["lup"], 16)
                        sp.dma_start(lup[64:128, :], a_up[:, bass.ds(hp * P, P)]).then_inc(s["lup"], 16)
                        for i, at in enumerate(firsts):
                            if i == 1:
                                sp.dma_start(par[:], cols[hp]).then_inc(s["par"], 16)
                            if i >= 2:
                                sp.wait_ge(s["u"], Q * (i - 1))
                            sp.dma_start(wt[i % 2][:], wv[:, :, bass.ds(hp * P + at, P)]).then_inc(s[f"w{i}"], 16)
                        sp.wait_ge(s["out"], 1)
                        sp.dma_start(mT[hp + 4], tmp[:]).then_inc(s["stored"], 16)
                        sp.wait_ge(s["stored"], 16)

                    @block.tensor
                    def _(pe):
                        pe.wait_ge(s["lup"], 32)
                        for i in range(2):
                            for q in range(Q):
                                nc.tensor.matmul(bank[4 * i + q][:], lup[64 * i:64 * i + 64, :],
                                                 lora[64 * i:64 * i + 64, q * QT:(q + 1) * QT], start=True, stop=True).then_inc(s["wa"], 1)

                        def block_of_u(i, first_bank, freed, count):
                            pe.wait_ge(s[f"w{i}"], 16)
                            for q in range(Q):
                                pe.wait_ge(s[freed], count + q + 1)
                                for kb in range(KD):
                                    mm = nc.tensor.matmul(bank[first_bank + q][:], wt[i % 2][:, kb, :],
                                                          hT[:, kb, q * QT:(q + 1) * QT], start=(kb == 0), stop=(kb == KD - 1))
                                mm.then_inc(s["u"], 1)
                        block_of_u(0, 0, "sig", 0)
                        block_of_u(1, 4, "sig", Q)
                        pe.wait_ge(s["kk_sq"], 1)
                        for q in range(Q):
                            nc.tensor.matmul(bank[q][:], k.mask("head_ones"), v[:, q * QT:(q + 1) * QT], start=True, stop=True).then_inc(s["ssq"], 1)
                        block_of_u(2, 0, "sqrt", 0)
                        block_of_u(3, 4, "raw", Q)
                        pe.wait_ge(s["rk"], 1)
                        pe.wait_ge(s["raw"], 3 * Q)
                        for q in range(Q):
                            nc.tensor.matmul(bank[q][:], k.mask("head_ones"), tmp[:, q * QT:(q + 1) * QT], start=True, stop=True).then_inc(s["bon"], 1)
                        pe.wait_ge(s["forms"], 1)
                        pe.wait_ge(s["gate"], Q)

                        def turn(j):
                            for n, src in enumerate((Pc[:, j, :], BB[:, j * P:(j + 1) * P], KT[:, j * P:(j + 1) * P], v[:, j * P:(j + 1) * P])):
                                mm = nc.tensor.transpose(bank[0][:, n * P:(n + 1) * P], src, k.ident[:])
                            mm.then_inc(s["tr"], 1)

                        def scores(j):
                            ts = slice(j * P, (j + 1) * P)
                            for h, hs in enumerate(heads2):
                                q = 2 * j + h
                                if q >= 2:
                                    pe.wait_ge(s["sc_kept"], q - 1)
                                rhs = PR[hs, j, :, :].rearrange("p a t -> p (a t)")
                                nc.tensor.matmul(bank[1 + h][:, 0:256], BB[hs, ts], rhs, start=True, stop=True)
                                nc.tensor.matmul(bank[1 + h][:, 256:512], KT[hs, ts], rhs, start=True, stop=True).then_inc(s["sc"], 1)
                            for h, hs in enumerate(heads2):
                                o = (j % 2) * P
                                mm = nc.tensor.matmul(bank[6 + h][:, o:o + P], Pc[hs, j, :], BB[hs, ts], start=True, stop=True)
                            if j % 2:
                                mm.then_inc(s["a"], 1)

                        def g_and_h(b, jj):
                            tm = ptm[b % 2]
                            for c, cr in enumerate(heads2):
                                nc.tensor.matmul(bank[1 + c][:, 0:P], wun[cr, jj, 0, :], tm[cr, jj, 0, :], start=True, stop=True)
                            for c, cr in enumerate(heads2):
                                nc.tensor.matmul(bank[1 + c][:, P:2 * P], tm[cr, jj, 1, :], tm[cr, jj, 2, :], start=True, stop=False)
                                mm = nc.tensor.matmul(bank[1 + c][:, P:2 * P], tm[cr, jj, 0, :], wun[cr, jj, 1, :], start=False, stop=True)
                            mm.then_inc(s["gh"], 1)

                        def y_inside(b, jj):
                            if jj:
                                pe.wait_ge(s["y_kept"], 2 * b + 1)
                            for h, hs in enumerate(heads2):
                                p = 2 * jj + h
                                nc.tensor.matmul(bank[0][:, hs], scm[b % 2][:, p, 3, :], ptm[b % 2][:, jj, 2, hs], start=(h == 0), stop=False, skip_group_check=True)
                                nc.tensor.matmul(bank[0][:, hs], scm[b % 2][:, p, 1, :], wun[:, jj, 1, hs], start=False, stop=False, skip_group_check=True)

                        def chunk(b, jj, c):
                            n, cr = 4 * b + 2 * jj + c, heads2[c]
                            pe.wait_ge(s["state"], n + 1)
                            mm = nc.tensor.matmul(bank[0][cr, 0:P], qp[:, jj, cr], M[:], start=False, stop=True, skip_group_check=True)
                            if c:
                                mm.then_inc(s["y"], 1)
                            nc.tensor.matmul(bank[7][:, 0:P], gt[:, jj, c, :], M[:], start=True, stop=True).then_inc(s["state_mm"], 1)

                        def beside(g, slot):
                            b, f = g - 1, g + 1
                            if b >= 0:
                                if slot == 0:
                                    for p in range(4):
                                        mm = nc.tensor.matmul(bank[6][:, p * 64:(p + 1) * 64], scm[b % 2][:, p, 2, :],
                                                              ptm[b % 2][:, p // 2, 2, heads2[p % 2]], start=True, stop=True)
                                    mm.then_inc(s["x"], 1)
                                elif slot == 1:
                                    pe.wait_ge(s["x_kept"], b + 1)
                                    pe.wait_ge(s["t"], g * (LEVELS + 1))
                                    for p in range(4):
                                        mm = nc.tensor.matmul(bank[6][:, p * P:(p + 1) * P], tt[b % 2][:, p, 1, :], px[:, b % 2, p, :], start=True, stop=True)
                                    mm.then_inc(s["wu"], 1)
                                elif slot == 2:
                                    pe.wait_ge(s["wu_kept"], 2 * g)
                                    for p in range(4):
                                        jj, h = p // 2, p % 2
                                        mm = nc.tensor.matmul(bank[6][heads2[h], jj * P:(jj + 1) * P],
                                                              wun[:, jj, 0, heads2[h]], scm[b % 2][:, p, 1, :], start=True, stop=True)
                                    mm.then_inc(s["q"], 1)
                                elif slot == 3:
                                    g_and_h(b, 0)
                                elif slot == 4:
                                    y_inside(b, 0)
                                    pe.wait_ge(s["q_kept"], b + 1)
                                    pe.wait_ge(s["gh_kept"], 2 * b + 1)
                                    chunk(b, 0, 0)
                                    g_and_h(b, 1)
                                elif slot == 5:
                                    chunk(b, 0, 1)
                                elif slot == 6:
                                    y_inside(b, 1)
                                    pe.wait_ge(s["gh_kept"], 2 * b + 2)
                                    chunk(b, 1, 0)
                                elif slot == 7:
                                    chunk(b, 1, 1)
                            if 0 <= f < NB:
                                if slot == 7:
                                    if b >= 0:
                                        pe.wait_ge(s["y_kept"], 2 * g)
                                    turn(2 * f)
                                elif slot == 8:
                                    if b >= 0:
                                        pe.wait_ge(s["state"], 4 * g + 1)
                                    scores(2 * f)
                                    pe.wait_ge(s["tr_kept"], 2 * f + 1)
                                    turn(2 * f + 1)
                                elif slot == 9:
                                    scores(2 * f + 1)

                        for slot in (7, 8, 9):
                            beside(-1, slot)
                        pe.wait_ge(s["tr_kept"], 2)
                        for g in range(NB + 1):
                            for l in range(LEVELS):
                                if g < NB:
                                    n = g * LEVELS + l
                                    inv = tt[g % 2]
                                    pe.wait_ge(s["t"], g * (LEVELS + 1) + l + 1)
                                    pe.wait_ge(s["nt"], n + 1)
                                    for p in range(4):
                                        mm = nc.tensor.matmul(bank[3][:, p * P:(p + 1) * P], nt[:, n % 2, p, :], inv[:, p, 0, :], start=True, stop=True)
                                    mm.then_inc(s["e"], 1)
                                beside(g, 2 * l)
                                if g < NB:
                                    pe.wait_ge(s["e_kept"], n + 1)
                                    for p in range(4):
                                        b, o = bank[4 + p // 2], 256 * (p % 2)
                                        nc.tensor.matmul(b[:, o:o + P], inv[:, p, 1, :], eb[:, p, :], start=True, stop=True)
                                        mm = nc.tensor.matmul(b[:, o + P:o + 2 * P], eb[:, p, :], inv[:, p, 1, :], start=True, stop=True)
                                        if p % 2:
                                            mm.then_inc(s["dt"], 1)
                                beside(g, 2 * l + 1)
                        pe.wait_ge(s["ynorm"], 1)
                        for q in range(Q):
                            for j in range(4):
                                mm = nc.tensor.transpose(bank[q][:, j * P:(j + 1) * P], Y[:, 4 * q + j, :], k.ident[:])
                            mm.then_inc(s["yt"], 1)

                    @block.scalar
                    def _(act):
                        go = Line(act, s["chain_a"])
                        act.wait_ge(s["par"], 16)
                        for i, (dst, bias) in enumerate(((sw, 3), (a, 4))):
                            for q in range(Q):
                                act.wait_ge(s["wa"], Q * i + q + 1)
                                go(nc.scalar.activation(dst[:, q * QT:(q + 1) * QT], bank[4 * i + q][:], ACT.Sigmoid, bias=par[:, bias:bias + 1]), s["sig"])

                        def keep_raw(i):
                            for q in range(Q):
                                act.wait_ge(s["u"], Q * i + q + 1)
                                go(nc.scalar.activation(raws[i % 2][:, 1 + q * QT:1 + (q + 1) * QT], bank[4 * (i % 2) + q][:], ACT.Copy), s["raw"])
                        act.wait_ge(s["cum"], 1)
                        go(nc.scalar.activation(Rc, cs[:].rearrange("p (j t) -> p j t", t=P), ACT.Exp, scale=-DECAY))
                        act.wait_ge(s["cum"], 2)
                        go(nc.scalar.activation(Pc, Pc, ACT.Exp, scale=-DECAY), s["exps"])
                        keep_raw(0)
                        act.wait_ge(s["kk"], 1)
                        go(nc.scalar.activation(v[:], tmp[:], ACT.Square), s["kk_sq"])
                        keep_raw(1)
                        for q in range(Q):
                            act.wait_ge(s["ssq"], q + 1)
                            go(nc.scalar.activation(v[:, q * QT:(q + 1) * QT], bank[q][:], ACT.Sqrt), s["sqrt"])
                        act.wait_ge(s["raw_read"], 1)
                        keep_raw(2)
                        act.wait_ge(s["raw_read"], 3)
                        go(nc.scalar.activation(KT, cs[:], ACT.Exp, scale=DECAY), s["inv"])
                        for q in range(Q):
                            act.wait_ge(s["u"], 3 * Q + q + 1)
                            go(nc.scalar.activation(sg[:, q * QT:(q + 1) * QT], bank[4 + q][:], ACT.Silu), s["gate"])

                        def beside(g, slot):
                            b = g - 1
                            if b < 0:
                                return
                            if slot == 0:
                                act.wait_ge(s["x"], b + 1)
                                go(nc.scalar.activation(px[:, b % 2, :, 64:128], bank[6][:, 0:256].rearrange("p (n c) -> p n c", c=64), ACT.Copy), s["x_kept"])
                            elif slot == 1:
                                act.wait_ge(s["wu"], b + 1)
                                for jj in range(2):
                                    src = bank[6][:, jj * 256:(jj + 1) * 256].rearrange("p (h u c) -> p u h c", h=2, u=2)
                                    go(nc.scalar.activation(wun[:, jj, :, :].rearrange("p u (h c) -> p u h c", h=2), src, ACT.Copy, scale=-1.0), s["wu_kept"])
                            elif slot in (5, 7):
                                j = 2 * b + (slot - 5) // 2
                                act.wait_ge(s["y"], j + 1)
                                go(nc.scalar.activation(Y[:, j, :], bank[0][:, 0:P], ACT.Copy), s["y_kept"])
                        for g in range(NB + 1):
                            for l in range(LEVELS):
                                if g < NB:
                                    act.wait_ge(s["e"], g * LEVELS + l + 1)
                                    go(nc.scalar.activation(eb, c3(bank[3][:]), ACT.Copy), s["e_kept"])
                                beside(g, 2 * l)
                                beside(g, 2 * l + 1)
                        act.wait_ge(s["yvar"], 1)
                        go(nc.scalar.activation(gst[:, 2, :], gst[:, 1, :], ACT.Sqrt), s["ysd"])

                    @block.vector
                    def _(dve):
                        go = Line(dve, s["chain_v"])
                        t3 = lambda ap: ap.rearrange("p (j t) -> p j t", t=P)
                        for i in range(2):
                            go(nc.vector.memset(raws[i][:, 0:1], 0.0))
                        go(nc.vector.memset(M[:], 0.0), s["state"])
                        dve.wait_ge(s["sig"], Q)
                        for n in range(NCH):
                            ins = nc.vector.tensor_tensor_scan(cs[:, n * C:(n + 1) * C], k.chunk_ones[:], sw[:, n * C:(n + 1) * C], 0.0, ALU.mult, ALU.add)
                        go(ins, s["cum"])
                        go(nc.vector.tensor_tensor(Pc, t3(cs[:]), t3(sw[:]), ALU.subtract), s["cum"])
                        dve.wait_ge(s["par"], 16)

                        def mix(i, dst, mu):
                            dve.wait_ge(s["raw"], Q * (i + 1))
                            raw = raws[i % 2]
                            go(nc.vector.tensor_tensor(dst[:], raw[:, 0:T], raw[:, 1:T + 1], ALU.subtract))
                            go(nc.vector.scalar_tensor_tensor(dst[:], dst[:], par[:, mu:mu + 1], raw[:, 1:T + 1], ALU.mult, ALU.add),
                               s["raw_read"])
                        mix(0, kx, 1)
                        go(nc.vector.tensor_scalar(tmp[:], kx[:], par[:, 5:6], None, ALU.mult), s["kk"])
                        mix(1, r, 0)
                        dve.wait_ge(s["exps"], 1)
                        go(nc.vector.tensor_copy(lc[:], PR[:, :, 1, :].rearrange("p j (c t) -> p j c t", c=2)[:, :, :, C - 1]))
                        go(nc.vector.tensor_tensor(Rc, Rc, t3(r[:]), ALU.mult))
                        dve.wait_ge(s["sqrt"], Q)
                        go(nc.vector.tensor_scalar_max(v[:], v[:], 1e-12))
                        go(nc.vector.reciprocal(v[:], v[:]))
                        go(nc.vector.tensor_tensor(tmp[:], tmp[:], v[:], ALU.mult))
                        go(nc.vector.tensor_tensor(Pc, Pc, t3(tmp[:]), ALU.mult))
                        dve.wait_ge(s["sig"], 2 * Q)
                        go(nc.vector.tensor_tensor(BB, tmp[:], a[:], ALU.mult))
                        go(nc.vector.tensor_scalar(a[:], a[:], -1.0, par[:, 6:7], ALU.add, ALU.mult))
                        go(nc.vector.scalar_tensor_tensor(kx[:], a[:], 1.0, kx[:], ALU.add, ALU.mult))
                        go(nc.vector.scalar_tensor_tensor(tmp[:], r[:], par[:, 7:8], kx[:], ALU.mult, ALU.mult), s["rk"])
                        mix(2, v, 2)
                        dve.wait_ge(s["inv"], 1)
                        go(nc.vector.tensor_tensor(BB, BB, KT, ALU.mult))
                        go(nc.vector.tensor_tensor(KT, KT, kx[:], ALU.mult))
                        for q in range(Q):
                            dve.wait_ge(s["bon"], q + 1)
                            ins = nc.vector.tensor_tensor(sw[:, q * QT:(q + 1) * QT], bank[q][:], v[:, q * QT:(q + 1) * QT], ALU.mult)
                            go(ins, s["forms"] if q == Q - 1 else None)

                        def keep_turned(j):
                            dve.wait_ge(s["tr"], j + 1)
                            par2 = (j // 2) % 2
                            go(nc.vector.tensor_copy(ptm[par2][:, j % 2, :, :], c3(bank[0][:, P:512])))
                            go(nc.vector.tensor_copy(px[:, par2, 2 * (j % 2):2 * (j % 2) + 2, 0:64], bank[0][:, 0:P].rearrange("p (h c) -> p h c", h=2)), s["tr_kept"])

                        def keep_scores(j):
                            for h in range(2):
                                dve.wait_ge(s["sc"], 2 * j + h + 1)
                                go(nc.vector.tensor_tensor(scm[(j // 2) % 2][:, 2 * (j % 2) + h, :, :], c3(bank[1 + h][:]), c3(mk("scores")), ALU.mult), s["sc_kept"])

                        def blocks_of_two(f):
                            inv = tt[f % 2]
                            n1t = mk("corner_t").unsqueeze(1).to_broadcast([P, 4, P])
                            one = k.ident[:].unsqueeze(1).to_broadcast([P, 4, P])
                            go(nc.vector.tensor_tensor(inv[:, :, 1, :], scm[f % 2][:, :, 0, :], n1t, ALU.mult))
                            go(nc.vector.tensor_tensor(inv[:, :, 1, :], inv[:, :, 1, :], one, ALU.add))
                            dve.wait_ge(s["a"], f + 1)
                            for h in range(2):
                                go(nc.vector.tensor_tensor(inv[:, h::2, 0, :], c3(bank[6 + h][:, 0:256]), mk("corner").unsqueeze(1).to_broadcast([P, 2, P]), ALU.mult))
                            go(nc.vector.tensor_tensor(inv[:, :, 0, :], inv[:, :, 0, :], one, ALU.add), s["t"])

                        def keep_g_and_h(b, jj):
                            j = 2 * b + jj
                            dve.wait_ge(s["gh"], j + 1)
                            for c in range(2):
                                n = 2 * j + c
                                go(nc.vector.tensor_tensor(gt[:, jj, c], bank[1 + c][:, 0:P], k.ident[:], ALU.add))
                                go(nc.vector.scalar_tensor_tensor(hh[:, jj, c, :], bank[1 + c][:, P:2 * P], lc[:, n:n + 1], mk("heads"), ALU.mult, ALU.mult))
                            go(nc.vector.tensor_tensor(gt[:, jj], gt[:, jj], mk("heads").unsqueeze(1).to_broadcast([P, 2, P]), ALU.mult), s["gh_kept"])

                        def chunk(b, jj, c):
                            n = 4 * b + 2 * jj + c
                            dve.wait_ge(s["state_mm"], n + 1)
                            go(nc.vector.scalar_tensor_tensor(M[:], bank[7][:, 0:P], lc[:, n:n + 1], hh[:, jj, c, :], ALU.mult, ALU.add), s["state"])

                        def beside(g, slot):
                            b, f = g - 1, g + 1
                            if b >= 0:
                                if slot == 2:
                                    dve.wait_ge(s["q"], b + 1)
                                    go(nc.vector.tensor_tensor(qp[:], c3(bank[6][:, 0:256]), PR[:, 2 * b:2 * b + 2, 1, :], ALU.add), s["q_kept"])
                                elif slot == 3:
                                    keep_g_and_h(b, 0)
                                elif slot == 4:
                                    chunk(b, 0, 0)
                                    keep_g_and_h(b, 1)
                                elif slot == 5:
                                    chunk(b, 0, 1)
                                elif slot == 6:
                                    chunk(b, 1, 0)
                                elif slot == 7:
                                    chunk(b, 1, 1)
                            if 0 <= f < NB:
                                if slot == 7:
                                    keep_turned(2 * f)
                                elif slot == 8:
                                    keep_scores(2 * f)
                                    keep_turned(2 * f + 1)
                                elif slot == 9:
                                    keep_scores(2 * f + 1)
                                    blocks_of_two(f)
                        for slot in (7, 8, 9):
                            beside(-1, slot)
                        for g in range(NB + 1):
                            for l in range(LEVELS):
                                beside(g, 2 * l)
                                if g < NB:
                                    inv = tt[g % 2]
                                    for b in range(2):
                                        dve.wait_ge(s["dt"], 2 * (g * LEVELS + l) + b + 1)
                                        dst = inv[:, 2 * b:2 * b + 2, :, :].rearrange("p n a t -> p (n a t)")
                                        go(nc.vector.tensor_tensor(dst, dst, bank[4 + b][:], ALU.add), s["t"] if b else None)
                                beside(g, 2 * l + 1)
                        dve.wait_ge(s["y_kept"], TT)
                        Yg = tmp[:].rearrange("p (g n) -> p g n", n=64)
                        KTg = KT.rearrange("p (g n) -> p g n", n=64)
                        NG = 2 * TT
                        bc = lambda i: gst[:, i, :].unsqueeze(2).to_broadcast([P, NG, 64])
                        go(nc.vector.tensor_reduce(gst[:, 0, :], Yg, AX.X, ALU.add))
                        go(nc.vector.tensor_scalar(gst[:, 0, :], gst[:, 0, :], 1.0 / 64, None, ALU.mult))
                        go(nc.vector.tensor_tensor(Yg, Yg, bc(0), ALU.subtract))
                        go(nc.vector.tensor_tensor(KT, tmp[:], tmp[:], ALU.mult))
                        go(nc.vector.tensor_reduce(gst[:, 1, :], KTg, AX.X, ALU.add))
                        go(nc.vector.tensor_scalar(gst[:, 1, :], gst[:, 1, :], 1.0 / 64, 64e-5, ALU.mult, ALU.add), s["yvar"])
                        dve.wait_ge(s["ysd"], 1)
                        go(nc.vector.reciprocal(gst[:, 0, :], gst[:, 2, :]))
                        go(nc.vector.tensor_tensor(Yg, Yg, bc(0), ALU.mult), s["ynorm"])
                        dve.wait_ge(s["yt"], Q)
                        for q in range(Q):
                            qs = slice(q * QT, (q + 1) * QT)
                            go(nc.vector.tensor_scalar(tmp[:, qs], bank[q][:], par[:, 8:9], par[:, 9:10], ALU.mult, ALU.add))
                        go(nc.vector.tensor_tensor(tmp[:], tmp[:], sw[:], ALU.add))
                        go(nc.vector.tensor_tensor(tmp[:], tmp[:], sg[:], ALU.mult), s["out"])

                    @block.gpsimd
                    def _(pool):
                        go = Line(pool, s["chain_g"])
                        lm = mk("levels").rearrange("p (l t) -> p l t", t=P)
                        for g in range(NB):
                            for l in range(LEVELS):
                                n = g * LEVELS + l
                                if l == 0:
                                    pool.wait_ge(s["sc_kept"], 4 * (g + 1))
                                if n >= 2:
                                    pool.wait_ge(s["e"], n - 1)
                                go(nc.gpsimd.tensor_tensor(nt[:, n % 2, :, :], scm[g % 2][:, :, 0, :], lm[:, l, :].unsqueeze(1).to_broadcast([P, 4, P]), ALU.mult), s["nt"])
                meet(nc, s)


def gla(nc, k, hT, w_in, gate_up, gate_bias_col, norm_col, mT):
    wv = w_in.rearrange("(kb p) n -> p kb n", p=P)
    with Phase("gl") as ctx:
        s = semaphores(nc, ctx, [
            "w0", "w1", "w2", "w3", "w4", "w5", "wl", "par", "par2", "par3", "u", "lr", "lr_kept", "z", "kept", "zk", "chain_v", "chain_a",
            "ab", "ez", "ln", "cum", "exps", "forms", "tr", "tr_kept", "sc", "sc_kept", "ds", "state", "o", "o_kept",
            "osq", "ovar", "osd", "onorm", "ot", "out0", "out", "stored"])
        wt = [sb(nc, ctx, f"w_block{i}", [P, KD, P]) for i in range(2)]
        wl = sb(nc, ctx, "w_lr", [P, KD, RANK])
        gup = sb(nc, ctx, "gate_up", [RANK, P])
        gb = sb(nc, ctx, "gate_bias", [P, 1])
        nw = sb(nc, ctx, "norm_col", [P, 1])
        glr = sb(nc, ctx, "glr", [RANK, T])
        qx, kx, v0, v1, g0, g1, cs, z = [sb(nc, ctx, n, [P, T]) for n in ("qx", "kx", "v0", "v1", "g0", "g1", "cs", "z")]
        kst = sb(nc, ctx, "kst", [P, T])
        lc = sb(nc, ctx, "chunk_decay", [P, NCH])
        tm = sb(nc, ctx, "tm", [P, 2, 3, P])
        scm = sb(nc, ctx, "scores", [P, 2, 2, P])
        S = sb(nc, ctx, "state", [P, 2, P])
        O = [sb(nc, ctx, f"o{h}", [P, TT, P]) for h in range(2)]
        st = sb(nc, ctx, "o_stat", [P, 3, 2 * TT])
        bank = k.bank
        with nc.Fori(0, 2) as gp:
            with nc.Block() as block:
                @block.sync
                def _(sp):
                    sp.dma_start(wl[:], wv[:, :, GLA_LR:GLA_LR + RANK]).then_inc(s["wl"], 16)
                    sp.dma_start(gup[:], gate_up[:, bass.ds(gp * P, P)]).then_inc(s["par"], 16)
                    sp.dma_start(gb[:], gate_bias_col[gp]).then_inc(s["par2"], 16)
                    sp.dma_start(nw[:], norm_col).then_inc(s["par3"], 16)
                    ats = (gp * P + GLA_Q, gp * P + GLA_K, gp * 256 + GLA_V, gp * 256 + (GLA_V + P), gp * 256 + GLA_G, gp * 256 + (GLA_G + P))
                    for i, at in enumerate(ats):
                        if i >= 2:
                            sp.wait_ge(s["u"], Q * (i - 1))
                        sp.dma_start(wt[i % 2][:], wv[:, :, bass.ds(at, P)]).then_inc((s["w0"], s["w1"], s["w2"], s["w3"], s["w4"], s["w5"])[i], 16)
                    sp.wait_ge(s["out"], 1)
                    sp.dma_start(mT[gp * 2], g0[:]).then_inc(s["stored"], 16)
                    sp.dma_start(mT[gp * 2 + 1], g1[:]).then_inc(s["stored"], 16)
                    sp.wait_ge(s["stored"], 32)

                @block.tensor
                def _(pe):
                    for i in range(6):
                        pe.wait_ge((s["w0"], s["w1"], s["w2"], s["w3"], s["w4"], s["w5"])[i], 16)
                        for q in range(Q):
                            if i >= 2:
                                pe.wait_ge(s["kept"], Q * (i - 2) + q + 1)
                            for kb in range(KD):
                                mm = nc.tensor.matmul(bank[4 * (i % 2) + q][:], wt[i % 2][:, kb, :],
                                                      hT[:, kb, q * QT:(q + 1) * QT], start=(kb == 0), stop=(kb == KD - 1))
                            mm.then_inc(s["u"], 1)
                    pe.wait_ge(s["wl"], 16)
                    pe.wait_ge(s["kept"], 5 * Q)
                    for q in range(Q):
                        for kb in range(KD):
                            mm = nc.tensor.matmul(bank[q][0:RANK, :], wl[:, kb, :], hT[:, kb, q * QT:(q + 1) * QT],
                                                  start=(kb == 0), stop=(kb == KD - 1))
                        mm.then_inc(s["lr"], 1)
                    pe.wait_ge(s["par"], 16)
                    pe.wait_ge(s["kept"], 6 * Q)
                    for q in range(Q):
                        pe.wait_ge(s["lr_kept"], q + 1)
                        nc.tensor.matmul(bank[4 + q][:], gup[:], glr[:, q * QT:(q + 1) * QT], start=True, stop=True).then_inc(s["z"], 1)
                    pe.wait_ge(s["forms"], 1)
                    for j in range(TT):
                        ts = slice(j * P, (j + 1) * P)
                        jj = j % 2
                        if j >= 2:
                            pe.wait_ge(s["tr_kept"], j - 1)
                        for n, src in enumerate((kst[:, ts], v0[:, ts], v1[:, ts])):
                            mm = nc.tensor.transpose(bank[7 * jj][:, n * P:(n + 1) * P], src, k.ident[:])
                        mm.then_inc(s["tr"], 1)
                        if j:
                            pe.wait_ge(s["sc_kept"], j)
                        for h in range(2):
                            hs = slice(64 * h, 64 * h + 64)
                            mm = nc.tensor.matmul(bank[1 + h][:, 0:P], kx[hs, ts], qx[hs, ts], start=True, stop=True)
                        mm.then_inc(s["sc"], 1)
                        pe.wait_ge(s["sc_kept"], j + 1)
                        pe.wait_ge(s["tr_kept"], j + 1)
                        if j:
                            pe.wait_ge(s["o_kept"], j)
                        for h in range(2):
                            nc.tensor.matmul(bank[3 + h][:, 0:P], scm[:, jj, h, :], tm[:, jj, 1 + h, :],
                                             start=True, stop=False, skip_group_check=True)
                        for c in range(2):
                            n = 2 * j + c
                            cr = slice(64 * c, 64 * c + 64)
                            pe.wait_ge(s["state"], n + 1)
                            for h in range(2):
                                hs = slice(64 * h, 64 * h + 64)
                                nc.tensor.matmul(bank[5 + c][hs, 0:P], tm[cr, jj, 0, hs], tm[cr, jj, 1 + h, :], start=True, stop=True)
                            for h in range(2):
                                hs = slice(64 * h, 64 * h + 64)
                                mm = nc.tensor.matmul(bank[3 + h][cr, 0:P], qx[hs, j * P + 64 * c:j * P + 64 * c + 64],
                                                      S[hs, n % 2, :], start=False, stop=True, skip_group_check=True)
                            mm.then_inc(s["ds"], 1)
                    pe.wait_ge(s["onorm"], 1)
                    for h in range(2):
                        for q in range(Q):
                            for j in range(4):
                                mm = nc.tensor.transpose(bank[4 * h + q][:, j * P:(j + 1) * P], O[h][:, 4 * q + j, :], k.ident[:])
                            mm.then_inc(s["ot"], 1)

                @block.scalar
                def _(act):
                    go = Line(act, s["chain_a"])
                    for i, (dst, fn, sc) in enumerate(((qx, ACT.Copy, 0.125), (kx, ACT.Copy, 1.0), (v0, ACT.Copy, 1.0),
                                                       (v1, ACT.Copy, 1.0), (g0, ACT.Silu, 1.0), (g1, ACT.Silu, 1.0))):
                        for q in range(Q):
                            act.wait_ge(s["u"], Q * i + q + 1)
                            go(nc.scalar.activation(dst[:, q * QT:(q + 1) * QT], bank[4 * (i % 2) + q][:], fn, scale=sc), s["kept"])
                    for q in range(Q):
                        act.wait_ge(s["lr"], q + 1)
                        go(nc.scalar.activation(glr[:, q * QT:(q + 1) * QT], bank[q][0:RANK, :], ACT.Copy), s["lr_kept"])
                    act.wait_ge(s["par2"], 16)
                    for q in range(Q):
                        act.wait_ge(s["z"], q + 1)
                        go(nc.scalar.activation(z[:, q * QT:(q + 1) * QT], bank[4 + q][:], ACT.Identity, bias=gb[:, 0:1]), s["zk"])
                    go(nc.scalar.activation(cs[:], z[:], ACT.Abs))
                    go(nc.scalar.activation(cs[:], cs[:], ACT.Exp, scale=-1.0))
                    go(nc.scalar.activation(cs[:], cs[:], ACT.Ln, bias=1.0), s["ln"])
                    act.wait_ge(s["cum"], 2)
                    go(nc.scalar.activation(O[0][:].rearrange("p j t -> p (j t)"), cs[:], ACT.Exp))
                    go(nc.scalar.activation(O[1][:].rearrange("p j t -> p (j t)"), cs[:], ACT.Exp, scale=-1.0))
                    go(nc.scalar.activation(kst[:], z[:], ACT.Exp), s["exps"])
                    for j in range(TT):
                        jj = j % 2
                        act.wait_ge(s["tr"], j + 1)
                        if j >= 2:
                            act.wait_ge(s["ds"], 2 * (j - 1))
                        go(nc.scalar.activation(tm[:, jj, :, :], bank[7 * jj][:, 0:3 * P].rearrange("p (n c) -> p n c", c=P), ACT.Copy), s["tr_kept"])
                        act.wait_ge(s["ds"], 2 * (j + 1))
                        for h in range(2):
                            ins = nc.scalar.activation(O[h][:, j, :], bank[3 + h][:, 0:P], ACT.Copy)
                            if h:
                                go(ins, s["o_kept"])
                            else:
                                go(ins)
                    go(nc.scalar.activation(z[:], O[0][:].rearrange("p j t -> p (j t)"), ACT.Square))
                    go(nc.scalar.activation(cs[:], O[1][:].rearrange("p j t -> p (j t)"), ACT.Square), s["osq"])
                    act.wait_ge(s["ovar"], 1)
                    go(nc.scalar.activation(st[:, 1, :], st[:, 0, :], ACT.Sqrt), s["osd"])

                @block.vector
                def _(dve):
                    go = Line(dve, s["chain_v"])
                    go(nc.vector.memset(S[:, 0, :], 0.0), s["state"])
                    dve.wait_ge(s["ln"], 1)
                    go(nc.vector.tensor_scalar(z[:], z[:], 0.0, None, ALU.min))
                    go(nc.vector.tensor_tensor(z[:], z[:], cs[:], ALU.subtract))
                    go(nc.vector.tensor_scalar(z[:], z[:], 1.0 / 16, None, ALU.mult))
                    for n in range(NCH):
                        ins = nc.vector.tensor_tensor_scan(cs[:, n * C:(n + 1) * C], k.chunk_ones[:], z[:, n * C:(n + 1) * C], 0.0, ALU.mult, ALU.add)
                    go(ins, s["cum"])
                    csn = cs[:].rearrange("p (n t) -> p n t", t=C)
                    go(nc.vector.tensor_copy(lc[:], csn[:, :, C - 1]))
                    go(nc.vector.tensor_tensor(z[:].rearrange("p (n t) -> p n t", t=C), lc[:].unsqueeze(2).to_broadcast([P, NCH, C]), csn, ALU.subtract), s["cum"])
                    dve.wait_ge(s["exps"], 1)
                    e0, e1 = [O[h][:].rearrange("p j t -> p (j t)") for h in range(2)]
                    go(nc.vector.tensor_copy(lc[:], e0.rearrange("p (n t) -> p n t", t=C)[:, :, C - 1]))
                    go(nc.vector.tensor_tensor(kst[:], kst[:], kx[:], ALU.mult))
                    go(nc.vector.tensor_tensor(kx[:], kx[:], e1, ALU.mult))
                    go(nc.vector.tensor_tensor(qx[:], qx[:], e0, ALU.mult), s["forms"])
                    for j in range(TT):
                        jj = j % 2
                        dve.wait_ge(s["sc"], j + 1)
                        if j >= 2:
                            dve.wait_ge(s["ds"], 2 * (j - 1))
                        for h in range(2):
                            ins = nc.vector.tensor_tensor(scm[:, jj, h, :], bank[1 + h][:, 0:P], k.mask("inclusive"), ALU.mult)
                            go(ins, s["sc_kept"] if h else None)
                        for c in range(2):
                            n = 2 * j + c
                            dve.wait_ge(s["ds"], n + 1)
                            go(nc.vector.scalar_tensor_tensor(S[:, (n + 1) % 2, :], S[:, n % 2, :], lc[:, n:n + 1], bank[5 + c][:, 0:P], ALU.mult, ALU.add), s["state"])
                    dve.wait_ge(s["osq"], 1)
                    for h, sq in enumerate((z, cs)):
                        go(nc.vector.tensor_reduce(st[:, 0, h * TT:(h + 1) * TT], sq[:].rearrange("p (j t) -> p j t", t=P), AX.X, ALU.add))
                    go(nc.vector.tensor_scalar(st[:, 0, :], st[:, 0, :], 1.0 / P, EPS, ALU.mult, ALU.add), s["ovar"])
                    dve.wait_ge(s["osd"], 1)
                    go(nc.vector.reciprocal(st[:, 2, :], st[:, 1, :]))
                    for h in range(2):
                        ins = nc.vector.tensor_tensor(O[h][:], O[h][:], st[:, 2, h * TT:(h + 1) * TT].unsqueeze(2).to_broadcast([P, TT, P]), ALU.mult)
                        if h:
                            go(ins, s["onorm"])
                        else:
                            go(ins)
                    dve.wait_ge(s["par3"], 16)
                    for h, g in enumerate((g0, g1)):
                        for q in range(Q):
                            dve.wait_ge(s["ot"], 4 * h + q + 1)
                            qs = slice(q * QT, (q + 1) * QT)
                            ins = nc.vector.scalar_tensor_tensor(g[:, qs], bank[4 * h + q][:], nw[:, 0:1], g[:, qs], ALU.mult, ALU.mult)
                            if h and q == Q - 1:
                                go(ins, s["out"])
                            else:
                                go(ins)
            meet(nc, s)


def out_product(nc, k, mT, w, resid, gate_row, norm_row, shift_row, store, turn_dst, gain, shift, final):
    first = final is not None
    G = 4
    rv = resid.rearrange("(g n p) d -> g p n d", n=G, p=P)
    mv = mT.rearrange("kb p (g t) -> g p kb t", g=TT // G)
    with Phase("op" if first else "oq") as ctx:
        names = ["m", "w", "rows", "r0", "r1", "r2", "r3", "y", "y_read", "chain_v", "chain_a", "sq", "var", "sd", "sq2", "var2", "sd2",
                 "lat", "h", "turned", "kept", "logit", "exp", "row_stat", "aff", "aff_t", "aff_kept", "st_lat", "st_h0", "st_h1"]
        s = semaphores(nc, ctx, names)
        wt = sb(nc, ctx, "w_out", [P, KD, D])
        mt = sb(nc, ctx, "m_tile", [P, KD, G * P])
        x = sb(nc, ctx, "x_tile", [P, G, D])
        h = sb(nc, ctx, "h_tile", [P, 2, D])
        junk = sb(nc, ctx, "square", [P, D])
        stat = sb(nc, ctx, "stat", [P, G, 8])
        row_a = sb(nc, ctx, "row_a", [P, D])
        if not first:
            gated = sb(nc, ctx, "gated", [P, D])
            row_g = sb(nc, ctx, "row_gain", [P, D])
            row_s = sb(nc, ctx, "row_shift", [P, D])
            hT2 = sb(nc, ctx, "h2_turned", [P, KD, P])
            lg = sb(nc, ctx, "softmax", [P, 2, NE])
            ls = sb(nc, ctx, "softmax_stat", [P, 2, 4])
            router = sb(nc, ctx, "router", [P, KD, NE])
        bank = k.bank
        rs = (s["r0"], s["r1"], s["r2"], s["r3"])
        with nc.Block() as block:
            @block.sync
            def _(sp):
                sp.dma_start(wt[:], w.rearrange("(kb p) n -> p kb n", p=P)).then_inc(s["w"], 16)
                if first:
                    sp.dma_start(row_a[:], norm_row.to_broadcast([P, D])).then_inc(s["rows"], 16)
                else:
                    sp.dma_start(row_a[:], gate_row.to_broadcast([P, D])).then_inc(s["rows"], 16)
                    sp.dma_start(row_g[:], norm_row.to_broadcast([P, D])).then_inc(s["rows"], 16)
                    sp.dma_start(row_s[:], shift_row.to_broadcast([P, D])).then_inc(s["rows"], 16)
                    sp.dma_start(router[:], k.router.rearrange("(kb p) n -> p kb n", p=P)).then_inc(s["rows"], 16)
                sp.wait_ge(s["w"], 16)
                sp.wait_ge(s["rows"], 16 if first else 64)
        meet(nc, s)
        with nc.Fori(0, TT // G) as g:
            with nc.Block() as block:
                @block.sync
                def _(sp):
                    sp.dma_start(mt[:], mv[g]).then_inc(s["m"], 16)
                    for n in range(G):
                        sp.dma_start(x[:, n, :], rv[g, :, n, :]).then_inc(rs[n], 16)
                    sv = store.rearrange("(g n p) d -> g p n d", n=G, p=P)
                    hv = k.h2.rearrange("(g n p) d -> g p n d", n=G, p=P)
                    for n in range(G):
                        sp.wait_ge(s["lat"], n + 1)
                        sp.dma_start(sv[g, :, n, :], x[:, n, :]).then_inc(s["st_lat"], 16)
                        if not first:
                            sp.wait_ge(s["h"], n + 1)
                            sp.dma_start(hv[g, :, n, :], h[:, n % 2, :]).then_inc((s["st_h0"], s["st_h1"])[n % 2], 16)
                    sp.wait_ge(s["st_lat"], 16 * G)
                    if not first:
                        sp.wait_ge(s["st_h0"], 32)
                        sp.wait_ge(s["st_h1"], 32)

                @block.tensor
                def _(pe):
                    pe.wait_ge(s["m"], 16)

                    def product(n):
                        if n:
                            pe.wait_ge(s["y_read"], 2 * n)
                        for b in range(2):
                            for kb in range(KD):
                                mm = nc.tensor.matmul(bank[b][:], mt[:, kb, n * P:(n + 1) * P], wt[:, kb, b * 512:(b + 1) * 512],
                                                      start=(kb == 0), stop=(kb == KD - 1))
                            mm.then_inc(s["y"], 1)

                    def turn(n):
                        pe.wait_ge(s["h"], n + 1)
                        if n:
                            pe.wait_ge(s["kept"], 2 * n)
                        for b in range(2):
                            for j in range(4):
                                kb = 4 * b + j
                                mm = nc.tensor.transpose(bank[2 + b][:, j * P:(j + 1) * P], h[:, n % 2, kb * P:(kb + 1) * P], k.ident[:])
                            mm.then_inc(s["turned"], 1)
                        if not first:
                            pe.wait_ge(s["kept"], 2 * n + 2)
                            if n:
                                pe.wait_ge(s["exp"], n)
                            for kb in range(KD):
                                mm = nc.tensor.matmul(bank[4][:, 0:NE], hT2[:, kb, :], router[:, kb, :], start=(kb == 0), stop=(kb == KD - 1))
                            mm.then_inc(s["logit"], 1)
                            pe.wait_ge(s["aff"], n + 1)
                            if n:
                                pe.wait_ge(s["aff_kept"], n)
                            nc.tensor.transpose(bank[5][0:NE, 0:P], lg[:, n % 2, :], k.ident[:]).then_inc(s["aff_t"], 1)
                    for n in range(G):
                        product(n)
                        if n:
                            turn(n - 1)
                    turn(G - 1)

                @block.scalar
                def _(act):
                    go = Line(act, s["chain_a"])

                    def exponential(n):
                        act.wait_ge(s["row_stat"], 2 * n + 1)
                        go(nc.scalar.activation(lg[:, n % 2, :], bank[4][:, 0:NE], ACT.Exp, bias=ls[:, n % 2, 0:1], accum_out=ls[:, n % 2, 1:2]), s["exp"])
                    for n in range(G):
                        if first:
                            act.wait_ge(s["y_read"], 2 * (n + 1))
                        else:
                            act.wait_ge(s["lat"], n + 1)
                        norm_stats(nc, go, None, act, None, s["sq"], s["var"], s["sd"], n, x[:, n, :], junk[:], stat[:, n, 0:4], "act")
                        if first:
                            act.wait_ge(s["lat"], n + 1)
                            norm_stats(nc, go, None, act, None, s["sq2"], s["var2"], s["sd2"], n, x[:, n, :], junk[:], stat[:, n, 4:8], "act")
                        elif n:
                            exponential(n - 1)
                    if not first:
                        exponential(G - 1)

                @block.vector
                def _(dve):
                    go = Line(dve, s["chain_v"])

                    def keep(n):
                        for b in range(2):
                            dve.wait_ge(s["turned"], 2 * n + b + 1)
                            src = bank[2 + b][:].rearrange("p (k t) -> p k t", t=P)
                            if first:
                                dst = turn_dst[:, 4 * b:4 * b + 4, bass.ds(g * (G * P) + n * P, P)]
                                go(nc.vector.tensor_tensor(dst, src, gain[:, 4 * b:4 * b + 4].unsqueeze(2).to_broadcast([P, 4, P]), ALU.mult))
                                go(nc.vector.tensor_tensor(dst, dst, shift[:, 4 * b:4 * b + 4].unsqueeze(2).to_broadcast([P, 4, P]), ALU.add), s["kept"])
                            else:
                                go(nc.vector.tensor_copy(hT2[:, 4 * b:4 * b + 4, :], src), s["kept"])

                    def softmax(n):
                        dve.wait_ge(s["logit"], n + 1)
                        go(nc.vector.tensor_reduce(ls[:, n % 2, 2:3], bank[4][:, 0:NE], AX.X, ALU.max))
                        go(nc.vector.tensor_scalar(ls[:, n % 2, 0:1], ls[:, n % 2, 2:3], -1.0, None, ALU.mult), s["row_stat"])
                        dve.wait_ge(s["exp"], n + 1)
                        go(nc.vector.reciprocal(ls[:, n % 2, 3:4], ls[:, n % 2, 1:2]), s["row_stat"])
                        go(nc.vector.tensor_scalar(lg[:, n % 2, :], lg[:, n % 2, :], ls[:, n % 2, 3:4], None, ALU.mult), s["aff"])
                        dve.wait_ge(s["aff_t"], n + 1)
                        go(nc.vector.tensor_copy(turn_dst[:, bass.ds(g * (G * P) + n * P, P)], bank[5][0:NE, 0:P]), s["aff_kept"])
                    for n in range(G):
                        dve.wait_ge(rs[n], 16)
                        for b in range(2):
                            dve.wait_ge(s["y"], 2 * n + b + 1)
                            bs = slice(b * 512, (b + 1) * 512)
                            if first:
                                go(nc.vector.tensor_tensor(x[:, n, bs], x[:, n, bs], bank[b][:], ALU.add), s["y_read"])
                            else:
                                go(nc.vector.tensor_tensor(gated[:, bs], bank[b][:], row_a[:, bs], ALU.mult), s["y_read"])
                        if not first:
                            go(nc.vector.tensor_tensor(x[:, n, :], x[:, n, :], gated[:], ALU.add), s["lat"])
                        norm_stats(nc, None, go, None, dve, s["sq"], s["var"], s["sd"], n, None, None, stat[:, n, 0:4], "dve")
                        if first:
                            go(nc.vector.scalar_tensor_tensor(x[:, n, :], x[:, n, :], stat[:, n, 3:4], row_a[:], ALU.mult, ALU.mult), s["lat"])
                            norm_stats(nc, None, go, None, dve, s["sq2"], s["var2"], s["sd2"], n, None, None, stat[:, n, 4:8], "dve")
                            if n >= 2:
                                dve.wait_ge(s["turned"], 2 * (n - 1))
                            go(nc.vector.tensor_scalar(h[:, n % 2, :], x[:, n, :], stat[:, n, 7:8], None, ALU.mult), s["h"])
                            if n:
                                keep(n - 1)
                        else:
                            if n >= 2:
                                dve.wait_ge(s["turned"], 2 * (n - 1))
                                dve.wait_ge((s["st_h0"], s["st_h1"])[n % 2], 16)
                            go(nc.vector.scalar_tensor_tensor(h[:, n % 2, :], x[:, n, :], stat[:, n, 3:4], row_g[:], ALU.mult, ALU.mult))
                            go(nc.vector.tensor_tensor(h[:, n % 2, :], h[:, n % 2, :], row_s[:], ALU.add), s["h"])
                            if n:
                                keep(n - 1)
                                softmax(n - 1)
                    keep(G - 1)
                    if not first:
                        softmax(G - 1)

            meet(nc, s)


def short_conv(nc, k, hT, w_in, conv_col, zT):
    wv = w_in.rearrange("(kb p) n -> p kb n", p=P)
    with Phase("sc") as ctx:
        s = semaphores(nc, ctx, ["w0", "w1", "w2", "par", "u", "c_kept", "g_kept", "b_kept", "chain_v", "chain_a", "out", "stored"])
        wt = [sb(nc, ctx, f"w_block{i}", [P, KD, P]) for i in range(3)]
        cw = sb(nc, ctx, "conv_cols", [P, 3])
        gv = sb(nc, ctx, "gated", [P, T + 2])
        acc = sb(nc, ctx, "conv", [P, T])
        bank = k.bank
        with nc.Fori(0, KD) as cb:
            with nc.Block() as block:
                @block.sync
                def _(sp):
                    for i, at in enumerate((D, 2 * D, 0)):
                        sp.dma_start(wt[i][:], wv[:, :, bass.ds(cb * P + at, P)]).then_inc((s["w0"], s["w1"], s["w2"])[i], 16)
                    sp.dma_start(cw[:], conv_col[cb]).then_inc(s["par"], 16)
                    sp.wait_ge(s["out"], Q)
                    sp.dma_start(zT[cb], acc[:]).then_inc(s["stored"], 16)
                    sp.wait_ge(s["stored"], 16)

                @block.tensor
                def _(pe):
                    for i in range(3):
                        pe.wait_ge((s["w0"], s["w1"], s["w2"])[i], 16)
                        for q in range(Q):
                            if i == 2:
                                pe.wait_ge(s["c_kept"], q + 1)
                            for kb in range(KD):
                                mm = nc.tensor.matmul(bank[4 * (i % 2) + q][:], wt[i][:, kb, :], hT[:, kb, q * QT:(q + 1) * QT],
                                                      start=(kb == 0), stop=(kb == KD - 1))
                            mm.then_inc(s["u"], 1)

                @block.scalar
                def _(act):
                    go = Line(act, s["chain_a"])
                    for q in range(Q):
                        act.wait_ge(s["u"], q + 1)
                        go(nc.scalar.activation(gv[:, 1 + q * QT:1 + (q + 1) * QT], bank[q][:], ACT.Copy), s["c_kept"])

                @block.vector
                def _(dve):
                    go = Line(dve, s["chain_v"])
                    go(nc.vector.memset(gv[:, 0:1], 0.0))
                    go(nc.vector.memset(gv[:, T + 1:T + 2], 0.0))
                    for q in range(Q):
                        dve.wait_ge(s["c_kept"], q + 1)
                        dve.wait_ge(s["u"], Q + q + 1)
                        qs = slice(1 + q * QT, 1 + (q + 1) * QT)
                        go(nc.vector.tensor_tensor(gv[:, qs], gv[:, qs], bank[4 + q][:], ALU.mult))
                    dve.wait_ge(s["par"], 16)
                    go(nc.vector.tensor_scalar(acc[:], gv[:, 0:T], cw[:, 0:1], None, ALU.mult))
                    go(nc.vector.scalar_tensor_tensor(acc[:], gv[:, 1:T + 1], cw[:, 1:2], acc[:], ALU.mult, ALU.add))
                    go(nc.vector.scalar_tensor_tensor(acc[:], gv[:, 2:T + 2], cw[:, 2:3], acc[:], ALU.mult, ALU.add))
                    for q in range(Q):
                        dve.wait_ge(s["u"], 2 * Q + q + 1)
                        qs = slice(q * QT, (q + 1) * QT)
                        go(nc.vector.tensor_tensor(acc[:, qs], acc[:, qs], bank[q][:], ALU.mult), s["out"])
            meet(nc, s)


def choose(nc, k, aff, idx_all, gate_all):
    with Phase("ch") as ctx:
        s = semaphores(nc, ctx, ["chain_v", "picked", "turned"])
        vals = sb(nc, ctx, "top", [NE, CAP])
        idx = sb(nc, ctx, "top_idx", [NE, CAP], U32)
        idf = sb(nc, ctx, "top_idx_f", [NE, CAP])
        bank = k.bank
        with nc.Block() as block:
            @block.vector
            def _(dve):
                go = Line(dve, s["chain_v"])
                for i in range(CAP // 8):
                    e = slice(8 * i, 8 * i + 8)
                    go(nc.vector.max(vals[:, e], aff[:]))
                    go(nc.vector.max_index(idx[:, e], vals[:, e], aff[:]))
                    if i < CAP // 8 - 1:
                        go(nc.vector.match_replace(aff[:], vals[:, e], aff[:], -1.0))
                go(nc.vector.tensor_copy(idf[:], idx[:]), s["picked"])
                dve.wait_ge(s["turned"], 1)
                go(nc.vector.tensor_copy(idx_all[:], bank[0][:, 0:2 * NE]))
                go(nc.vector.tensor_copy(gate_all[:], bank[0][:, 2 * NE:4 * NE]))

            @block.tensor
            def _(pe):
                pe.wait_ge(s["picked"], 1)
                for n, src in enumerate((idf, vals)):
                    for h in range(2):
                        o = (2 * n + h) * NE
                        mm = nc.tensor.transpose(bank[0][:, o:o + NE], src[:, h * P:(h + 1) * P], k.ident[0:NE, 0:NE])
                mm.then_inc(s["turned"], 1)
        meet(nc, s)


def experts(nc, k, wg, wu, wd, idx_all, gate_all, out):
    gv = wg.rearrange("o e (kb p) f -> (o e) p kb f", p=P)
    uv = wu.rearrange("o e (kb p) f -> (o e) p kb f", p=P)
    dv = wd.rearrange("o e (kb p) d -> p (o e kb) d", p=P)
    CH, LOADED, SPLIT, W = 12, 4, 6, KD * 256
    F32R = mybir.dt.float32r
    with Phase("ex") as ctx:
        s = semaphores(nc, ctx, ["row", "load0", "load1", "load2", "load3", "hi", "lo", "used", "turned", "x_hi", "x_lo", "gu", "silu",
                                 "hid", "hid_hi", "hid_lo", "y", "ys", "idx", "gates", "chain_v"])
        gathered = [ctx.enter_context(nc.semaphore(f"gathered{h}")) for h in range(2)]
        sent = [ctx.enter_context(nc.semaphore(f"sent{h}")) for h in range(2)]
        mark = sb(nc, ctx, "mark", [P, 1])
        raw = sb(nc, ctx, "w_loaded", [P, LOADED, W])
        w_hi = [sb(nc, ctx, f"w_hi{i}", [P, W], F32R) for i in range(SPLIT)]
        w_lo = [sb(nc, ctx, f"w_lo{i}", [P, W], F32R) for i in range(SPLIT)]
        xg = sb(nc, ctx, "x_gathered", [P, 2, D])
        x_hi = sb(nc, ctx, "x_hi", [P, KD, CAP], F32R)
        x_lo = sb(nc, ctx, "x_lo", [P, KD, CAP], F32R)
        h_hi = sb(nc, ctx, "hid_hi", [P, KD, CAP], F32R)
        h_lo = sb(nc, ctx, "hid_lo", [P, KD, CAP], F32R)
        sl = sb(nc, ctx, "silu", [P, 2, CAP])
        hid = sb(nc, ctx, "hidden", [P, 2, CAP])
        ys = sb(nc, ctx, "y", [P, 2, D])
        g2 = sb(nc, ctx, "g2_row", [P, D])
        idx = sb(nc, ctx, "idx", [P, 2, 2], U32)
        gates = sb(nc, ctx, "gates", [P, 2])
        bank = k.bank
        idv = idx_all[:].rearrange("p (h e) -> p h e", h=2)
        gav = gate_all[:].rearrange("p (h e) -> p h e", h=2)
        loads = [s[f"load{i}"] for i in range(LOADED)]

        def load(sp, e, c):
            views = (gv, uv) if c < CH else (gv[1:], uv[1:])
            c = c % CH
            dst = raw[:, c % LOADED, :]
            if c < 8:
                src = views[c % 2][e, :, :, (c // 2) * 256:(c // 2 + 1) * 256]
                dst = dst.rearrange("p (kb f) -> p kb f", f=256)
            else:
                dst = dst.rearrange("p (kb d) -> p kb d", d=D)
                src = dv[:, bass.ds(e * KD + (c - 8) * 2, 2), :]
            sp.dma_start(dst, src).then_inc(loads[c % LOADED], 16)

        def split_hi(act, e, c):
            act.wait_ge(loads[c % LOADED], e * 48 + 16 * (c // LOADED + 1))
            nc.scalar.activation(w_hi[c % SPLIT][:], raw[:, c % LOADED, :], ACT.Copy).then_inc(s["hi"], 1)

        def split_lo(dve, e, c):
            dve.wait_ge(s["hi"], e * CH + c + 1)
            nc.vector.tensor_tensor(w_lo[c % SPLIT][:], raw[:, c % LOADED, :], w_hi[c % SPLIT][:].bitcast(F32), ALU.subtract).then_inc(s["lo"], 1)

        def passes(psum, lh, ll, rh, rl, first, last):
            nc.tensor.matmul(psum, ll, rh, start=first, stop=False)
            nc.tensor.matmul(psum, lh, rl, start=False, stop=False)
            return nc.tensor.matmul(psum, lh, rh, start=False, stop=last)

        def turn_tokens(pe):
            for h in range(2):
                for b in range(2):
                    for j in range(4):
                        kb = 4 * b + j
                        mm = nc.tensor.transpose(bank[2 * h + b][:, j * P:(j + 1) * P], xg[:, h, kb * P:(kb + 1) * P], k.ident[:])
                    mm.then_inc(s["turned"], 1)

        def each_turned(do):
            for h in range(2):
                for b in range(2):
                    do(2 * h + b, (slice(None), slice(4 * b, 4 * b + 4), slice(h * P, (h + 1) * P)), bank[2 * h + b][:].rearrange("p (k t) -> p k t", t=P))

        with nc.Block() as block:
            @block.sync
            def _(sp):
                sp.dma_start(g2[:], k.rows_dram[3:4, :].to_broadcast([P, D])).then_inc(s["row"], 16)
                for c in range(LOADED):
                    load(sp, 0, c)

                def turn(e, last):
                    for c in range(CH - LOADED if last else CH):
                        sp.wait_ge(s["lo"], e * CH + c + 1)
                        load(sp, e, c + LOADED)
                with sp.Fori(0, NE - 1) as e:
                    turn(e, False)
                turn(NE - 1, True)

            @block.gpsimd
            def _(pool):
                def passed(pool):
                    nc.gpsimd.tensor_tensor(mark[:], k.ident[:, 0:1], k.ident[:, 0:1], ALU.mult).then_inc(s["idx"], 1)

                def gather(e, copied):
                    nc.gpsimd.tensor_copy(idx[:, :, 1:2], idv[:, :, bass.ds(e, 1)]).then_inc(s["idx"], 1)
                    pool.wait_ge(s["idx"], copied)
                    passed(pool)
                    for h in range(2):
                        pool.indirect_dma_start(out=xg[:, h, :], out_offset=None, in_=k.h2,
                                                in_offset=bass.IndirectOffsetOnAxis(ap=idx[:, h, 1:2], axis=0)).then_inc(gathered[h], 16)

                def scatter(e, copied):
                    nc.gpsimd.tensor_copy(idx[:, :, 0:1], idv[:, :, bass.ds(e, 1)]).then_inc(s["idx"], 1)
                    pool.wait_ge(s["idx"], copied)
                    pool.wait_ge(s["ys"], e * 2 + 3)
                    passed(pool)
                    for h in range(2):
                        pool.indirect_dma_start(out=out, out_offset=bass.IndirectOffsetOnAxis(ap=idx[:, h, 0:1], axis=0),
                                                in_=ys[:, h, :], in_offset=None, compute_op=ALU.add).then_inc(sent[h], 16)
                    for h in range(2):
                        pool.wait_ge(sent[h], e * 16 + 16)
                gather(0, 1)
                with pool.Fori(0, NE - 1) as e:
                    for h in range(2):
                        pool.wait_ge(gathered[h], e * 16 + 16)
                    pool.wait_ge(s["turned"], e * 4 + 4)
                    gather(e + 1, e * 4 + 3)
                    scatter(e, e * 4 + 5)
                scatter(NE - 1, NE * 4 - 1)

            @block.tensor
            def _(pe):
                for h in range(2):
                    pe.wait_ge(gathered[h], 16)
                turn_tokens(pe)

                def turn(e, last):
                    pe.wait_ge(s["x_lo"], e * 4 + 4)
                    for f in range(KD):
                        q = f // 2
                        if f >= 2:
                            pe.wait_ge(s["hid"], e * KD + f - 1)
                        for half in range(2):
                            c = 2 * q + half
                            if f % 2 == 0:
                                pe.wait_ge(s["lo"], e * CH + c + 1)
                            for kb in range(KD):
                                o = kb * 256 + (f % 2) * P
                                mm = passes(bank[2 * (f % 2) + half][:, 0:CAP], w_hi[c % SPLIT][:, o:o + P], w_lo[c % SPLIT][:, o:o + P],
                                            x_hi[:, kb, :], x_lo[:, kb, :], kb == 0, kb == KD - 1)
                            mm.then_inc(s["gu"], 1)
                    if not last:
                        pe.wait_ge(s["hid"], e * KD + KD)
                        for h in range(2):
                            pe.wait_ge(gathered[h], e * 16 + 32)
                        turn_tokens(pe)
                    pe.wait_ge(s["ys"], e * 2 + 1)
                    for f in range(KD):
                        c = 8 + f // 2
                        pe.wait_ge(s["hid_lo"], e * KD + f + 1)
                        if f % 2 == 0:
                            pe.wait_ge(s["lo"], e * CH + c + 1)
                        for h in range(2):
                            hs = slice(h * P, (h + 1) * P)
                            for b in range(2):
                                o = (f % 2) * D + b * 512
                                mm = passes(bank[4 + 2 * h + b][:], h_hi[:, f, hs], h_lo[:, f, hs], w_hi[c % SPLIT][:, o:o + 512],
                                            w_lo[c % SPLIT][:, o:o + 512], f == 0, f == KD - 1)
                        if f % 2:
                            mm.then_inc(s["y"], 1)
                with pe.Fori(0, NE - 1) as e:
                    turn(e, False)
                turn(NE - 1, True)

            @block.scalar
            def _(act):
                for c in range(SPLIT):
                    split_hi(act, 0, c)

                def keep(n, at, src):
                    nc.scalar.activation(x_hi[at], src, ACT.Copy).then_inc(s["x_hi"], 1)

                def first(n, at, src):
                    act.wait_ge(s["turned"], n + 1)
                    keep(n, at, src)
                each_turned(first)

                def turn(e, last):
                    for f in range(KD):
                        act.wait_ge(s["gu"], e * 2 * KD + 2 * f + 1)
                        nc.scalar.activation(sl[:, f % 2, :], bank[2 * (f % 2)][:, 0:CAP], ACT.Silu).then_inc(s["silu"], 1)
                        act.wait_ge(s["hid"], e * KD + f + 1)
                        nc.scalar.activation(h_hi[:, f, :], hid[:, f % 2, :], ACT.Copy).then_inc(s["hid_hi"], 1)
                        if f % 2:
                            for c in (f - 1, f):
                                if last and c + SPLIT >= CH:
                                    continue
                                act.wait_ge(s["gu"], e * 2 * KD + 2 * f + 2)
                                wrap = (e + 1, c + SPLIT - CH) if c + SPLIT >= CH else (e, c + SPLIT)
                                split_hi(act, *wrap)
                    if not last:
                        def following(n, at, src):
                            act.wait_ge(s["turned"], e * 4 + 5 + n)
                            keep(n, at, src)
                        each_turned(following)
                        for d in range(4):
                            act.wait_ge(s["y"], e * 4 + d + 1)
                            split_hi(act, e + 1, 2 + d)
                with act.Fori(0, NE - 1) as e:
                    turn(e, False)
                turn(NE - 1, True)

            @block.vector
            def _(dve):
                nc.vector.memset(ys[:], 0.0).then_inc(s["ys"], 1)
                dve.wait_ge(s["row"], 16)
                for c in range(SPLIT):
                    split_lo(dve, 0, c)

                def keep(n, at, src):
                    nc.vector.tensor_tensor(x_lo[at], src, x_hi[at].bitcast(F32), ALU.subtract).then_inc(s["x_lo"], 1)

                def first(n, at, src):
                    dve.wait_ge(s["x_hi"], n + 1)
                    keep(n, at, src)
                each_turned(first)

                def turn(e, last):
                    for f in range(KD):
                        dve.wait_ge(s["gu"], e * 2 * KD + 2 * f + 2)
                        dve.wait_ge(s["silu"], e * KD + f + 1)
                        nc.vector.tensor_tensor(hid[:, f % 2, :], sl[:, f % 2, :], bank[2 * (f % 2) + 1][:, 0:CAP], ALU.mult).then_inc(s["hid"], 1)
                        dve.wait_ge(s["hid_hi"], e * KD + f + 1)
                        nc.vector.tensor_tensor(h_lo[:, f, :], hid[:, f % 2, :], h_hi[:, f, :].bitcast(F32), ALU.subtract).then_inc(s["hid_lo"], 1)
                        if f % 2:
                            for c in (f - 1, f):
                                if last and c + SPLIT >= CH:
                                    continue
                                wrap = (e + 1, c + SPLIT - CH) if c + SPLIT >= CH else (e, c + SPLIT)
                                split_lo(dve, *wrap)
                    if not last:
                        def following(n, at, src):
                            dve.wait_ge(s["x_hi"], e * 4 + 5 + n)
                            keep(n, at, src)
                        each_turned(following)
                        for d in range(4):
                            split_lo(dve, e + 1, 2 + d)
                    nc.vector.tensor_copy(gates[:], gav[:, :, bass.ds(e, 1)].rearrange("p h e -> p (h e)")).then_inc(s["gates"], 1)
                    dve.wait_ge(s["gates"], e + 1)
                    dve.wait_ge(s["y"], e * 4 + 4)
                    for h in range(2):
                        dve.wait_ge(s["idx"], e * 4 + 3)
                        for b in range(2):
                            bs = slice(b * 512, (b + 1) * 512)
                            ins = nc.vector.scalar_tensor_tensor(ys[:, h, bs], bank[4 + 2 * h + b][:], gates[:, h:h + 1], g2[:, bs], ALU.mult, ALU.mult)
                        ins.then_inc(s["ys"], 1)
                with dve.Fori(0, NE - 1) as e:
                    turn(e, False)
                turn(NE - 1, True)
        meet(nc, s)


MASKS = ("ident", "head_ones", "heads", "scores", "corner", "corner_t", "levels", "inclusive")


def mask_constants():
    i = np.arange(P)
    s, t = i[:, None], i[None, :]
    same = (s // C) == (t // C)
    strict, incl = (s < t) & same, (s <= t) & same
    heads = (s // 64) == (t // 64)

    def merge(b):
        return (s // (2 * b) == t // (2 * b)) & (s // b % 2 == 0) & (t // b % 2 == 1)

    parts = {
        "ident": s == t, "head_ones": heads, "heads": heads,
        "scores": np.concatenate([strict, incl, strict, incl], 1),
        "corner": -(merge(1).T.astype(np.float32)), "corner_t": -(merge(1).astype(np.float32)),
        "levels": np.concatenate([-(merge(2 << l).astype(np.float32)) for l in range(LEVELS)], 1),
        "inclusive": incl,
    }
    place, at, cols = {}, 0, []
    for name in MASKS:
        a = parts[name].astype(np.float32)
        place[name] = (at, a.shape[1])
        at += a.shape[1]
        cols.append(a)
    return np.ascontiguousarray(np.concatenate(cols, 1)), place, at


def hybrid_conv_moe(nc, x, norm_w_col, w_in, gate_up, gate_bias_col, gla_norm_col, mu_lora_col, w_up, a_up,
                    rwkv_cols, w_out, final_norm, c_col, ada_w, ada_b, ada_b_col, norm_g, norm_g_col,
                    sc_w_in, sc_conv_col, sc_w_out, router, wg, wu, wd, masks, out):
    _, place, width = mask_constants()
    k = Shared()
    k.router = router
    k.rows_dram = nc.dram_tensor("mod_rows_dram", [4, D], F32).ap()
    k.h2 = nc.dram_tensor("h2_dram", [T, D], F32).ap()
    lat = nc.dram_tensor("lat_dram", [T, D], F32).ap()
    mT = nc.dram_tensor("merged_dram", [KD, P, T], F32).ap()
    zT = nc.dram_tensor("z_dram", [KD, P, T], F32).ap()
    k.mask_in = masks
    k.bank = [nc.alloc_psum_tensor(f"bank{i}", [P, 512], F32) for i in range(8)]
    with Phase("mixers") as top:
        k.mask_sb = sb(nc, top, "masks", [P, width])
        k.mask = lambda name: k.mask_sb[:, place[name][0]:place[name][0] + place[name][1]]
        k.ident = k.mask_sb[:, 0:P]
        k.ones = sb(nc, top, "ones", [P, C])
        k.chunk_ones = k.ones
        k.shift1 = sb(nc, top, "shift1", [P, KD])
        k.gain1 = sb(nc, top, "gain1", [P, KD])
        modulation(nc, k, c_col, ada_w[0], ada_b, ada_b_col, norm_g[0], norm_g_col)
        hT = sb(nc, top, "hT", [P, KD, T])
        first_norm(nc, k, x, hT, norm_w_col)
        rwkv(nc, k, hT, w_in[0], w_up[0], a_up[0], rwkv_cols, mu_lora_col, mT)
        gla(nc, k, hT, w_in[0], gate_up[0], gate_bias_col, gla_norm_col, mT)
        out_product(nc, k, mT, w_out[0], x[0], None, final_norm, None, lat, hT, k.gain1, k.shift1, True)
        short_conv(nc, k, hT, sc_w_in[0], sc_conv_col, zT)
    with Phase("moe") as top:
        mask2 = sb(nc, top, "ident2", [P, P])
        aff = sb(nc, top, "affinity", [NE, T])
        idx_all = sb(nc, top, "idx_all", [P, 2 * NE], U32)
        gate_all = sb(nc, top, "gate_all", [P, 2 * NE])
        k.ident = mask2
        s = semaphores(nc, top, ["load"])
        with nc.Block() as block:
            @block.sync
            def _(sp):
                sp.dma_start(mask2[:], masks[:, 0:P]).then_inc(s["load"], 16)
                sp.wait_ge(s["load"], 16)
        meet(nc, s)
        rows = k.rows_dram
        out_product(nc, k, zT, sc_w_out[0], lat, rows[0:1, :], rows[2:3, :], rows[1:2, :], out[0], aff, None, None, None)
        choose(nc, k, aff, idx_all, gate_all)
        experts(nc, k, wg, wu, wd, idx_all, gate_all, out[0])


def lay_out(inputs):
    f = lambda name: np.ascontiguousarray(inputs[name])
    col = lambda v, n: np.ascontiguousarray(v.reshape(n, P).T)
    mu = f("rwkv_mu")[0]
    hp = lambda v: v.reshape(4, P)
    zero = np.zeros((4, P), np.float32)
    params = [hp(mu[0:512]), hp(mu[512:1024]), hp(mu[1024:1536]), hp(f("rwkv_w0")[0]), hp(f("rwkv_a0")[0]),
              hp(f("rwkv_k_k")[0]), hp(f("rwkv_k_a")[0]), hp(f("rwkv_r_k")[0].reshape(-1)),
              hp(f("rwkv_ln_w")[0]), hp(f("rwkv_ln_b")[0]), zero, zero]
    ada_b = f("ada_b_2")
    return {
        "x": f("x"), "norm_w_col": col(f("norm_w")[0], KD), "w_in": f("w_in"), "gate_up": f("gla_gate_up"),
        "gate_bias_col": np.ascontiguousarray(f("gla_gate_bias")[0].reshape(2, P, 1)),
        "gla_norm_col": np.ascontiguousarray(f("gla_norm_w")[0].reshape(P, 1)),
        "mu_lora_col": np.ascontiguousarray(mu[1536:1664].reshape(P, 1)), "w_up": f("rwkv_w_up"), "a_up": f("rwkv_a_up"),
        "rwkv_cols": np.ascontiguousarray(np.stack(params, -1)), "w_out": f("w_out"),
        "final_norm": np.ascontiguousarray(f("final_norm_w").reshape(1, D)), "c_col": col(f("c_2")[0], KD),
        "ada_w": f("ada_w_2"), "ada_b": ada_b, "ada_b_col": col(ada_b[0, 0:2 * D], 2 * KD), "norm_g": f("norm_g_2"),
        "norm_g_col": col(f("norm_g_2")[0, 0], KD), "sc_w_in": f("sc_w_in_2"),
        "sc_conv_col": np.ascontiguousarray(f("sc_conv_2")[0].reshape(3, KD, P).transpose(1, 2, 0)),
        "sc_w_out": f("sc_w_out_2"), "router": np.ascontiguousarray(f("moe_router_2")[0]),
        "wg": f("moe_w_gate_2"), "wu": f("moe_w_up_2"), "wd": f("moe_w_down_2"), "masks": mask_constants()[0],
    }


def kernel(**inputs):
    import concourse.bacc as bacc
    from concourse.bass_utils import run_bass_kernel_spmd

    nc = bacc.Bacc("TRN2", target_bir_lowering=False, num_devices=1)
    arrays, args = {}, []
    for name, a in lay_out(inputs).items():
        arrays[f"in_{name}"] = a
        args.append(nc.dram_tensor(f"in_{name}", a.shape, mybir.dt.from_np(a.dtype), kind="ExternalInput").ap())
    args.append(nc.dram_tensor("out_0", (1, T, D), F32, kind="ExternalOutput").ap())
    hybrid_conv_moe(nc, *args)
    r = run_bass_kernel_spmd(nc, [arrays], core_ids=[0])
    return r.results[0]["out_0"]
```

```python
from contextlib import ExitStack

import numpy as np

import concourse.bass as bass
from concourse import mybir

F32 = mybir.dt.float32
U32 = mybir.dt.uint32
ALU = mybir.AluOpType
ACT = mybir.ActivationFunctionType
AX = mybir.AxisListType

P = 128
T = 2048
D = 1024
KD = D // P
TT = T // P
Q = 4
QT = T // Q
EPS = 1e-6
C = 64
NCH = T // C
GLA_Q, GLA_K, GLA_V, GLA_LR, GLA_G = 0, 256, 512, 1024, 1040
RWKV0 = 1552
RW_R, RW_K, RW_V, RW_L, RW_G = RWKV0, RWKV0 + 512, RWKV0 + 1024, RWKV0 + 1536, RWKV0 + 1664
RANK = 16
DECAY = float(np.exp(-0.5))
NE, CAP = 16, 256
LEVELS = 5


class Shared:
    pass


class Line:

    def __init__(self, engine, chain):
        self.engine, self.chain, self.n = engine, chain, {}

    def __call__(self, instruction, signal=None):
        s = signal if signal is not None else self.chain
        self.n[s.num] = self.n.get(s.num, 0) + 1
        instruction.then_inc(s, 1)
        self.engine.wait_ge(s, self.n[s.num])


def semaphores(nc, ctx, names):
    return {name: ctx.enter_context(nc.semaphore(f"{ctx.name}_{name}")) for name in names}


def meet(nc, s):
    numbers = [x.num for x in s.values()]
    nc.all_engine_barrier(sems_to_clear=range(min(numbers), max(numbers) + 1))


class Phase(ExitStack):

    def __init__(self, name):
        super().__init__()
        self.name = name


def sb(nc, ctx, name, shape, dt=F32):
    return ctx.enter_context(nc.sbuf_tensor(f"{ctx.name}_{name}", shape, dt))


def wait_for(engine, semaphore, value):
    if not isinstance(value, int) or value > 0:
        engine.wait_ge(semaphore, value)


def modulate_and_norm(nc, k, c_col, ada_w, ada_b, ada_b_col, norm_g, norm_g_col, x, hT, norm_w_col):
    G = 4
    TURNS = TT // G
    with Phase("mod") as ctx:
        s = semaphores(nc, ctx, ["small", "w0", "w1", "x0", "x1", "x2", "x3", "late", "ones", "silu", "used", "summed", "rows_part", "rows", "columns",
                                 "stored", "sq", "var", "sd", "rstd", "scaled", "turned", "kept"])
        w = sb(nc, ctx, "ada_tile", [P, 2, 6 * D])
        acc = sb(nc, ctx, "ada_acc", [P, 6 * D])
        cc = sb(nc, ctx, "c_cols", [P, KD])
        b_col = sb(nc, ctx, "ada_b_cols", [P, 2 * KD])
        g_col = sb(nc, ctx, "norm_g_cols", [P, KD])
        xt = sb(nc, ctx, "x_tile", [P, G, D])
        junk = sb(nc, ctx, "square", [P, D])
        stat = sb(nc, ctx, "stat", [P, G, 4])
        wc = sb(nc, ctx, "norm_cols", [P, KD])
        b_row, g_row, rows = w[0:1, 0, 0:4 * D], w[0:1, 0, 4 * D:5 * D], w[0:1, 1, 0:4 * D]
        bank = k.bank
        w_in, x_in = (s["w0"], s["w1"]), (s["x0"], s["x1"], s["x2"], s["x3"])
        at = lambda n: bass.ds(n * P, P)
        with nc.Block() as block:
            @block.sync
            def _(sp):
                for n in range(2):
                    sp.dma_start(xt[:, n, :], x[0, at(n), :]).then_inc(x_in[n], 16)
                sp.dma_start(k.mask_sb[:], k.mask_in).then_inc(s["small"], 16)
                sp.dma_start(cc[:], c_col).then_inc(s["small"], 16)
                sp.dma_start(b_col[:], ada_b_col).then_inc(s["small"], 16)
                sp.dma_start(g_col[:], norm_g_col).then_inc(s["small"], 16)
                sp.dma_start(wc[:], norm_w_col).then_inc(s["small"], 16)
                for half in range(2):
                    sp.dma_start(w[:, half, :], ada_w[at(half), :]).then_inc(w_in[half], 16)
                    if half == 0:
                        for n in range(2, G):
                            sp.dma_start(xt[:, n, :], x[0, at(n), :]).then_inc(x_in[n], 16)
                with sp.Fori(0, TURNS - 1) as g:
                    for half in range(2):
                        for n in (2 * half, 2 * half + 1):
                            sp.wait_ge(s["turned"], g * (2 * G) + 2 * n + 2)
                            sp.dma_start(xt[:, n, :], x[0, at(g * G + (n + G)), :]).then_inc(x_in[n], 16)
                        sp.wait_ge(s["used"], g * 2 + half + 1)
                        sp.dma_start(w[:, half, :], ada_w[at(g * 2 + (half + 2)), :]).then_inc(w_in[half], 16)
                sp.wait_ge(s["used"], KD)
                sp.dma_start(b_row, ada_b[:, 2 * D:]).then_inc(s["late"], 16)
                sp.dma_start(g_row, norm_g[1:2, :]).then_inc(s["late"], 16)
                sp.wait_ge(s["rows"], 6)
                sp.dma_start(k.rows_dram.rearrange("(a r) d -> a (r d)", a=1), rows).then_inc(s["stored"], 16)
                sp.wait_ge(s["stored"], 16)

            @block.scalar
            def _(act):
                act.wait_ge(s["small"], 80)
                nc.scalar.activation(cc[:], cc[:], ACT.Silu).then_inc(s["silu"], 1)

                def turn(g):
                    for n in range(G):
                        t = g * G + n
                        act.wait_ge(x_in[n], g * 16 + 16)
                        wait_for(act, s["sq"], t)
                        nc.scalar.activation(junk[:], xt[:, n, :], ACT.Square, accum_out=stat[:, n, 0:1]).then_inc(s["sq"], 1)
                        act.wait_ge(s["var"], t + 1)
                        nc.scalar.activation(stat[:, n, 2:3], stat[:, n, 1:2], ACT.Sqrt).then_inc(s["sd"], 1)
                turn(0)
                with act.Fori(1, TURNS) as g:
                    turn(g)

            @block.vector
            def _(dve):
                def keep(t, n):
                    for b in range(2):
                        dve.wait_ge(s["turned"], 2 * t + b + 1)
                        nc.vector.tensor_tensor(hT[:, 4 * b:4 * b + 4, at(t)], bank[2 * (n % 2) + b][:].rearrange("p (k t) -> p k t", t=P),
                                                wc[:, 4 * b:4 * b + 4].unsqueeze(2).to_broadcast([P, 4, P]), ALU.mult).then_inc(s["kept"], 1)

                def turn(g, first):
                    for n in range(G):
                        t = g * G + n
                        dve.wait_ge(s["sq"], t + 1)
                        nc.vector.tensor_scalar(stat[:, n, 1:2], stat[:, n, 0:1], 1.0 / D, EPS, ALU.mult, ALU.add).then_inc(s["var"], 1)
                        dve.wait_ge(s["sd"], t + 1)
                        nc.vector.reciprocal(stat[:, n, 3:4], stat[:, n, 2:3]).then_inc(s["rstd"], 1)
                        dve.wait_ge(s["rstd"], t + 1)
                        nc.vector.tensor_scalar(xt[:, n, :], xt[:, n, :], stat[:, n, 3:4], None, ALU.mult).then_inc(s["scaled"], 1)
                        if n or not first:
                            keep(t - 1, n - 1)
                        if n % 2:
                            half = n // 2
                            dve.wait_ge(w_in[half], g * 16 + 16)
                            if first and half == 0:
                                dve.wait_ge(s["silu"], 1)
                                nc.vector.tensor_scalar(acc[:], w[:, 0, :], cc[:, 0:1], None, ALU.mult).then_inc(s["used"], 1)
                            else:
                                dve.wait_ge(s["used"], g * 2 + half)
                                nc.vector.scalar_tensor_tensor(acc[:], w[:, half, :], cc[:, bass.ds(g * 2 + half, 1)], acc[:],
                                                               ALU.mult, ALU.add).then_inc(s["used"], 1)
                nc.vector.memset(k.ones[:], 1.0).then_inc(s["ones"], 1)
                dve.wait_ge(s["small"], 80)
                turn(0, True)
                with dve.Fori(1, TURNS) as g:
                    turn(g, False)
                keep(TT - 1, G - 1)
                go = Line(dve, s["columns"])
                dve.wait_ge(s["summed"], 1)
                go(nc.vector.tensor_tensor(k.shift1[:], bank[7][:, 0:KD], b_col[:, 0:KD], ALU.add))
                go(nc.vector.tensor_tensor(k.gain1[:], bank[7][:, KD:2 * KD], b_col[:, KD:2 * KD], ALU.add))
                go(nc.vector.tensor_scalar_add(k.gain1[:], k.gain1[:], 1.0))
                go(nc.vector.tensor_tensor(k.gain1[:], k.gain1[:], g_col[:], ALU.mult))
                dve.wait_ge(s["late"], 32)
                for n in range(4):
                    dve.wait_ge(s["summed"], 2 if n < 2 else 3)
                    for h in range(2):
                        o = n * D + h * 512
                        ins = nc.vector.tensor_tensor(rows[:, o:o + 512], bank[(2 * n + h) % 4][0:1, :], b_row[:, o:o + 512], ALU.add)
                        go(ins, s["rows"] if h else s["rows_part"])
                go(nc.vector.tensor_scalar_add(rows[:, 2 * D:3 * D], rows[:, 2 * D:3 * D], 1.0), s["rows"])
                go(nc.vector.tensor_tensor(rows[:, 2 * D:3 * D], rows[:, 2 * D:3 * D], g_row, ALU.mult), s["rows"])

            @block.tensor
            def _(pe):
                pe.wait_ge(s["small"], 80)

                def turn(g):
                    for n in range(G):
                        t = g * G + n
                        pe.wait_ge(s["scaled"], t + 1)
                        wait_for(pe, s["kept"], 2 * t - 2)
                        for b in range(2):
                            for j in range(4):
                                kb = 4 * b + j
                                mm = nc.tensor.transpose(bank[2 * (n % 2) + b][:, j * P:(j + 1) * P], xt[:, n, kb * P:(kb + 1) * P], k.ident[:])
                            mm.then_inc(s["turned"], 1)
                turn(0)
                with pe.Fori(1, TURNS) as g:
                    turn(g)
                pe.wait_ge(s["ones"], 1)
                pe.wait_ge(s["used"], KD)
                for j in range(2 * KD):
                    mm = nc.tensor.matmul(bank[7][:, j:j + 1], acc[:, j * P:(j + 1) * P], k.ones[:, 0:1], start=True, stop=True)
                mm.then_inc(s["summed"], 1)
                pe.wait_ge(s["kept"], 2 * TT)
                for n in range(8):
                    if n == 4:
                        pe.wait_ge(s["rows"], 2)
                    o = 2 * D + n * 512
                    mm = nc.tensor.matmul(bank[n % 4][0:1, :], k.ones[:, 0:1], acc[:, o:o + 512], start=True, stop=True)
                    if n % 4 == 3:
                        mm.then_inc(s["summed"], 1)
        meet(nc, s)


def rwkv(nc, k, hT, w_in, w_up, a_up, cols, mu_lora_col, mT):
    HP = 4
    wv = w_in.rearrange("(kb p) n -> p kb n", p=P)
    with Phase("heads") as outer:
        lora = sb(nc, outer, "lora", [P, T])
        with Phase("lr") as ctx:
            s = semaphores(nc, ctx, ["w", "mu", "u", "chain_v", "chain_a", "raw", "mixed"])
            w = sb(nc, ctx, "lora_w", [P, KD, P])
            raw = sb(nc, ctx, "lora_raw", [P, T + 1])
            mu = sb(nc, ctx, "lora_mu", [P, 1])
            diff = sb(nc, ctx, "lora_diff", [P, T])
            bank = k.bank
            with nc.Block() as block:
                @block.sync
                def _(sp):
                    sp.dma_start(w[:], wv[:, :, RW_L:RW_L + P]).then_inc(s["w"], 16)
                    sp.dma_start(mu[:], mu_lora_col).then_inc(s["mu"], 16)

                @block.tensor
                def _(pe):
                    pe.wait_ge(s["w"], 16)
                    for q in range(Q):
                        for kb in range(KD):
                            mm = nc.tensor.matmul(bank[q][:], w[:, kb, :], hT[:, kb, q * QT:(q + 1) * QT],
                                                  start=(kb == 0), stop=(kb == KD - 1))
                        mm.then_inc(s["u"], 1)

                @block.scalar
                def _(act):
                    go = Line(act, s["chain_a"])
                    for q in range(Q):
                        act.wait_ge(s["u"], q + 1)
                        go(nc.scalar.activation(raw[:, 1 + q * QT:1 + (q + 1) * QT], bank[q][:], ACT.Copy), s["raw"])
                    act.wait_ge(s["mixed"], 1)
                    go(nc.scalar.activation(lora[0:64, :], lora[0:64, :], ACT.Tanh))

                @block.vector
                def _(dve):
                    go = Line(dve, s["chain_v"])
                    go(nc.vector.memset(raw[:, 0:1], 0.0))
                    dve.wait_ge(s["raw"], Q)
                    dve.wait_ge(s["mu"], 16)
                    go(nc.vector.tensor_tensor(diff[:], raw[:, 0:T], raw[:, 1:T + 1], ALU.subtract))
                    go(nc.vector.scalar_tensor_tensor(lora[:], diff[:], mu[:, 0:1], raw[:, 1:T + 1], ALU.mult, ALU.add), s["mixed"])
            meet(nc, s)

        with Phase("rw") as ctx:
            s = semaphores(nc, ctx, [
                "w0", "w1", "w2", "w3", "par", "lup", "u", "wa", "ssq", "bon", "chain_v", "chain_a", "chain_g",
                "raw", "raw_read", "gate", "sig", "cum", "exps", "inv", "kk", "kk_sq", "sqrt", "forms", "rk",
                "tr", "tr_kept", "sc", "sc_kept", "nt", "a", "t", "t_turned", "e", "e_kept", "dt", "x", "x_kept", "wu", "wu_kept",
                "q", "q_kept", "gh", "gh_kept", "state_mm", "state", "y", "y_kept", "yvar", "ysd", "ynorm",
                "yt", "out", "stored"])
            w1_stored = ctx.enter_context(nc.semaphore("rw_w1_and_stored"))
            wt = [sb(nc, ctx, f"w_block{i}", [P, KD, P]) for i in range(2)]
            lup = sb(nc, ctx, "lora_up", [P, P])
            par = sb(nc, ctx, "head_params", [P, 12])
            raws = [sb(nc, ctx, f"raw{i}", [P, T + 1]) for i in range(2)]
            KT, BB = raws[0][:, 0:T], raws[1][:, 0:T]
            r, kx, v, sg, sw, a, cs = [sb(nc, ctx, n, [P, T]) for n in ("r", "kx", "v", "sg", "sw", "a", "cs")]
            PR = sb(nc, ctx, "PR", [P, TT, 2, P])
            Pc, Rc = PR[:, :, 0, :], PR[:, :, 1, :]
            tmp = sb(nc, ctx, "tmp", [P, T])
            Y = tmp[:].rearrange("p (j n) -> p j n", n=P)
            lc = sb(nc, ctx, "chunk_decay", [P, NCH])
            scm = [x[:].rearrange("p (q n t) -> p q n t", q=4, n=4) for x in (a, cs)]
            tt = [kx[:, i * 1024:(i + 1) * 1024].rearrange("p (q n t) -> p q n t", q=4, n=2) for i in range(2)]
            ptm = [r[:, i * 768:(i + 1) * 768].rearrange("p (j n t) -> p j n t", j=2, n=3) for i in range(2)]
            eb = r[:, 1536:2048].rearrange("p (q t) -> p q t", q=4)
            px = sb(nc, ctx, "PX", [P, 2, 4, P])
            wun = sb(nc, ctx, "WU", [P, 2, 2, P])
            qp = sb(nc, ctx, "Qp", [P, 2, P])
            gt = sb(nc, ctx, "GT", [P, 2, 2, P])
            hh = sb(nc, ctx, "H", [P, 2, 2, P])
            nt = sb(nc, ctx, "levels", [P, 2, 4, P])
            M = sb(nc, ctx, "state", [P, P])
            gst = sb(nc, ctx, "group_stat", [P, 3, 2 * TT])
            bank = k.bank
            mk = k.mask
            NB = TT // 2
            c3 = lambda ap: ap.rearrange("p (n c) -> p n c", c=P)
            heads2 = [slice(0, 64), slice(64, 128)]
            with nc.Fori(0, HP) as hp:
                with nc.Block() as block:
                    firsts = (RW_K, RW_R, RW_V, RW_G)

                    @block.sync
                    def _(sp):
                        sp.dma_start(lup[0:64, :], w_up[:, bass.ds(hp * P, P)]).then_inc(s["lup"], 16)
                        sp.dma_start(lup[64:128, :], a_up[:, bass.ds(hp * P, P)]).then_inc(s["lup"], 16)
                        for i, at in enumerate(firsts):
                            if i == 1:
                                sp.dma_start(par[:], cols[hp]).then_inc(s["par"], 16)
                            if i >= 2:
                                sp.wait_ge(s["u"], Q * (i - 1))
                            sp.dma_start(wt[i % 2][:], wv[:, :, bass.ds(hp * P + at, P)]).then_inc(w1_stored if i == 1 else s[f"w{i}"], 16)
                        sp.wait_ge(s["out"], Q)
                        sp.dma_start(mT[hp + 4], tmp[:]).then_inc(w1_stored, 16)

                    @block.tensor
                    def _(pe):
                        pe.wait_ge(s["lup"], 32)
                        for i in range(2):
                            for q in range(Q):
                                nc.tensor.matmul(bank[4 * i + q][:], lup[64 * i:64 * i + 64, :],
                                                 lora[64 * i:64 * i + 64, q * QT:(q + 1) * QT], start=True, stop=True).then_inc(s["wa"], 1)

                        def block_of_u(i, first_bank, freed, count, quarters=range(Q)):
                            if i == 1:
                                pe.wait_ge(w1_stored, hp * 32 + 16)
                            else:
                                pe.wait_ge(s[f"w{i}"], 16)
                            for q in quarters:
                                pe.wait_ge(s[freed], count + q + 1)
                                for kb in range(KD):
                                    mm = nc.tensor.matmul(bank[first_bank + q][:], wt[i % 2][:, kb, :],
                                                          hT[:, kb, q * QT:(q + 1) * QT], start=(kb == 0), stop=(kb == KD - 1))
                                mm.then_inc(s["u"], 1)
                        block_of_u(0, 0, "sig", 0)
                        block_of_u(1, 4, "sig", Q)
                        pe.wait_ge(s["kk_sq"], 1)
                        for q in range(Q):
                            nc.tensor.matmul(bank[q][:], k.mask("head_ones"), v[:, q * QT:(q + 1) * QT], start=True, stop=True).then_inc(s["ssq"], 1)
                        block_of_u(2, 0, "sqrt", 0)
                        block_of_u(3, 4, "raw", Q, (0, 1))
                        pe.wait_ge(s["rk"], 1)
                        pe.wait_ge(s["raw"], 3 * Q)
                        for q in range(Q):
                            nc.tensor.matmul(bank[q][:], k.mask("head_ones"), tmp[:, q * QT:(q + 1) * QT], start=True, stop=True).then_inc(s["bon"], 1)
                        pe.wait_ge(s["forms"], 1)
                        pe.wait_ge(s["gate"], 2)

                        def turn(j):
                            for n, src in enumerate((Pc[:, j, :], BB[:, j * P:(j + 1) * P], KT[:, j * P:(j + 1) * P], v[:, j * P:(j + 1) * P])):
                                mm = nc.tensor.transpose(bank[0][:, n * P:(n + 1) * P], src, k.ident[:])
                            mm.then_inc(s["tr"], 1)

                        def scores(j):
                            ts = slice(j * P, (j + 1) * P)
                            for h, hs in enumerate(heads2):
                                q = 2 * j + h
                                if q >= 2:
                                    pe.wait_ge(s["sc_kept"], q - 1)
                                rhs = PR[hs, j, :, :].rearrange("p a t -> p (a t)")
                                nc.tensor.matmul(bank[1 + h][:, 0:256], BB[hs, ts], rhs, start=True, stop=True)
                                nc.tensor.matmul(bank[1 + h][:, 256:512], KT[hs, ts], rhs, start=True, stop=True).then_inc(s["sc"], 1)
                            for h, hs in enumerate(heads2):
                                o = (j % 2) * P
                                mm = nc.tensor.matmul(bank[6 + h][:, o:o + P], Pc[hs, j, :], BB[hs, ts], start=True, stop=True)
                            if j % 2:
                                mm.then_inc(s["a"], 1)

                        def g_and_h(b, jj):
                            tm = ptm[b % 2]
                            for c, cr in enumerate(heads2):
                                nc.tensor.matmul(bank[1 + c][:, 0:P], wun[cr, jj, 0, :], tm[cr, jj, 0, :], start=True, stop=True)
                            for c, cr in enumerate(heads2):
                                nc.tensor.matmul(bank[1 + c][:, P:2 * P], tm[cr, jj, 1, :], tm[cr, jj, 2, :], start=True, stop=False)
                                mm = nc.tensor.matmul(bank[1 + c][:, P:2 * P], tm[cr, jj, 0, :], wun[cr, jj, 1, :], start=False, stop=True)
                            mm.then_inc(s["gh"], 1)

                        def y_inside(b, jj):
                            if jj:
                                pe.wait_ge(s["y_kept"], 2 * b + 1)
                            for h, hs in enumerate(heads2):
                                p = 2 * jj + h
                                nc.tensor.matmul(bank[0][:, hs], scm[b % 2][:, p, 3, :], ptm[b % 2][:, jj, 2, hs], start=(h == 0), stop=False, skip_group_check=True)
                                nc.tensor.matmul(bank[0][:, hs], scm[b % 2][:, p, 1, :], wun[:, jj, 1, hs], start=False, stop=False, skip_group_check=True)

                        def chunk(b, jj, c):
                            n, cr = 4 * b + 2 * jj + c, heads2[c]
                            pe.wait_ge(s["state"], n + 1)
                            mm = nc.tensor.matmul(bank[0][cr, 0:P], qp[:, jj, cr], M[:], start=False, stop=True, skip_group_check=True)
                            if c:
                                mm.then_inc(s["y"], 1)
                            nc.tensor.matmul(bank[7][:, 0:P], gt[:, jj, c, :], M[:], start=True, stop=True).then_inc(s["state_mm"], 1)

                        def beside(g, slot):
                            b, f = g - 1, g + 1
                            if b >= 0:
                                if slot == 0:
                                    for p in range(4):
                                        mm = nc.tensor.matmul(bank[6][:, p * 64:(p + 1) * 64], scm[b % 2][:, p, 2, :],
                                                              ptm[b % 2][:, p // 2, 2, heads2[p % 2]], start=True, stop=True)
                                    mm.then_inc(s["x"], 1)
                                elif slot == 1:
                                    pe.wait_ge(s["x_kept"], b + 1)
                                    pe.wait_ge(s["t"], g * (LEVELS + 1))
                                    for p in range(4):
                                        mm = nc.tensor.matmul(bank[6][:, p * P:(p + 1) * P], tt[b % 2][:, p, 1, :], px[:, b % 2, p, :], start=True, stop=True)
                                    mm.then_inc(s["wu"], 1)
                                elif slot == 2:
                                    pe.wait_ge(s["wu_kept"], 2 * g)
                                    for p in range(4):
                                        jj, h = p // 2, p % 2
                                        mm = nc.tensor.matmul(bank[6][heads2[h], jj * P:(jj + 1) * P],
                                                              wun[:, jj, 0, heads2[h]], scm[b % 2][:, p, 1, :], start=True, stop=True)
                                    mm.then_inc(s["q"], 1)
                                elif slot == 3:
                                    g_and_h(b, 0)
                                elif slot == 4:
                                    y_inside(b, 0)
                                    pe.wait_ge(s["q_kept"], b + 1)
                                    pe.wait_ge(s["gh_kept"], 2 * b + 1)
                                    chunk(b, 0, 0)
                                    g_and_h(b, 1)
                                elif slot == 5:
                                    chunk(b, 0, 1)
                                elif slot == 6:
                                    y_inside(b, 1)
                                    pe.wait_ge(s["gh_kept"], 2 * b + 2)
                                    chunk(b, 1, 0)
                                elif slot == 7:
                                    chunk(b, 1, 1)
                            if 0 <= f < NB:
                                if slot == 7:
                                    if b >= 0:
                                        pe.wait_ge(s["y_kept"], 2 * g)
                                    turn(2 * f)
                                elif slot == 8:
                                    if b >= 0:
                                        pe.wait_ge(s["state"], 4 * g + 1)
                                    scores(2 * f)
                                    pe.wait_ge(s["tr_kept"], 2 * f + 1)
                                    turn(2 * f + 1)
                                elif slot == 9:
                                    scores(2 * f + 1)

                        for slot in (7, 8, 9):
                            beside(-1, slot)
                        pe.wait_ge(s["tr_kept"], 2)
                        for g in range(NB + 1):
                            for l in range(LEVELS):
                                if g < NB:
                                    n = g * LEVELS + l
                                    inv = tt[g % 2]
                                    pe.wait_ge(s["t"], g * (LEVELS + 1) + l + 1)
                                    pe.wait_ge(s["nt"], n + 1)
                                    for p in range(4):
                                        mm = nc.tensor.matmul(bank[3][:, p * P:(p + 1) * P], nt[:, n % 2, p, :], inv[:, p, 0, :], start=True, stop=True)
                                    mm.then_inc(s["e"], 1)
                                beside(g, 2 * l)
                                if g < NB:
                                    pe.wait_ge(s["e_kept"], n + 1)
                                    if l == 0:
                                        pe.wait_ge(s["t_turned"], g + 1)
                                    for p in range(4):
                                        b, o = bank[4 + p // 2], 256 * (p % 2)
                                        if l < LEVELS - 1:
                                            nc.tensor.matmul(b[:, o:o + P], inv[:, p, 1, :], eb[:, p, :], start=True, stop=True)
                                        mm = nc.tensor.matmul(b[:, o + P:o + 2 * P], eb[:, p, :], inv[:, p, 1, :], start=True, stop=True)
                                        if p % 2:
                                            mm.then_inc(s["dt"], 1)
                                beside(g, 2 * l + 1)
                        pe.wait_ge(s["state"], NCH + 1)
                        pe.wait_ge(s["q_kept"], NB)
                        block_of_u(3, 4, "raw", Q, (2, 3))
                        pe.wait_ge(s["ynorm"], 1)
                        for q in range(Q):
                            for j in range(4):
                                mm = nc.tensor.transpose(bank[q][:, j * P:(j + 1) * P], Y[:, 4 * q + j, :], k.ident[:])
                            mm.then_inc(s["yt"], 1)

                    @block.scalar
                    def _(act):
                        go = Line(act, s["chain_a"])
                        act.wait_ge(s["par"], 16)
                        for i, (dst, bias) in enumerate(((sw, 3), (a, 4))):
                            for q in range(Q):
                                act.wait_ge(s["wa"], Q * i + q + 1)
                                go(nc.scalar.activation(dst[:, q * QT:(q + 1) * QT], bank[4 * i + q][:], ACT.Sigmoid, bias=par[:, bias:bias + 1]), s["sig"])

                        def keep_raw(i):
                            for q in range(Q):
                                act.wait_ge(s["u"], Q * i + q + 1)
                                go(nc.scalar.activation(raws[i % 2][:, 1 + q * QT:1 + (q + 1) * QT], bank[4 * (i % 2) + q][:], ACT.Copy), s["raw"])
                        act.wait_ge(s["cum"], 1)
                        go(nc.scalar.activation(Rc, cs[:].rearrange("p (j t) -> p j t", t=P), ACT.Exp, scale=-DECAY))
                        act.wait_ge(s["cum"], 2)
                        go(nc.scalar.activation(Pc, Pc, ACT.Exp, scale=-DECAY), s["exps"])
                        keep_raw(0)
                        act.wait_ge(s["kk"], 1)
                        go(nc.scalar.activation(v[:], tmp[:], ACT.Square), s["kk_sq"])
                        keep_raw(1)
                        for q in range(Q):
                            act.wait_ge(s["ssq"], q + 1)
                            go(nc.scalar.activation(v[:, q * QT:(q + 1) * QT], bank[q][:], ACT.Sqrt), s["sqrt"])
                        act.wait_ge(s["raw_read"], 1)
                        keep_raw(2)
                        act.wait_ge(s["raw_read"], 3)
                        go(nc.scalar.activation(KT, cs[:], ACT.Exp, scale=DECAY), s["inv"])

                        def keep_gate(quarters):
                            for q in quarters:
                                act.wait_ge(s["u"], 3 * Q + q + 1)
                                go(nc.scalar.activation(sg[:, q * QT:(q + 1) * QT], bank[4 + q][:], ACT.Silu), s["gate"])
                        keep_gate((0, 1))

                        def beside(g, slot):
                            b = g - 1
                            if b < 0:
                                return
                            if slot == 0:
                                act.wait_ge(s["x"], b + 1)
                                go(nc.scalar.activation(px[:, b % 2, :, 64:128], bank[6][:, 0:256].rearrange("p (n c) -> p n c", c=64), ACT.Copy), s["x_kept"])
                            elif slot == 1:
                                act.wait_ge(s["wu"], b + 1)
                                for jj in range(2):
                                    src = bank[6][:, jj * 256:(jj + 1) * 256].rearrange("p (h u c) -> p u h c", h=2, u=2)
                                    go(nc.scalar.activation(wun[:, jj, :, :].rearrange("p u (h c) -> p u h c", h=2), src, ACT.Copy, scale=-1.0), s["wu_kept"])
                            elif slot in (5, 7):
                                j = 2 * b + (slot - 5) // 2
                                act.wait_ge(s["y"], j + 1)
                                go(nc.scalar.activation(Y[:, j, :], bank[0][:, 0:P], ACT.Copy), s["y_kept"])
                        for g in range(NB + 1):
                            for l in range(LEVELS):
                                if g < NB:
                                    act.wait_ge(s["e"], g * LEVELS + l + 1)
                                    go(nc.scalar.activation(eb, c3(bank[3][:]), ACT.Copy), s["e_kept"])
                                beside(g, 2 * l)
                                beside(g, 2 * l + 1)
                        act.wait_ge(s["yvar"], 1)
                        go(nc.scalar.activation(gst[:, 2, :], gst[:, 1, :], ACT.Sqrt), s["ysd"])
                        keep_gate((2, 3))

                    @block.vector
                    def _(dve):
                        go = Line(dve, s["chain_v"])
                        t3 = lambda ap: ap.rearrange("p (j t) -> p j t", t=P)
                        for i in range(2):
                            go(nc.vector.memset(raws[i][:, 0:1], 0.0))
                        go(nc.vector.memset(M[:], 0.0), s["state"])
                        dve.wait_ge(s["sig"], Q)
                        for n in range(NCH):
                            ins = nc.vector.tensor_tensor_scan(cs[:, n * C:(n + 1) * C], k.chunk_ones[:], sw[:, n * C:(n + 1) * C], 0.0, ALU.mult, ALU.add)
                        go(ins, s["cum"])
                        go(nc.vector.tensor_tensor(Pc, t3(cs[:]), t3(sw[:]), ALU.subtract), s["cum"])
                        dve.wait_ge(s["par"], 16)

                        def mix(i, dst, mu):
                            dve.wait_ge(s["raw"], Q * (i + 1))
                            raw = raws[i % 2]
                            go(nc.vector.tensor_tensor(dst[:], raw[:, 0:T], raw[:, 1:T + 1], ALU.subtract))
                            go(nc.vector.scalar_tensor_tensor(dst[:], dst[:], par[:, mu:mu + 1], raw[:, 1:T + 1], ALU.mult, ALU.add),
                               s["raw_read"])
                        mix(0, kx, 1)
                        dve.wait_ge(w1_stored, hp * 32 + 16)
                        go(nc.vector.tensor_scalar(tmp[:], kx[:], par[:, 5:6], None, ALU.mult), s["kk"])
                        mix(1, r, 0)
                        dve.wait_ge(s["exps"], 1)
                        go(nc.vector.tensor_copy(lc[:], PR[:, :, 1, :].rearrange("p j (c t) -> p j c t", c=2)[:, :, :, C - 1]))
                        go(nc.vector.tensor_tensor(Rc, Rc, t3(r[:]), ALU.mult))
                        dve.wait_ge(s["sqrt"], Q)
                        go(nc.vector.tensor_scalar_max(v[:], v[:], 1e-12))
                        go(nc.vector.reciprocal(v[:], v[:]))
                        go(nc.vector.tensor_tensor(tmp[:], tmp[:], v[:], ALU.mult))
                        go(nc.vector.tensor_tensor(Pc, Pc, t3(tmp[:]), ALU.mult))
                        dve.wait_ge(s["sig"], 2 * Q)
                        go(nc.vector.tensor_tensor(BB, tmp[:], a[:], ALU.mult))
                        go(nc.vector.tensor_scalar(a[:], a[:], -1.0, par[:, 6:7], ALU.add, ALU.mult))
                        go(nc.vector.scalar_tensor_tensor(kx[:], a[:], 1.0, kx[:], ALU.add, ALU.mult))
                        go(nc.vector.scalar_tensor_tensor(tmp[:], r[:], par[:, 7:8], kx[:], ALU.mult, ALU.mult), s["rk"])
                        mix(2, v, 2)
                        dve.wait_ge(s["inv"], 1)
                        go(nc.vector.tensor_tensor(BB, BB, KT, ALU.mult))
                        go(nc.vector.tensor_tensor(KT, KT, kx[:], ALU.mult))
                        for q in range(Q):
                            dve.wait_ge(s["bon"], q + 1)
                            ins = nc.vector.tensor_tensor(sw[:, q * QT:(q + 1) * QT], bank[q][:], v[:, q * QT:(q + 1) * QT], ALU.mult)
                            go(ins, s["forms"] if q == Q - 1 else None)
                        go(nc.vector.tensor_scalar(sw[:], sw[:], par[:, 9:10], None, ALU.add))

                        def keep_turned(j):
                            dve.wait_ge(s["tr"], j + 1)
                            par2 = (j // 2) % 2
                            go(nc.vector.tensor_copy(ptm[par2][:, j % 2, :, :], c3(bank[0][:, P:512])))
                            go(nc.vector.tensor_copy(px[:, par2, 2 * (j % 2):2 * (j % 2) + 2, 0:64], bank[0][:, 0:P].rearrange("p (h c) -> p h c", h=2)), s["tr_kept"])

                        def keep_scores(j):
                            for h in range(2):
                                dve.wait_ge(s["sc"], 2 * j + h + 1)
                                go(nc.vector.tensor_tensor(scm[(j // 2) % 2][:, 2 * (j % 2) + h, :, :], c3(bank[1 + h][:]), c3(mk("scores")), ALU.mult), s["sc_kept"])

                        def blocks_of_two(f):
                            inv = tt[f % 2]
                            n1t = mk("corner_t").unsqueeze(1).to_broadcast([P, 4, P])
                            one = k.ident[:].unsqueeze(1).to_broadcast([P, 4, P])
                            dve.wait_ge(s["a"], f + 1)
                            for h in range(2):
                                go(nc.vector.tensor_tensor(inv[:, h::2, 0, :], c3(bank[6 + h][:, 0:256]), mk("corner").unsqueeze(1).to_broadcast([P, 2, P]), ALU.mult))
                            go(nc.vector.tensor_tensor(inv[:, :, 0, :], inv[:, :, 0, :], one, ALU.add), s["t"])
                            go(nc.vector.tensor_tensor(inv[:, :, 1, :], scm[f % 2][:, :, 0, :], n1t, ALU.mult))
                            go(nc.vector.tensor_tensor(inv[:, :, 1, :], inv[:, :, 1, :], one, ALU.add), s["t_turned"])

                        def keep_g_and_h(b, jj):
                            j = 2 * b + jj
                            dve.wait_ge(s["gh"], j + 1)
                            for c in range(2):
                                n = 2 * j + c
                                go(nc.vector.tensor_tensor(gt[:, jj, c], bank[1 + c][:, 0:P], k.ident[:], ALU.add))
                                go(nc.vector.scalar_tensor_tensor(hh[:, jj, c, :], bank[1 + c][:, P:2 * P], lc[:, n:n + 1], mk("heads"), ALU.mult, ALU.mult))
                            go(nc.vector.tensor_tensor(gt[:, jj], gt[:, jj], mk("heads").unsqueeze(1).to_broadcast([P, 2, P]), ALU.mult), s["gh_kept"])

                        def chunk(b, jj, c):
                            n = 4 * b + 2 * jj + c
                            dve.wait_ge(s["state_mm"], n + 1)
                            go(nc.vector.scalar_tensor_tensor(M[:], bank[7][:, 0:P], lc[:, n:n + 1], hh[:, jj, c, :], ALU.mult, ALU.add), s["state"])

                        def beside(g, slot):
                            b, f = g - 1, g + 1
                            if b >= 0:
                                if slot == 2:
                                    dve.wait_ge(s["q"], b + 1)
                                    go(nc.vector.tensor_tensor(qp[:], c3(bank[6][:, 0:256]), PR[:, 2 * b:2 * b + 2, 1, :], ALU.add), s["q_kept"])
                                elif slot == 3:
                                    keep_g_and_h(b, 0)
                                elif slot == 4:
                                    chunk(b, 0, 0)
                                    keep_g_and_h(b, 1)
                                elif slot == 5:
                                    chunk(b, 0, 1)
                                elif slot == 6:
                                    chunk(b, 1, 0)
                                elif slot == 7:
                                    chunk(b, 1, 1)
                            if 0 <= f < NB:
                                if slot == 7:
                                    keep_turned(2 * f)
                                elif slot == 8:
                                    keep_scores(2 * f)
                                    keep_turned(2 * f + 1)
                                elif slot == 9:
                                    keep_scores(2 * f + 1)
                                    blocks_of_two(f)
                        for slot in (7, 8, 9):
                            beside(-1, slot)
                        for g in range(NB + 1):
                            for l in range(LEVELS):
                                beside(g, 2 * l)
                                if g < NB:
                                    inv = tt[g % 2]
                                    for b in range(2):
                                        dve.wait_ge(s["dt"], 2 * (g * LEVELS + l) + b + 1)
                                        which = slice(1 if l == LEVELS - 1 else 0, 2)
                                        dst = inv[:, 2 * b:2 * b + 2, which, :]
                                        src = bank[4 + b][:].rearrange("p (n a t) -> p n a t", n=2, a=2)[:, :, which, :]
                                        go(nc.vector.tensor_tensor(dst, dst, src, ALU.add), s["t"] if b else None)
                                beside(g, 2 * l + 1)
                        dve.wait_ge(s["y_kept"], TT)
                        Yg = tmp[:].rearrange("p (g n) -> p g n", n=64)
                        KTg = KT.rearrange("p (g n) -> p g n", n=64)
                        NG = 2 * TT
                        bc = lambda i: gst[:, i, :].unsqueeze(2).to_broadcast([P, NG, 64])
                        go(nc.vector.tensor_reduce(gst[:, 0, :], Yg, AX.X, ALU.add))
                        go(nc.vector.tensor_scalar(gst[:, 0, :], gst[:, 0, :], 1.0 / 64, None, ALU.mult))
                        go(nc.vector.tensor_tensor(Yg, Yg, bc(0), ALU.subtract))
                        go(nc.vector.tensor_tensor(KT, tmp[:], tmp[:], ALU.mult))
                        go(nc.vector.tensor_reduce(gst[:, 1, :], KTg, AX.X, ALU.add))
                        go(nc.vector.tensor_scalar(gst[:, 1, :], gst[:, 1, :], 1.0 / 64, 64e-5, ALU.mult, ALU.add), s["yvar"])
                        dve.wait_ge(s["ysd"], 1)
                        go(nc.vector.reciprocal(gst[:, 0, :], gst[:, 2, :]))
                        go(nc.vector.tensor_tensor(Yg, Yg, bc(0), ALU.mult), s["ynorm"])
                        dve.wait_ge(s["gate"], Q)
                        for q in range(Q):
                            qs = slice(q * QT, (q + 1) * QT)
                            dve.wait_ge(s["yt"], q + 1)
                            go(nc.vector.scalar_tensor_tensor(tmp[:, qs], bank[q][:], par[:, 8:9], sw[:, qs], ALU.mult, ALU.add))
                            go(nc.vector.tensor_tensor(tmp[:, qs], tmp[:, qs], sg[:, qs], ALU.mult), s["out"])

                    @block.gpsimd
                    def _(pool):
                        go = Line(pool, s["chain_g"])
                        lm = mk("levels").rearrange("p (l t) -> p l t", t=P)
                        for g in range(NB):
                            for l in range(LEVELS):
                                n = g * LEVELS + l
                                if l == 0:
                                    pool.wait_ge(s["sc_kept"], 4 * (g + 1))
                                if n >= 2:
                                    pool.wait_ge(s["e"], n - 1)
                                go(nc.gpsimd.tensor_tensor(nt[:, n % 2, :, :], scm[g % 2][:, :, 0, :], lm[:, l, :].unsqueeze(1).to_broadcast([P, 4, P]), ALU.mult), s["nt"])
                meet(nc, s)
            with nc.Block() as block:
                @block.sync
                def _(sp):
                    sp.wait_ge(w1_stored, HP * 32)
            nc.all_engine_barrier()


def gla(nc, k, hT, w_in, gate_up, gate_bias_col, norm_col, mT):
    wv = w_in.rearrange("(kb p) n -> p kb n", p=P)
    with Phase("gl") as ctx:
        s = semaphores(nc, ctx, [
            "w0", "w1", "w2", "w3", "w4", "w5", "wl", "par", "par2", "par3", "u", "lr", "lr_kept", "z", "kept", "zk", "chain_v", "chain_a",
            "ab", "ez", "ln", "cum", "exps", "forms", "tr", "tr_kept", "sc", "sc_kept", "ds", "state", "o", "o_kept",
            "osq", "ovar", "osd", "onorm", "ot", "out0", "out", "stored"])
        wt = [sb(nc, ctx, f"w_block{i}", [P, KD, P]) for i in range(2)]
        wl = sb(nc, ctx, "w_lr", [P, KD, RANK])
        gup = sb(nc, ctx, "gate_up", [RANK, P])
        gb = sb(nc, ctx, "gate_bias", [P, 1])
        nw = sb(nc, ctx, "norm_col", [P, 1])
        glr = sb(nc, ctx, "glr", [RANK, T])
        qx, kx, v0, v1, g0, g1, cs, z = [sb(nc, ctx, n, [P, T]) for n in ("qx", "kx", "v0", "v1", "g0", "g1", "cs", "z")]
        kst = sb(nc, ctx, "kst", [P, T])
        lc = sb(nc, ctx, "chunk_decay", [P, NCH])
        tm = sb(nc, ctx, "tm", [P, 2, 3, P])
        scm = sb(nc, ctx, "scores", [P, 2, 2, P])
        S = sb(nc, ctx, "state", [P, 2, P])
        O = [sb(nc, ctx, f"o{h}", [P, TT, P]) for h in range(2)]
        st = sb(nc, ctx, "o_stat", [P, 3, 2 * TT])
        bank = k.bank
        with nc.Block() as block:
            @block.sync
            def _(sp):
                sp.dma_start(wl[:], wv[:, :, GLA_LR:GLA_LR + RANK]).then_inc(s["wl"], 16)

            @block.tensor
            def _(pe):
                pe.wait_ge(s["wl"], 16)
                for q in range(Q):
                    for kb in range(KD):
                        mm = nc.tensor.matmul(bank[q][0:RANK, :], wl[:, kb, :], hT[:, kb, q * QT:(q + 1) * QT],
                                              start=(kb == 0), stop=(kb == KD - 1))
                    mm.then_inc(s["lr"], 1)

            @block.scalar
            def _(act):
                go = Line(act, s["chain_a"])
                for q in range(Q):
                    act.wait_ge(s["lr"], q + 1)
                    go(nc.scalar.activation(glr[:, q * QT:(q + 1) * QT], bank[q][0:RANK, :], ACT.Copy), s["lr_kept"])
        meet(nc, s)
        with nc.Fori(0, 2) as gp:
            with nc.Block() as block:
                @block.sync
                def _(sp):
                    sp.dma_start(gup[:], gate_up[:, bass.ds(gp * P, P)]).then_inc(s["par"], 16)
                    sp.dma_start(gb[:], gate_bias_col[gp]).then_inc(s["par2"], 16)
                    sp.dma_start(nw[:], norm_col).then_inc(s["par3"], 16)
                    ats = (gp * P + GLA_Q, gp * P + GLA_K, gp * 256 + GLA_V, gp * 256 + (GLA_V + P), gp * 256 + GLA_G, gp * 256 + (GLA_G + P))
                    for i, at in enumerate(ats):
                        if i >= 2:
                            sp.wait_ge(s["u"], Q * (i - 1))
                        sp.dma_start(wt[i % 2][:], wv[:, :, bass.ds(at, P)]).then_inc((s["w0"], s["w1"], s["w2"], s["w3"], s["w4"], s["w5"])[i], 16)
                    sp.wait_ge(s["out0"], 1)
                    sp.dma_start(mT[gp * 2], g0[:]).then_inc(s["stored"], 16)
                    sp.wait_ge(s["out"], 1)
                    sp.dma_start(mT[gp * 2 + 1], g1[:]).then_inc(s["stored"], 16)
                    sp.wait_ge(s["stored"], 32)

                @block.tensor
                def _(pe):
                    pe.wait_ge(s["par"], 16)
                    for q in range(Q):
                        nc.tensor.matmul(bank[4 + q][:], gup[:], glr[:, q * QT:(q + 1) * QT], start=True, stop=True).then_inc(s["z"], 1)

                    def block_of_u(i):
                        pe.wait_ge((s["w0"], s["w1"], s["w2"], s["w3"], s["w4"], s["w5"])[i], 16)
                        for q in range(Q):
                            if i == 1:
                                pe.wait_ge(s["zk"], q + 1)
                            elif i in (2, 3):
                                pe.wait_ge(s["kept"], Q * (i - 2) + q + 1)
                            for kb in range(KD):
                                mm = nc.tensor.matmul(bank[4 * (i % 2) + q][:], wt[i % 2][:, kb, :],
                                                      hT[:, kb, q * QT:(q + 1) * QT], start=(kb == 0), stop=(kb == KD - 1))
                            mm.then_inc(s["u"], 1)
                    for i in range(4):
                        block_of_u(i)
                    pe.wait_ge(s["kept"], 4 * Q)
                    pe.wait_ge(s["forms"], 1)

                    def prepare(j):
                        ts = slice(j * P, (j + 1) * P)
                        jj = j % 2
                        if j >= 2:
                            pe.wait_ge(s["tr_kept"], j - 1)
                        for n, src in enumerate((kst[:, ts], v0[:, ts], v1[:, ts])):
                            mm = nc.tensor.transpose(bank[7 * jj][:, n * P:(n + 1) * P], src, k.ident[:])
                        mm.then_inc(s["tr"], 1)
                        if j:
                            pe.wait_ge(s["sc_kept"], j)
                        for h in range(2):
                            hs = slice(64 * h, 64 * h + 64)
                            mm = nc.tensor.matmul(bank[1 + h][:, 0:P], kx[hs, ts], qx[hs, ts], start=True, stop=True)
                        mm.then_inc(s["sc"], 1)
                    prepare(0)
                    for j in range(TT):
                        jj = j % 2
                        pe.wait_ge(s["sc_kept"], j + 1)
                        pe.wait_ge(s["tr_kept"], j + 1)
                        if j:
                            pe.wait_ge(s["o_kept"], j)
                        for h in range(2):
                            nc.tensor.matmul(bank[3 + h][:, 0:P], scm[:, jj, h, :], tm[:, jj, 1 + h, :],
                                             start=True, stop=False, skip_group_check=True)
                        for c in range(2):
                            n = 2 * j + c
                            cr = slice(64 * c, 64 * c + 64)
                            pe.wait_ge(s["state"], n + 1)
                            for h in range(2):
                                hs = slice(64 * h, 64 * h + 64)
                                nc.tensor.matmul(bank[5 + c][hs, 0:P], tm[cr, jj, 0, hs], tm[cr, jj, 1 + h, :], start=True, stop=True)
                            for h in range(2):
                                hs = slice(64 * h, 64 * h + 64)
                                mm = nc.tensor.matmul(bank[3 + h][cr, 0:P], qx[hs, j * P + 64 * c:j * P + 64 * c + 64],
                                                      S[hs, n % 2, :], start=False, stop=True, skip_group_check=True)
                            mm.then_inc(s["ds"], 1)
                            if c == 0 and j < TT - 1:
                                prepare(j + 1)
                    pe.wait_ge(s["o_kept"], TT)
                    pe.wait_ge(s["state"], NCH + 1)
                    for i in (4, 5):
                        block_of_u(i)
                    pe.wait_ge(s["onorm"], 1)
                    for h in range(2):
                        for q in range(Q):
                            pe.wait_ge(s["kept"], Q * (4 + h) + q + 1)
                            for j in range(4):
                                mm = nc.tensor.transpose(bank[4 * h + q][:, j * P:(j + 1) * P], O[h][:, 4 * q + j, :], k.ident[:])
                            mm.then_inc(s["ot"], 1)

                @block.scalar
                def _(act):
                    go = Line(act, s["chain_a"])
                    act.wait_ge(s["par2"], 16)
                    for q in range(Q):
                        act.wait_ge(s["z"], q + 1)
                        go(nc.scalar.activation(z[:, q * QT:(q + 1) * QT], bank[4 + q][:], ACT.Identity, bias=gb[:, 0:1]), s["zk"])
                    go(nc.scalar.activation(cs[:], z[:], ACT.Abs))
                    go(nc.scalar.activation(cs[:], cs[:], ACT.Exp, scale=-1.0))
                    go(nc.scalar.activation(cs[:], cs[:], ACT.Ln, bias=1.0), s["ln"])

                    def keep(i, dst, fn, sc):
                        for q in range(Q):
                            act.wait_ge(s["u"], Q * i + q + 1)
                            go(nc.scalar.activation(dst[:, q * QT:(q + 1) * QT], bank[4 * (i % 2) + q][:], fn, scale=sc), s["kept"])
                    keep(0, qx, ACT.Copy, 0.125)
                    act.wait_ge(s["cum"], 2)
                    go(nc.scalar.activation(O[0][:].rearrange("p j t -> p (j t)"), cs[:], ACT.Exp))
                    go(nc.scalar.activation(O[1][:].rearrange("p j t -> p (j t)"), cs[:], ACT.Exp, scale=-1.0))
                    go(nc.scalar.activation(kst[:], z[:], ACT.Exp), s["exps"])
                    keep(1, kx, ACT.Copy, 1.0)
                    keep(2, v0, ACT.Copy, 1.0)
                    keep(3, v1, ACT.Copy, 1.0)
                    act.wait_ge(s["forms"], 1)

                    def keep_turned(j):
                        act.wait_ge(s["tr"], j + 1)
                        if j >= 2:
                            act.wait_ge(s["ds"], 2 * (j - 1))
                        go(nc.scalar.activation(tm[:, j % 2, :, :], bank[7 * (j % 2)][:, 0:3 * P].rearrange("p (n c) -> p n c", c=P), ACT.Copy), s["tr_kept"])
                    keep_turned(0)
                    for j in range(TT):
                        if j < TT - 1:
                            keep_turned(j + 1)
                        act.wait_ge(s["ds"], 2 * (j + 1))
                        for h in range(2):
                            ins = nc.scalar.activation(O[h][:, j, :], bank[3 + h][:, 0:P], ACT.Copy)
                            if h:
                                go(ins, s["o_kept"])
                            else:
                                go(ins)
                    go(nc.scalar.activation(z[:], O[0][:].rearrange("p j t -> p (j t)"), ACT.Square))
                    go(nc.scalar.activation(cs[:], O[1][:].rearrange("p j t -> p (j t)"), ACT.Square), s["osq"])
                    act.wait_ge(s["ovar"], 1)
                    go(nc.scalar.activation(st[:, 1, :], st[:, 0, :], ACT.Sqrt), s["osd"])
                    keep(4, g0, ACT.Silu, 1.0)
                    keep(5, g1, ACT.Silu, 1.0)

                @block.vector
                def _(dve):
                    go = Line(dve, s["chain_v"])
                    go(nc.vector.memset(S[:, 0, :], 0.0), s["state"])
                    dve.wait_ge(s["ln"], 1)
                    go(nc.vector.tensor_scalar(z[:], z[:], 0.0, None, ALU.min))
                    go(nc.vector.tensor_tensor(z[:], z[:], cs[:], ALU.subtract))
                    go(nc.vector.tensor_scalar(z[:], z[:], 1.0 / 16, None, ALU.mult))
                    for n in range(NCH):
                        ins = nc.vector.tensor_tensor_scan(cs[:, n * C:(n + 1) * C], k.chunk_ones[:], z[:, n * C:(n + 1) * C], 0.0, ALU.mult, ALU.add)
                    go(ins, s["cum"])
                    csn = cs[:].rearrange("p (n t) -> p n t", t=C)
                    go(nc.vector.tensor_copy(lc[:], csn[:, :, C - 1]))
                    go(nc.vector.tensor_tensor(z[:].rearrange("p (n t) -> p n t", t=C), lc[:].unsqueeze(2).to_broadcast([P, NCH, C]), csn, ALU.subtract), s["cum"])
                    dve.wait_ge(s["exps"], 1)
                    e0, e1 = [O[h][:].rearrange("p j t -> p (j t)") for h in range(2)]
                    go(nc.vector.tensor_copy(lc[:], e0.rearrange("p (n t) -> p n t", t=C)[:, :, C - 1]))
                    dve.wait_ge(s["kept"], 2 * Q)
                    go(nc.vector.tensor_tensor(kst[:], kst[:], kx[:], ALU.mult))
                    go(nc.vector.tensor_tensor(kx[:], kx[:], e1, ALU.mult))
                    go(nc.vector.tensor_tensor(qx[:], qx[:], e0, ALU.mult), s["forms"])

                    def keep_scores(j):
                        dve.wait_ge(s["sc"], j + 1)
                        if j >= 2:
                            dve.wait_ge(s["ds"], 2 * (j - 1))
                        for h in range(2):
                            ins = nc.vector.tensor_tensor(scm[:, j % 2, h, :], bank[1 + h][:, 0:P], k.mask("inclusive"), ALU.mult)
                            go(ins, s["sc_kept"] if h else None)
                    keep_scores(0)
                    for j in range(TT):
                        for c in range(2):
                            n = 2 * j + c
                            dve.wait_ge(s["ds"], n + 1)
                            go(nc.vector.scalar_tensor_tensor(S[:, (n + 1) % 2, :], S[:, n % 2, :], lc[:, n:n + 1], bank[5 + c][:, 0:P], ALU.mult, ALU.add), s["state"])
                            if c == 0 and j < TT - 1:
                                keep_scores(j + 1)
                    dve.wait_ge(s["osq"], 1)
                    for h, sq in enumerate((z, cs)):
                        go(nc.vector.tensor_reduce(st[:, 0, h * TT:(h + 1) * TT], sq[:].rearrange("p (j t) -> p j t", t=P), AX.X, ALU.add))
                    go(nc.vector.tensor_scalar(st[:, 0, :], st[:, 0, :], 1.0 / P, EPS, ALU.mult, ALU.add), s["ovar"])
                    dve.wait_ge(s["osd"], 1)
                    go(nc.vector.reciprocal(st[:, 2, :], st[:, 1, :]))
                    for h in range(2):
                        ins = nc.vector.tensor_tensor(O[h][:], O[h][:], st[:, 2, h * TT:(h + 1) * TT].unsqueeze(2).to_broadcast([P, TT, P]), ALU.mult)
                        if h:
                            go(ins, s["onorm"])
                        else:
                            go(ins)
                    dve.wait_ge(s["par3"], 16)
                    for h, g in enumerate((g0, g1)):
                        for q in range(Q):
                            dve.wait_ge(s["ot"], 4 * h + q + 1)
                            dve.wait_ge(s["kept"], Q * (4 + h) + q + 1)
                            qs = slice(q * QT, (q + 1) * QT)
                            ins = nc.vector.scalar_tensor_tensor(g[:, qs], bank[4 * h + q][:], nw[:, 0:1], g[:, qs], ALU.mult, ALU.mult)
                            go(ins, (s["out0"], s["out"])[h] if q == Q - 1 else None)
            meet(nc, s)


def each_step(engine, step):
    for t in range(4):
        step(t, t % 2, t // 2)
    with engine.Fori(2, TT // 2 - 1) as pair:
        for odd in range(2):
            step(pair * 2 + odd, odd, pair)
    for t in range(TT - 2, TT + 3):
        step(t, t % 2, t // 2)


def is_tile(t):
    return not isinstance(t, int) or 0 <= t < TT


def out_product(nc, k, mT, w, resid, gate_row, norm_row, shift_row, store, turn_dst, gain, shift, final):
    first = final is not None
    mv = mT.rearrange("kb p t -> p kb t")
    at = lambda t: bass.ds(t * P, P)
    wv = w.rearrange("(kb p) n -> p kb n", p=P)
    F32R = mybir.dt.float32r
    with Phase("op" if first else "oq") as ctx:
        names = ["w0", "w1", "w_hi", "w_lo", "rows", "m0", "m1", "m_hi", "m_lo", "x0", "x1", "y", "y_read", "lat", "sq", "var", "sd", "rstd",
                 "sq2", "var2", "sd2", "rstd2", "scaled", "h", "turned", "kept", "st_lat0", "st_lat1"]
        if not first:
            names += ["logit", "largest", "less", "exp", "sum", "aff", "aff_t", "aff_kept", "st_h0", "st_h1"]
        s = semaphores(nc, ctx, names)
        wt = sb(nc, ctx, "w_out", [P, KD, D])
        mt = [sb(nc, ctx, f"m_tile{i}", [P, KD, P]) for i in range(2)]
        x = sb(nc, ctx, "x_tile", [P, 2, D])
        h = sb(nc, ctx, "h_tile", [P, 2, D])
        junk = sb(nc, ctx, "square", [P, D])
        stat = sb(nc, ctx, "stat", [P, 2, 8])
        row_a = sb(nc, ctx, "row_a", [P, D])
        if not first:
            w_hi, w_lo = [sb(nc, ctx, n, [P, KD, D], F32R) for n in ("w_hi", "w_lo")]
            m_hi, m_lo = [[sb(nc, ctx, f"{n}{i}", [P, KD, P], F32R) for i in range(2)] for n in ("m_hi", "m_lo")]
            gated = sb(nc, ctx, "gated", [P, D])
            row_g = sb(nc, ctx, "row_gain", [P, D])
            row_s = sb(nc, ctx, "row_shift", [P, D])
            hT2 = sb(nc, ctx, "h2_turned", [P, KD, P])
            lg = sb(nc, ctx, "softmax", [P, 2, NE])
            ls = sb(nc, ctx, "softmax_stat", [P, 2, 4])
            router = sb(nc, ctx, "router", [P, KD, NE])
        ROWS = 16 if first else 80
        bank = k.bank
        m_in, x_in, st_lat = (s["m0"], s["m1"]), (s["x0"], s["x1"]), (s["st_lat0"], s["st_lat1"])
        st_h = None if first else (s["st_h0"], s["st_h1"])
        half = lambda b: slice(b * 512, (b + 1) * 512)
        with nc.Block() as block:
            @block.sync
            def _(sp):
                for b in range(2):
                    sp.dma_start(wt[:, :, half(b)], wv[:, :, half(b)]).then_inc((s["w0"], s["w1"])[b], 16)
                    if b == 0:
                        sp.dma_start(mt[0][:], mv[:, :, at(0)]).then_inc(m_in[0], 16)
                        sp.dma_start(x[:, 0, :], resid[at(0), :]).then_inc(x_in[0], 16)
                if first:
                    sp.dma_start(row_a[:], norm_row.to_broadcast([P, D])).then_inc(s["rows"], 16)
                else:
                    sp.dma_start(k.ident, k.mask_in[:, 0:P]).then_inc(s["rows"], 16)
                    sp.dma_start(row_a[:], gate_row.to_broadcast([P, D])).then_inc(s["rows"], 16)
                    sp.dma_start(row_g[:], norm_row.to_broadcast([P, D])).then_inc(s["rows"], 16)
                    sp.dma_start(row_s[:], shift_row.to_broadcast([P, D])).then_inc(s["rows"], 16)
                    sp.dma_start(router[:], k.router.rearrange("(kb p) n -> p kb n", p=P)).then_inc(s["rows"], 16)

                def step(t, odd, pair):
                    if is_tile(t + 1):
                        if first:
                            wait_for(sp, s["y"], 2 * t)
                        else:
                            wait_for(sp, s["m_lo"], t)
                        sp.dma_start(mt[1 - odd][:], mv[:, :, at(t + 1)]).then_inc(m_in[1 - odd], 16)
                    if is_tile(t - 1):
                        sp.wait_ge(s["lat"], t)
                        sp.dma_start(store[at(t - 1), :], x[:, 1 - odd, :]).then_inc(st_lat[1 - odd], 16)
                        if not first:
                            sp.wait_ge(s["h"], t)
                            sp.dma_start(k.h2[at(t - 1), :], h[:, 1 - odd, :]).then_inc(st_h[1 - odd], 16)
                    if is_tile(t + 1):
                        if is_tile(t - 1):
                            sp.wait_ge(st_lat[1 - odd], (pair + odd) * 16)
                            sp.wait_ge(s["h"], t)
                        sp.dma_start(x[:, 1 - odd, :], resid[at(t + 1), :]).then_inc(x_in[1 - odd], 16)
                each_step(sp, step)
                for i in range(2):
                    sp.wait_ge(st_lat[i], 16 * TT // 2)
                    if not first:
                        sp.wait_ge(st_h[i], 16 * TT // 2)

            @block.tensor
            def _(pe):
                def weights(b):
                    if first:
                        pe.wait_ge((s["w0"], s["w1"])[b], 16)
                    else:
                        pe.wait_ge(s["w_lo"], b + 1)

                def product(t, odd, b):
                    for kb in range(KD):
                        psum = bank[2 * odd + b][:]
                        if first:
                            mm = nc.tensor.matmul(psum, mt[odd][:, kb, :], wt[:, kb, half(b)], start=(kb == 0), stop=(kb == KD - 1))
                            continue
                        nc.tensor.matmul(psum, m_lo[odd][:, kb, :], w_hi[:, kb, half(b)], start=(kb == 0), stop=False)
                        nc.tensor.matmul(psum, m_hi[odd][:, kb, :], w_lo[:, kb, half(b)], start=False, stop=False)
                        mm = nc.tensor.matmul(psum, m_hi[odd][:, kb, :], w_hi[:, kb, half(b)], start=False, stop=(kb == KD - 1))
                    mm.then_inc(s["y"], 1)

                def step(t, odd, pair):
                    if is_tile(t):
                        if isinstance(t, int) and t == 0:
                            weights(0)
                        if first:
                            pe.wait_ge(m_in[odd], pair * 16 + 16)
                        else:
                            pe.wait_ge(s["m_lo"], t + 1)
                        wait_for(pe, s["y_read"], 2 * t - 2)
                        product(t, odd, 0)
                    if is_tile(t - 2):
                        if isinstance(t, int) and t == 2:
                            pe.wait_ge(s["rows"], ROWS)
                        pe.wait_ge(s["h"], t - 1)
                        wait_for(pe, s["kept"], 2 * t - 4)
                        for b in range(2):
                            for j in range(4):
                                kb = 4 * b + j
                                mm = nc.tensor.transpose(bank[4 + b][:, j * P:(j + 1) * P], h[:, odd, kb * P:(kb + 1) * P], k.ident)
                            mm.then_inc(s["turned"], 1)
                    if is_tile(t):
                        if isinstance(t, int) and t == 0:
                            weights(1)
                        product(t, odd, 1)
                    if not first:
                        if is_tile(t - 3):
                            pe.wait_ge(s["aff"], t - 2)
                            wait_for(pe, s["aff_kept"], t - 3)
                            nc.tensor.transpose(bank[7][0:NE, 0:P], lg[:, 1 - odd, :], k.ident).then_inc(s["aff_t"], 1)
                        if is_tile(t - 2):
                            pe.wait_ge(s["kept"], 2 * t - 2)
                            wait_for(pe, s["exp"], t - 2)
                            for kb in range(KD):
                                mm = nc.tensor.matmul(bank[6][:, 0:NE], hT2[:, kb, :], router[:, kb, :], start=(kb == 0), stop=(kb == KD - 1))
                            mm.then_inc(s["logit"], 1)
                each_step(pe, step)

            @block.scalar
            def _(act):
                def split(t, odd, pair):
                    act.wait_ge(m_in[odd], pair * 16 + 16)
                    wait_for(act, s["y"], 2 * t - 2)
                    nc.scalar.activation(m_hi[odd][:], mt[odd][:], ACT.Copy).then_inc(s["m_hi"], 1)

                def root_mean(t, odd, c, sq, var, sd):
                    nc.scalar.activation(junk[:], x[:, odd, :], ACT.Square, accum_out=stat[:, odd, c:c + 1]).then_inc(sq, 1)
                    act.wait_ge(var, t + 1)
                    nc.scalar.activation(stat[:, odd, c + 2:c + 3], stat[:, odd, c + 1:c + 2], ACT.Sqrt).then_inc(sd, 1)
                if not first:
                    split(0, 0, 0)
                    for b in range(2):
                        act.wait_ge((s["w0"], s["w1"])[b], 16)
                        nc.scalar.activation(w_hi[:, :, half(b)], wt[:, :, half(b)], ACT.Copy).then_inc(s["w_hi"], 1)

                def step(t, odd, pair):
                    if not first and is_tile(t + 1):
                        split(t + 1, 1 - odd, pair + odd)
                    if not first and is_tile(t - 3):
                        act.wait_ge(s["less"], t - 2)
                        wait_for(act, s["aff_t"], t - 4)
                        nc.scalar.activation(lg[:, 1 - odd, :], bank[6][:, 0:NE], ACT.Exp, bias=ls[:, 1 - odd, 0:1],
                                             accum_out=ls[:, 1 - odd, 1:2]).then_inc(s["exp"], 1)
                    if is_tile(t):
                        if first:
                            act.wait_ge(s["y_read"], 2 * t + 2)
                        else:
                            act.wait_ge(s["lat"], t + 1)
                        wait_for(act, s["sq2"] if first else s["sq"], t)
                        root_mean(t, odd, 0, s["sq"], s["var"], s["sd"])
                        if first:
                            act.wait_ge(s["lat"], t + 1)
                            root_mean(t, odd, 4, s["sq2"], s["var2"], s["sd2"])
                each_step(act, step)

            @block.vector
            def _(dve):
                def split(t, odd):
                    dve.wait_ge(s["m_hi"], t + 1)
                    nc.vector.tensor_tensor(m_lo[odd][:], mt[odd][:], m_hi[odd][:].bitcast(F32), ALU.subtract).then_inc(s["m_lo"], 1)

                def inverse_root(t, odd, c, sq, var, sd, rstd):
                    dve.wait_ge(sq, t + 1)
                    nc.vector.tensor_scalar(stat[:, odd, c + 1:c + 2], stat[:, odd, c:c + 1], 1.0 / D, EPS, ALU.mult, ALU.add).then_inc(var, 1)
                    dve.wait_ge(sd, t + 1)
                    nc.vector.reciprocal(stat[:, odd, c + 3:c + 4], stat[:, odd, c + 2:c + 3]).then_inc(rstd, 1)
                    dve.wait_ge(rstd, t + 1)

                def keep(t):
                    for b in range(2):
                        dve.wait_ge(s["turned"], 2 * t + b + 1)
                        if first:
                            for j in range(4):
                                kb = 4 * b + j
                                ins = nc.vector.tensor_scalar(turn_dst[:, kb, at(t)], bank[4 + b][:, j * P:(j + 1) * P],
                                                              gain[:, kb:kb + 1], shift[:, kb:kb + 1], ALU.mult, ALU.add)
                        else:
                            wait_for(dve, s["logit"], t)
                            ins = nc.vector.tensor_copy(hT2[:, 4 * b:4 * b + 4, :], bank[4 + b][:].rearrange("p (k t) -> p k t", t=P))
                        ins.then_inc(s["kept"], 1)

                def softmax(t, odd):
                    dve.wait_ge(s["logit"], t + 1)
                    nc.vector.tensor_reduce(ls[:, odd, 2:3], bank[6][:, 0:NE], AX.X, ALU.max).then_inc(s["largest"], 1)
                    dve.wait_ge(s["largest"], t + 1)
                    nc.vector.tensor_scalar(ls[:, odd, 0:1], ls[:, odd, 2:3], -1.0, None, ALU.mult).then_inc(s["less"], 1)
                    dve.wait_ge(s["exp"], t + 1)
                    nc.vector.reciprocal(ls[:, odd, 3:4], ls[:, odd, 1:2]).then_inc(s["sum"], 1)
                    dve.wait_ge(s["sum"], t + 1)
                    nc.vector.tensor_scalar(lg[:, odd, :], lg[:, odd, :], ls[:, odd, 3:4], None, ALU.mult).then_inc(s["aff"], 1)
                if not first:
                    split(0, 0)
                    for b in range(2):
                        dve.wait_ge(s["w_hi"], b + 1)
                        nc.vector.tensor_tensor(w_lo[:, :, half(b)], wt[:, :, half(b)], w_hi[:, :, half(b)].bitcast(F32),
                                                ALU.subtract).then_inc(s["w_lo"], 1)
                dve.wait_ge(s["rows"], ROWS)

                def step(t, odd, pair):
                    if not first and is_tile(t + 1):
                        split(t + 1, 1 - odd)
                    for b in range(2):
                        if is_tile(t):
                            if b == 0:
                                dve.wait_ge(x_in[odd], pair * 16 + 16)
                            dve.wait_ge(s["y"], 2 * t + b + 1)
                            if first:
                                nc.vector.tensor_tensor(x[:, odd, half(b)], x[:, odd, half(b)], bank[2 * odd + b][:], ALU.add).then_inc(s["y_read"], 1)
                            else:
                                wait_for(dve, s["lat"], t)
                                nc.vector.tensor_tensor(gated[:, half(b)], bank[2 * odd + b][:], row_a[:, half(b)], ALU.mult).then_inc(s["y_read"], 1)
                        if b == 0:
                            if is_tile(t - 2):
                                keep(t - 2)
                            if not first and is_tile(t - 3):
                                softmax(t - 3, 1 - odd)
                    if is_tile(t):
                        if not first:
                            dve.wait_ge(s["y_read"], 2 * t + 2)
                            nc.vector.tensor_tensor(x[:, odd, :], x[:, odd, :], gated[:], ALU.add).then_inc(s["lat"], 1)
                    if not first and is_tile(t - 3):
                        dve.wait_ge(s["aff_t"], t - 2)
                        nc.vector.tensor_copy(turn_dst[:, at(t - 3)], bank[7][0:NE, 0:P]).then_inc(s["aff_kept"], 1)
                    if is_tile(t):
                        inverse_root(t, odd, 0, s["sq"], s["var"], s["sd"], s["rstd"])
                        if first:
                            nc.vector.scalar_tensor_tensor(x[:, odd, :], x[:, odd, :], stat[:, odd, 3:4], row_a[:], ALU.mult, ALU.mult).then_inc(s["lat"], 1)
                            inverse_root(t, odd, 4, s["sq2"], s["var2"], s["sd2"], s["rstd2"])
                        wait_for(dve, s["turned"], 2 * t - 2)
                        if first:
                            nc.vector.tensor_scalar(h[:, odd, :], x[:, odd, :], stat[:, odd, 7:8], None, ALU.mult).then_inc(s["h"], 1)
                        else:
                            if is_tile(t - 2):
                                dve.wait_ge(st_h[odd], pair * 16)
                            nc.vector.scalar_tensor_tensor(h[:, odd, :], x[:, odd, :], stat[:, odd, 3:4], row_g[:], ALU.mult, ALU.mult).then_inc(s["scaled"], 1)
                            dve.wait_ge(s["scaled"], t + 1)
                            nc.vector.tensor_tensor(h[:, odd, :], h[:, odd, :], row_s[:], ALU.add).then_inc(s["h"], 1)
                each_step(dve, step)
        meet(nc, s)


def short_conv(nc, k, hT, hidden, w_in, conv_col, zT):
    wv = w_in.rearrange("(kb p) n -> p kb n", p=P)
    F32R = mybir.dt.float32r
    with Phase("sc") as ctx:
        s = semaphores(nc, ctx, ["w0", "w1", "w2", "par", "x_hi", "x_lo", "hi", "lo", "u", "c_kept", "edges", "gated", "conv", "out", "stored"])
        hidden.close()
        hT_lo = sb(nc, ctx, "hT_lo", [P, KD, T], F32R)
        raw = [sb(nc, ctx, f"w_loaded{i}", [P, KD, P]) for i in range(3)]
        w_hi = [sb(nc, ctx, f"w_hi{i}", [P, KD, P], F32R) for i in range(3)]
        w_lo = [sb(nc, ctx, f"w_lo{i}", [P, KD, P], F32R) for i in range(3)]
        x_hi = sb(nc, ctx, "x_hi", [P, KD, T], F32R)
        cw = sb(nc, ctx, "conv_cols", [P, KD * 3])
        gv = sb(nc, ctx, "gated", [P, T + 2])
        acc = sb(nc, ctx, "conv", [P, T])
        bank = k.bank
        AT = (D, 2 * D, 0)
        loads = (s["w0"], s["w1"], s["w2"])
        of = lambda q: slice(q * QT, (q + 1) * QT)

        def split_hi(act, cb, i):
            act.wait_ge(loads[i], cb * 16 + 16)
            nc.scalar.activation(w_hi[i][:], raw[i][:], ACT.Copy).then_inc(s["hi"], 1)

        def split_lo(dve, cb, i):
            dve.wait_ge(s["hi"], cb * 3 + i + 1)
            nc.vector.tensor_tensor(w_lo[i][:], raw[i][:], w_hi[i][:].bitcast(F32), ALU.subtract).then_inc(s["lo"], 1)

        with nc.Block() as block:
            @block.sync
            def _(sp):
                for i in range(3):
                    sp.dma_start(raw[i][:], wv[:, :, AT[i]:AT[i] + P]).then_inc(loads[i], 16)
                sp.dma_start(cw[:].rearrange("p (b c) -> p b c", c=3), conv_col.rearrange("b p c -> p b c")).then_inc(s["par"], 16)

                def store(cb):
                    sp.wait_ge(s["out"], cb * Q + Q)
                    sp.dma_start(zT[cb], acc[:]).then_inc(s["stored"], 16)
                with sp.Fori(0, KD - 1) as cb:
                    for i in range(3):
                        sp.wait_ge(s["lo"], cb * 3 + i + 1)
                        sp.dma_start(raw[i][:], wv[:, :, bass.ds(cb * P + (AT[i] + P), P)]).then_inc(loads[i], 16)
                    store(cb)
                store(KD - 1)
                sp.wait_ge(s["stored"], KD * 16)

            @block.tensor
            def _(pe):
                def turn(cb):
                    for i in range(3):
                        pe.wait_ge(s["lo"], cb * 3 + i + 1)
                        for q in range(Q):
                            if i == 0:
                                pe.wait_ge(s["x_lo"], q + 1)
                                wait_for(pe, s["out"], cb * Q)
                            elif i == 1:
                                wait_for(pe, s["gated"], cb * Q)
                            else:
                                pe.wait_ge(s["c_kept"], cb * Q + q + 1)
                            for kb in range(KD):
                                psum, x = bank[4 * (i % 2) + q][:], (slice(None), kb, of(q))
                                nc.tensor.matmul(psum, w_lo[i][:, kb, :], x_hi[x], start=(kb == 0), stop=False)
                                nc.tensor.matmul(psum, w_hi[i][:, kb, :], hT_lo[x], start=False, stop=False)
                                mm = nc.tensor.matmul(psum, w_hi[i][:, kb, :], x_hi[x], start=False, stop=(kb == KD - 1))
                            mm.then_inc(s["u"], 1)
                turn(0)
                with pe.Fori(1, KD) as cb:
                    turn(cb)

            @block.scalar
            def _(act):
                split_hi(act, 0, 0)
                for q in range(Q):
                    nc.scalar.activation(x_hi[:, :, of(q)], hT[:, :, of(q)], ACT.Copy).then_inc(s["x_hi"], 1)
                split_hi(act, 0, 1)
                split_hi(act, 0, 2)

                def turn(cb, last):
                    wait_for(act, s["conv"], cb * 3)
                    for q in range(Q):
                        act.wait_ge(s["u"], cb * 3 * Q + q + 1)
                        nc.scalar.activation(gv[:, 1 + q * QT:1 + (q + 1) * QT], bank[q][:], ACT.Copy).then_inc(s["c_kept"], 1)
                    for i in range(0 if last else 3):
                        act.wait_ge(s["u"], (cb * 3 + i + 1) * Q)
                        split_hi(act, cb + 1, i)
                turn(0, False)
                with act.Fori(1, KD - 1) as cb:
                    turn(cb, False)
                turn(KD - 1, True)

            @block.vector
            def _(dve):
                nc.vector.memset(gv[:, 0:1], 0.0).then_inc(s["edges"], 1)
                nc.vector.memset(gv[:, T + 1:T + 2], 0.0).then_inc(s["edges"], 1)
                split_lo(dve, 0, 0)
                for q in range(Q):
                    dve.wait_ge(s["x_hi"], q + 1)
                    nc.vector.tensor_tensor(hT_lo[:, :, of(q)], hT[:, :, of(q)], x_hi[:, :, of(q)].bitcast(F32), ALU.subtract).then_inc(s["x_lo"], 1)
                split_lo(dve, 0, 1)
                split_lo(dve, 0, 2)
                dve.wait_ge(s["par"], 16)
                dve.wait_ge(s["edges"], 2)

                def turn(cb, last):
                    if not last:
                        split_lo(dve, cb + 1, 0)
                    for q in range(Q):
                        dve.wait_ge(s["c_kept"], cb * Q + q + 1)
                        dve.wait_ge(s["u"], (cb * 3 + 1) * Q + q + 1)
                        qs = slice(1 + q * QT, 1 + (q + 1) * QT)
                        nc.vector.tensor_tensor(gv[:, qs], gv[:, qs], bank[4 + q][:], ALU.mult).then_inc(s["gated"], 1)
                    wait_for(dve, s["stored"], cb * 16)
                    dve.wait_ge(s["gated"], cb * Q + Q)
                    tap = lambda c: cw[:, bass.ds(cb * 3 + c, 1)]
                    nc.vector.tensor_scalar(acc[:], gv[:, 0:T], tap(0), None, ALU.mult).then_inc(s["conv"], 1)
                    for c in (1, 2):
                        dve.wait_ge(s["conv"], cb * 3 + c)
                        nc.vector.scalar_tensor_tensor(acc[:], gv[:, c:T + c], tap(c), acc[:], ALU.mult, ALU.add).then_inc(s["conv"], 1)
                    if not last:
                        split_lo(dve, cb + 1, 1)
                    dve.wait_ge(s["conv"], cb * 3 + 3)
                    for q in range(Q):
                        dve.wait_ge(s["u"], (cb * 3 + 2) * Q + q + 1)
                        nc.vector.tensor_tensor(acc[:, of(q)], acc[:, of(q)], bank[q][:], ALU.mult).then_inc(s["out"], 1)
                    if not last:
                        split_lo(dve, cb + 1, 2)
                turn(0, False)
                with dve.Fori(1, KD - 1) as cb:
                    turn(cb, False)
                turn(KD - 1, True)
        meet(nc, s)


def choose(nc, k, aff, idx_all, gate_all, beside):
    HALF, R = T // 2, 2 * NE
    with Phase("ch") as ctx:
        s = semaphores(nc, ctx, ["spread", "chain_v", "ranked", "moved", "picked", "turned"])
        seg = sb(nc, ctx, "segments", [R, HALF])
        idx = sb(nc, ctx, "top_idx", [R, CAP], U32)
        top = sb(nc, ctx, "top", [R, 2, CAP])
        flip = [sb(nc, ctx, f"flipped{i}", [NE, 2, CAP]) for i in range(2)]
        won = sb(nc, ctx, "won", [NE, CAP])
        bank = k.bank
        with nc.Block() as block:
            @block.sync
            def _(sp):
                for h in range(2):
                    sp.dma_start(seg[h * NE:(h + 1) * NE, :], aff[:, h * HALF:(h + 1) * HALF]).then_inc(s["spread"], 16)
                beside.sync(sp)
                sp.wait_ge(s["ranked"], 1)
                sp.dma_start(flip[0][:], top[NE:R]).then_inc(s["moved"], 16)

            @block.scalar
            def _(act):
                beside.scalar(act)

            @block.gpsimd
            def _(pool):
                beside.gpsimd(pool)

            @block.vector
            def _(dve):
                go = Line(dve, s["chain_v"])
                dve.wait_ge(s["spread"], 32)
                for i in range(CAP // 8):
                    e = slice(8 * i, 8 * i + 8)
                    go(nc.vector.max(top[:, 0, e], seg[:]))
                    go(nc.vector.max_index(idx[:, e], top[:, 0, e], seg[:]))
                    if i < CAP // 8 - 1:
                        go(nc.vector.match_replace(seg[:], top[:, 0, e], seg[:], -1.0))
                go(nc.vector.tensor_copy(top[:, 1, :], idx[:]), s["ranked"])
                dve.wait_ge(s["moved"], 16)
                bits = CAP.bit_length() - 1
                for b in range(bits):
                    view = lambda x: x[:].rearrange("p n (o two i) -> p (n o) two i", two=2, i=1 << b)
                    for side in range(2):
                        go(nc.vector.tensor_copy(view(flip[(b + 1) % 2])[:, :, side, :], view(flip[b % 2])[:, :, 1 - side, :]))
                second = flip[bits % 2]
                first = top[0:NE]
                go(nc.vector.tensor_scalar(second[:, 1, :], second[:, 1, :], float(HALF), None, ALU.add))
                go(nc.vector.tensor_tensor(won[:], first[:, 0, :], second[:, 0, :], ALU.is_ge))
                go(nc.vector.tensor_tensor(first[:, 0, :], first[:, 0, :], second[:, 0, :], ALU.max))
                go(nc.vector.tensor_tensor(first[:, 1, :], first[:, 1, :], second[:, 1, :], ALU.subtract))
                go(nc.vector.tensor_tensor(first[:, 1, :], first[:, 1, :], won[:], ALU.mult))
                go(nc.vector.tensor_tensor(first[:, 1, :], first[:, 1, :], second[:, 1, :], ALU.add), s["picked"])
                dve.wait_ge(s["turned"], 1)
                go(nc.vector.tensor_copy(gate_all[:], bank[0][:, 0:2 * NE]))
                go(nc.vector.tensor_copy(idx_all[:], bank[0][:, 2 * NE:4 * NE]))

            @block.tensor
            def _(pe):
                pe.wait_ge(s["picked"], 1)
                for n in range(2):
                    for h in range(2):
                        o = (2 * n + h) * NE
                        mm = nc.tensor.transpose(bank[0][:, o:o + NE], top[0:NE, n, h * P:(h + 1) * P], k.ident[0:NE, 0:NE])
                mm.then_inc(s["turned"], 1)
        meet(nc, s)


def experts(nc, k, wg, wu, wd, aff, idx_all, gate_all, out):
    gv = wg.rearrange("o e (kb p) f -> (o e) p kb f", p=P)
    uv = wu.rearrange("o e (kb p) f -> (o e) p kb f", p=P)
    dv = wd.rearrange("o e (kb p) d -> p (o e kb) d", p=P)
    CH, LOADED, SPLIT, W = 12, 4, 6, KD * 256
    F32R = mybir.dt.float32r
    with Phase("ex") as ctx:
        s = semaphores(nc, ctx, ["row", "load0", "load1", "load2", "load3", "hi", "lo", "used", "turned", "x_hi", "x_lo", "gu", "silu",
                                 "hid", "hid_hi", "hid_lo", "y", "ys", "idx", "gates", "chain_v"])
        gathered = [ctx.enter_context(nc.semaphore(f"gathered{h}")) for h in range(2)]
        sent = [ctx.enter_context(nc.semaphore(f"sent{h}")) for h in range(2)]
        mark = sb(nc, ctx, "mark", [P, 1])
        raw = sb(nc, ctx, "w_loaded", [P, LOADED, W])
        w_hi = [sb(nc, ctx, f"w_hi{i}", [P, W], F32R) for i in range(SPLIT)]
        w_lo = [sb(nc, ctx, f"w_lo{i}", [P, W], F32R) for i in range(SPLIT)]
        xg = sb(nc, ctx, "x_gathered", [P, 2, D])
        x_hi = sb(nc, ctx, "x_hi", [P, KD, CAP], F32R)
        x_lo = sb(nc, ctx, "x_lo", [P, KD, CAP], F32R)
        h_hi = sb(nc, ctx, "hid_hi", [P, KD, CAP], F32R)
        h_lo = sb(nc, ctx, "hid_lo", [P, KD, CAP], F32R)
        sl = sb(nc, ctx, "silu", [P, 2, CAP])
        hid = sb(nc, ctx, "hidden", [P, 2, CAP])
        ys = sb(nc, ctx, "y", [P, 2, D])
        g2 = sb(nc, ctx, "g2_row", [P, D])
        idx = sb(nc, ctx, "idx", [P, 2, 2], U32)
        gates = sb(nc, ctx, "gates", [P, 2])
        bank = k.bank
        idv = idx_all[:].rearrange("p (h e) -> p h e", h=2)
        gav = gate_all[:].rearrange("p (h e) -> p h e", h=2)
        loads = [s[f"load{i}"] for i in range(LOADED)]

        def load(sp, e, c):
            views = (gv, uv) if c < CH else (gv[1:], uv[1:])
            c = c % CH
            dst = raw[:, c % LOADED, :]
            if c < 8:
                src = views[c % 2][e, :, :, (c // 2) * 256:(c // 2 + 1) * 256]
                dst = dst.rearrange("p (kb f) -> p kb f", f=256)
            else:
                dst = dst.rearrange("p (kb d) -> p kb d", d=D)
                src = dv[:, bass.ds(e * KD + (c - 8) * 2, 2), :]
            sp.dma_start(dst, src).then_inc(loads[c % LOADED], 16)

        def split_hi(act, e, c):
            act.wait_ge(loads[c % LOADED], e * 48 + 16 * (c // LOADED + 1))
            nc.scalar.activation(w_hi[c % SPLIT][:], raw[:, c % LOADED, :], ACT.Copy).then_inc(s["hi"], 1)

        def split_lo(dve, e, c, engine=nc.vector):
            dve.wait_ge(s["hi"], e * CH + c + 1)
            engine.tensor_tensor(w_lo[c % SPLIT][:], raw[:, c % LOADED, :], w_hi[c % SPLIT][:].bitcast(F32), ALU.subtract).then_inc(s["lo"], 1)

        def passes(psum, lh, ll, rh, rl, first, last):
            nc.tensor.matmul(psum, ll, rh, start=first, stop=False)
            nc.tensor.matmul(psum, lh, rl, start=False, stop=False)
            return nc.tensor.matmul(psum, lh, rh, start=False, stop=last)

        def turn_tokens(pe):
            for h in range(2):
                for b in range(2):
                    for j in range(4):
                        kb = 4 * b + j
                        mm = nc.tensor.transpose(bank[2 * h + b][:, j * P:(j + 1) * P], xg[:, h, kb * P:(kb + 1) * P], k.ident[:])
                    mm.then_inc(s["turned"], 1)

        def each_turned(do):
            for h in range(2):
                for b in range(2):
                    do(2 * h + b, (slice(None), slice(4 * b, 4 * b + 4), slice(h * P, (h + 1) * P)), bank[2 * h + b][:].rearrange("p (k t) -> p k t", t=P))

        class Beside:

            def sync(self, sp):
                for c in range(SPLIT):
                    if c >= LOADED:
                        sp.wait_ge(s["lo"], c - LOADED + 1)
                    load(sp, 0, c)
                sp.dma_start(g2[:], k.rows_dram[3:4, :].to_broadcast([P, D])).then_inc(s["row"], 16)

            def scalar(self, act):
                for c in range(SPLIT):
                    split_hi(act, 0, c)

            def gpsimd(self, pool):
                for c in range(SPLIT):
                    split_lo(pool, 0, c, nc.gpsimd)
        choose(nc, k, aff, idx_all, gate_all, Beside())
        with nc.Block() as block:
            @block.sync
            def _(sp):
                def turn(e, last, c0=0):
                    for c in range(c0, CH - LOADED if last else CH):
                        sp.wait_ge(s["lo"], e * CH + c + 1)
                        load(sp, e, c + LOADED)
                turn(0, False, SPLIT - LOADED)
                with sp.Fori(1, NE - 1) as e:
                    turn(e, False)
                turn(NE - 1, True)

            @block.gpsimd
            def _(pool):
                def passed(pool):
                    nc.gpsimd.tensor_tensor(mark[:], k.ident[:, 0:1], k.ident[:, 0:1], ALU.mult).then_inc(s["idx"], 1)

                def gather(e, copied):
                    nc.gpsimd.tensor_copy(idx[:, :, 1:2], idv[:, :, bass.ds(e, 1)]).then_inc(s["idx"], 1)
                    pool.wait_ge(s["idx"], copied)
                    passed(pool)
                    for h in range(2):
                        pool.indirect_dma_start(out=xg[:, h, :], out_offset=None, in_=k.h2,
                                                in_offset=bass.IndirectOffsetOnAxis(ap=idx[:, h, 1:2], axis=0)).then_inc(gathered[h], 16)

                def scatter(e, copied):
                    nc.gpsimd.tensor_copy(idx[:, :, 0:1], idv[:, :, bass.ds(e, 1)]).then_inc(s["idx"], 1)
                    pool.wait_ge(s["idx"], copied)
                    pool.wait_ge(s["ys"], e * 2 + 3)
                    passed(pool)
                    for h in range(2):
                        pool.indirect_dma_start(out=out, out_offset=bass.IndirectOffsetOnAxis(ap=idx[:, h, 0:1], axis=0),
                                                in_=ys[:, h, :], in_offset=None, compute_op=ALU.add).then_inc(sent[h], 16)
                    for h in range(2):
                        pool.wait_ge(sent[h], e * 16 + 16)
                gather(0, 1)
                with pool.Fori(0, NE - 1) as e:
                    for h in range(2):
                        pool.wait_ge(gathered[h], e * 16 + 16)
                    pool.wait_ge(s["turned"], e * 4 + 4)
                    gather(e + 1, e * 4 + 3)
                    scatter(e, e * 4 + 5)
                scatter(NE - 1, NE * 4 - 1)

            @block.tensor
            def _(pe):
                for h in range(2):
                    pe.wait_ge(gathered[h], 16)
                turn_tokens(pe)

                def turn(e, last):
                    pe.wait_ge(s["x_lo"], e * 4 + 4)
                    for f in range(KD):
                        q = f // 2
                        if f >= 2:
                            pe.wait_ge(s["hid"], e * KD + f - 1)
                        for half in range(2):
                            c = 2 * q + half
                            if f % 2 == 0:
                                pe.wait_ge(s["lo"], e * CH + c + 1)
                            for kb in range(KD):
                                o = kb * 256 + (f % 2) * P
                                mm = passes(bank[2 * (f % 2) + half][:, 0:CAP], w_hi[c % SPLIT][:, o:o + P], w_lo[c % SPLIT][:, o:o + P],
                                            x_hi[:, kb, :], x_lo[:, kb, :], kb == 0, kb == KD - 1)
                            mm.then_inc(s["gu"], 1)
                    if not last:
                        pe.wait_ge(s["hid"], e * KD + KD)
                        for h in range(2):
                            pe.wait_ge(gathered[h], e * 16 + 32)
                        turn_tokens(pe)
                    pe.wait_ge(s["ys"], e * 2 + 1)
                    for f in range(KD):
                        c = 8 + f // 2
                        pe.wait_ge(s["hid_lo"], e * KD + f + 1)
                        if f % 2 == 0:
                            pe.wait_ge(s["lo"], e * CH + c + 1)
                        for h in range(2):
                            hs = slice(h * P, (h + 1) * P)
                            for b in range(2):
                                o = (f % 2) * D + b * 512
                                mm = passes(bank[4 + 2 * h + b][:], h_hi[:, f, hs], h_lo[:, f, hs], w_hi[c % SPLIT][:, o:o + 512],
                                            w_lo[c % SPLIT][:, o:o + 512], f == 0, f == KD - 1)
                        if f % 2:
                            mm.then_inc(s["y"], 1)
                with pe.Fori(0, NE - 1) as e:
                    turn(e, False)
                turn(NE - 1, True)

            @block.scalar
            def _(act):
                def keep(n, at, src):
                    nc.scalar.activation(x_hi[at], src, ACT.Copy).then_inc(s["x_hi"], 1)

                def first(n, at, src):
                    act.wait_ge(s["turned"], n + 1)
                    keep(n, at, src)
                each_turned(first)

                def turn(e, last):
                    for f in range(KD):
                        act.wait_ge(s["gu"], e * 2 * KD + 2 * f + 1)
                        nc.scalar.activation(sl[:, f % 2, :], bank[2 * (f % 2)][:, 0:CAP], ACT.Silu).then_inc(s["silu"], 1)
                        act.wait_ge(s["hid"], e * KD + f + 1)
                        nc.scalar.activation(h_hi[:, f, :], hid[:, f % 2, :], ACT.Copy).then_inc(s["hid_hi"], 1)
                        if f % 2:
                            for c in (f - 1, f):
                                if last and c + SPLIT >= CH:
                                    continue
                                act.wait_ge(s["gu"], e * 2 * KD + 2 * f + 2)
                                wrap = (e + 1, c + SPLIT - CH) if c + SPLIT >= CH else (e, c + SPLIT)
                                split_hi(act, *wrap)
                    if not last:
                        def following(n, at, src):
                            act.wait_ge(s["turned"], e * 4 + 5 + n)
                            keep(n, at, src)
                        each_turned(following)
                        for d in range(4):
                            act.wait_ge(s["y"], e * 4 + d + 1)
                            split_hi(act, e + 1, 2 + d)
                with act.Fori(0, NE - 1) as e:
                    turn(e, False)
                turn(NE - 1, True)

            @block.vector
            def _(dve):
                nc.vector.memset(ys[:], 0.0).then_inc(s["ys"], 1)
                dve.wait_ge(s["row"], 16)

                def keep(n, at, src):
                    nc.vector.tensor_tensor(x_lo[at], src, x_hi[at].bitcast(F32), ALU.subtract).then_inc(s["x_lo"], 1)

                def first(n, at, src):
                    dve.wait_ge(s["x_hi"], n + 1)
                    keep(n, at, src)
                each_turned(first)

                def turn(e, last):
                    for f in range(KD):
                        dve.wait_ge(s["gu"], e * 2 * KD + 2 * f + 2)
                        dve.wait_ge(s["silu"], e * KD + f + 1)
                        nc.vector.tensor_tensor(hid[:, f % 2, :], sl[:, f % 2, :], bank[2 * (f % 2) + 1][:, 0:CAP], ALU.mult).then_inc(s["hid"], 1)
                        dve.wait_ge(s["hid_hi"], e * KD + f + 1)
                        nc.vector.tensor_tensor(h_lo[:, f, :], hid[:, f % 2, :], h_hi[:, f, :].bitcast(F32), ALU.subtract).then_inc(s["hid_lo"], 1)
                        if f % 2:
                            for c in (f - 1, f):
                                if last and c + SPLIT >= CH:
                                    continue
                                wrap = (e + 1, c + SPLIT - CH) if c + SPLIT >= CH else (e, c + SPLIT)
                                split_lo(dve, *wrap)
                    if not last:
                        def following(n, at, src):
                            dve.wait_ge(s["x_hi"], e * 4 + 5 + n)
                            keep(n, at, src)
                        each_turned(following)
                        for d in range(4):
                            split_lo(dve, e + 1, 2 + d)
                    nc.vector.tensor_copy(gates[:], gav[:, :, bass.ds(e, 1)].rearrange("p h e -> p (h e)")).then_inc(s["gates"], 1)
                    dve.wait_ge(s["gates"], e + 1)
                    dve.wait_ge(s["y"], e * 4 + 4)
                    for h in range(2):
                        dve.wait_ge(s["idx"], e * 4 + 3)
                        for b in range(2):
                            bs = slice(b * 512, (b + 1) * 512)
                            ins = nc.vector.scalar_tensor_tensor(ys[:, h, bs], bank[4 + 2 * h + b][:], gates[:, h:h + 1], g2[:, bs], ALU.mult, ALU.mult)
                        ins.then_inc(s["ys"], 1)
                with dve.Fori(0, NE - 1) as e:
                    turn(e, False)
                turn(NE - 1, True)
        meet(nc, s)


MASKS = ("ident", "head_ones", "heads", "scores", "corner", "corner_t", "levels", "inclusive")


def mask_constants():
    i = np.arange(P)
    s, t = i[:, None], i[None, :]
    same = (s // C) == (t // C)
    strict, incl = (s < t) & same, (s <= t) & same
    heads = (s // 64) == (t // 64)

    def merge(b):
        return (s // (2 * b) == t // (2 * b)) & (s // b % 2 == 0) & (t // b % 2 == 1)

    parts = {
        "ident": s == t, "head_ones": heads, "heads": heads,
        "scores": np.concatenate([strict, incl, strict, incl], 1),
        "corner": -(merge(1).T.astype(np.float32)), "corner_t": -(merge(1).astype(np.float32)),
        "levels": np.concatenate([-(merge(2 << l).astype(np.float32)) for l in range(LEVELS)], 1),
        "inclusive": incl,
    }
    place, at, cols = {}, 0, []
    for name in MASKS:
        a = parts[name].astype(np.float32)
        place[name] = (at, a.shape[1])
        at += a.shape[1]
        cols.append(a)
    return np.ascontiguousarray(np.concatenate(cols, 1)), place, at


def hybrid_conv_moe(nc, x, norm_w_col, w_in, gate_up, gate_bias_col, gla_norm_col, mu_lora_col, w_up, a_up,
                    rwkv_cols, w_out, final_norm, c_col, ada_w, ada_b, ada_b_col, norm_g, norm_g_col,
                    sc_w_in, sc_conv_col, sc_w_out, router, wg, wu, wd, masks, out):
    _, place, width = mask_constants()
    k = Shared()
    k.router = router
    k.rows_dram = nc.dram_tensor("mod_rows_dram", [4, D], F32).ap()
    k.h2 = nc.dram_tensor("h2_dram", [T, D], F32).ap()
    lat = nc.dram_tensor("lat_dram", [T, D], F32).ap()
    mT = nc.dram_tensor("merged_dram", [KD, P, T], F32).ap()
    zT = nc.dram_tensor("z_dram", [KD, P, T], F32).ap()
    k.mask_in = masks
    k.bank = [nc.alloc_psum_tensor(f"bank{i}", [P, 512], F32) for i in range(8)]
    with Phase("mixers") as top:
        k.mask_sb = sb(nc, top, "masks", [P, width])
        k.mask = lambda name: k.mask_sb[:, place[name][0]:place[name][0] + place[name][1]]
        k.ident = k.mask_sb[:, 0:P]
        k.ones = sb(nc, top, "ones", [P, C])
        k.chunk_ones = k.ones
        k.shift1 = sb(nc, top, "shift1", [P, KD])
        k.gain1 = sb(nc, top, "gain1", [P, KD])
        hidden = Phase("hidden")
        hT = sb(nc, hidden, "hT", [P, KD, T])
        modulate_and_norm(nc, k, c_col, ada_w[0], ada_b, ada_b_col, norm_g[0], norm_g_col, x, hT, norm_w_col)
        rwkv(nc, k, hT, w_in[0], w_up[0], a_up[0], rwkv_cols, mu_lora_col, mT)
        gla(nc, k, hT, w_in[0], gate_up[0], gate_bias_col, gla_norm_col, mT)
        out_product(nc, k, mT, w_out[0], x[0], None, final_norm, None, lat, hT, k.gain1, k.shift1, True)
        short_conv(nc, k, hT, hidden, sc_w_in[0], sc_conv_col, zT)
    with Phase("moe") as top:
        mask2 = sb(nc, top, "ident2", [P, P])
        aff = sb(nc, top, "affinity", [NE, T])
        idx_all = sb(nc, top, "idx_all", [P, 2 * NE], U32)
        gate_all = sb(nc, top, "gate_all", [P, 2 * NE])
        k.ident = mask2[:]
        rows = k.rows_dram
        out_product(nc, k, zT, sc_w_out[0], lat, rows[0:1, :], rows[2:3, :], rows[1:2, :], out[0], aff, None, None, None)
        experts(nc, k, wg, wu, wd, aff, idx_all, gate_all, out[0])


def lay_out(inputs):
    f = lambda name: np.ascontiguousarray(inputs[name])
    col = lambda v, n: np.ascontiguousarray(v.reshape(n, P).T)
    mu = f("rwkv_mu")[0]
    hp = lambda v: v.reshape(4, P)
    zero = np.zeros((4, P), np.float32)
    params = [hp(mu[0:512]), hp(mu[512:1024]), hp(mu[1024:1536]), hp(f("rwkv_w0")[0]), hp(f("rwkv_a0")[0]),
              hp(f("rwkv_k_k")[0]), hp(f("rwkv_k_a")[0]), hp(f("rwkv_r_k")[0].reshape(-1)),
              hp(f("rwkv_ln_w")[0]), hp(f("rwkv_ln_b")[0]), zero, zero]
    ada_b = f("ada_b_2")
    return {
        "x": f("x"), "norm_w_col": col(f("norm_w")[0], KD), "w_in": f("w_in"), "gate_up": f("gla_gate_up"),
        "gate_bias_col": np.ascontiguousarray(f("gla_gate_bias")[0].reshape(2, P, 1)),
        "gla_norm_col": np.ascontiguousarray(f("gla_norm_w")[0].reshape(P, 1)),
        "mu_lora_col": np.ascontiguousarray(mu[1536:1664].reshape(P, 1)), "w_up": f("rwkv_w_up"), "a_up": f("rwkv_a_up"),
        "rwkv_cols": np.ascontiguousarray(np.stack(params, -1)), "w_out": f("w_out"),
        "final_norm": np.ascontiguousarray(f("final_norm_w").reshape(1, D)), "c_col": col(f("c_2")[0], KD),
        "ada_w": f("ada_w_2"), "ada_b": ada_b, "ada_b_col": col(ada_b[0, 0:2 * D], 2 * KD), "norm_g": f("norm_g_2"),
        "norm_g_col": col(f("norm_g_2")[0, 0], KD), "sc_w_in": f("sc_w_in_2"),
        "sc_conv_col": np.ascontiguousarray(f("sc_conv_2")[0].reshape(3, KD, P).transpose(1, 2, 0)),
        "sc_w_out": f("sc_w_out_2"), "router": np.ascontiguousarray(f("moe_router_2")[0]),
        "wg": f("moe_w_gate_2"), "wu": f("moe_w_up_2"), "wd": f("moe_w_down_2"), "masks": mask_constants()[0],
    }


def kernel(**inputs):
    import concourse.bacc as bacc
    from concourse.bass_utils import run_bass_kernel_spmd

    nc = bacc.Bacc("TRN2", target_bir_lowering=False, num_devices=1)
    arrays, args = {}, []
    for name, a in lay_out(inputs).items():
        arrays[f"in_{name}"] = a
        args.append(nc.dram_tensor(f"in_{name}", a.shape, mybir.dt.from_np(a.dtype), kind="ExternalInput").ap())
    args.append(nc.dram_tensor("out_0", (1, T, D), F32, kind="ExternalOutput").ap())
    hybrid_conv_moe(nc, *args)
    r = run_bass_kernel_spmd(nc, [arrays], core_ids=[0])
    return r.results[0]["out_0"]
```
